# Optimizing a Trainium2 kernel written in Bass

```python
import jax
import jax.numpy as jnp
from jax import lax
import numpy as np
import jax, jax.numpy as jnp

D_MODEL = 2048
BATCH = 1
SEQ = 256
DEPTH = 2

N_MIXERS = 2
N_RET_LAYERS = (DEPTH + 1) // 2
N_MLA_LAYERS = DEPTH // 2
EPS = 1e-6
ROPE_BASE = 10000.0
BLOCK = 128

RET_HEADS = 8
RET_DK = D_MODEL // RET_HEADS
RET_DV = 2 * RET_DK
RET_WIDTH = RET_HEADS * RET_DV
RET_QK = RET_HEADS * RET_DK
RET_IN = 2 * RET_QK + 2 * RET_WIDTH

MLA_HEADS = 16
MLA_NOPE = 128
MLA_ROPE = 64
MLA_V = 128
MLA_Q_RANK = 512
MLA_KV_RANK = 512
MLA_WIDTH = MLA_HEADS * MLA_V
MLA_IN = MLA_Q_RANK + MLA_KV_RANK + MLA_ROPE + MLA_WIDTH


def rmsnorm(x, g):
    xf = x.astype(jnp.float32)
    y = xf * lax.rsqrt(jnp.mean(xf * xf, axis=-1, keepdims=True) + EPS)
    return (y * g.astype(jnp.float32)).astype(x.dtype)

def rope(x, pos):
    d = x.shape[-1]
    inv_freq = ROPE_BASE ** (-jnp.arange(0, d, 2, dtype=jnp.float32) / d)
    ang = pos.astype(jnp.float32)[:, :, None, None] * inv_freq
    cos = jnp.cos(ang).astype(x.dtype)
    sin = jnp.sin(ang).astype(x.dtype)
    x1, x2 = x[..., : d // 2], x[..., d // 2:]
    return jnp.concatenate([x1 * cos - x2 * sin, x2 * cos + x1 * sin], axis=-1)

def chunkwise_retention(q, k, v):
    B, S, H, _ = q.shape
    nc = S // BLOCK
    log_gamma = jnp.log1p(-jnp.exp2(-5.0 - jnp.arange(H, dtype=jnp.float32)))
    idx = jnp.arange(BLOCK, dtype=jnp.float32)
    diff = idx[:, None] - idx[None, :]
    d_intra = jnp.where(diff >= 0, jnp.exp(log_gamma[:, None, None] * jnp.maximum(diff, 0.0)), 0.0)
    xi = jnp.exp(log_gamma[:, None] * (idx + 1.0))[None, :, :, None]
    zeta = jnp.exp(log_gamma[:, None] * (BLOCK - 1.0 - idx))[None, :, :, None]
    chunk_decay = jnp.exp(log_gamma * BLOCK)[None, :, None, None]

    def to_chunks(t):
        return t.astype(jnp.float32).reshape(B, nc, BLOCK, H, t.shape[-1]).transpose(1, 0, 3, 2, 4)

    def step(state, inp):
        qi, ki, vi = inp
        scores = jnp.einsum('bhnd,bhmd->bhnm', qi, ki) * d_intra
        inner = jnp.einsum('bhnm,bhmv->bhnv', scores, vi)
        cross = jnp.einsum('bhnd,bhdv->bhnv', qi, state) * xi
        state = state * chunk_decay + jnp.einsum('bhmd,bhmv->bhdv', ki, vi * zeta)
        return state, inner + cross

    state0 = jnp.zeros((B, H, q.shape[-1], v.shape[-1]), jnp.float32)
    _, out = lax.scan(step, state0, (to_chunks(q), to_chunks(k), to_chunks(v)))
    return out.transpose(1, 0, 3, 2, 4).reshape(B, S, H, v.shape[-1])

def retention_branch(h, pos, w_in, gn_g, w_out):
    B, S, _ = h.shape
    proj = h @ w_in
    q, k, v, g = jnp.split(proj, [RET_QK, 2 * RET_QK, 2 * RET_QK + RET_WIDTH], axis=-1)
    q = rope(q.reshape(B, S, RET_HEADS, RET_DK), pos)
    k = rope(k.reshape(B, S, RET_HEADS, RET_DK), pos) * (RET_DK ** -0.5)
    v = v.reshape(B, S, RET_HEADS, RET_DV)
    y = chunkwise_retention(q, k, v)
    mu = jnp.mean(y, axis=-1, keepdims=True)
    var = jnp.mean(jnp.square(y - mu), axis=-1, keepdims=True)
    y = (y - mu) * lax.rsqrt(var + EPS)
    y = (y.reshape(B, S, RET_WIDTH) * gn_g.astype(jnp.float32)).astype(h.dtype)
    return (jax.nn.silu(g) * y) @ w_out

def causal_block_attention(q, k, v):
    B, S, H, dq = q.shape
    nb = S // BLOCK
    scale = dq ** -0.5
    qb = q.reshape(B, nb, BLOCK, H, dq).transpose(1, 0, 3, 2, 4)
    kt = k.transpose(0, 2, 1, 3)
    vt = v.transpose(0, 2, 1, 3)
    key_pos = jnp.arange(S)

    def one_block(args):
        i, qi = args
        s = jnp.einsum('bhqd,bhkd->bhqk', qi, kt).astype(jnp.float32) * scale
        qpos = i * BLOCK + jnp.arange(BLOCK)
        s = jnp.where(key_pos[None, :] <= qpos[:, None], s, -1e30)
        p = jax.nn.softmax(s, axis=-1).astype(vt.dtype)
        return jnp.einsum('bhqk,bhkd->bhqd', p, vt)

    o = lax.map(one_block, (jnp.arange(nb), qb))
    return o.transpose(1, 0, 3, 2, 4).reshape(B, S, H, v.shape[-1])

def mla_branch(h, pos, w_in, q_norm_g, w_uq, kv_norm_g, w_ukv, w_out):
    B, S, _ = h.shape
    proj = h @ w_in
    cq, ckv, k_rope, g = jnp.split(
        proj, [MLA_Q_RANK, MLA_Q_RANK + MLA_KV_RANK, MLA_Q_RANK + MLA_KV_RANK + MLA_ROPE], axis=-1)
    q = (rmsnorm(cq, q_norm_g) @ w_uq).reshape(B, S, MLA_HEADS, MLA_NOPE + MLA_ROPE)
    q = jnp.concatenate([q[..., :MLA_NOPE], rope(q[..., MLA_NOPE:], pos)], axis=-1)
    kv = (rmsnorm(ckv, kv_norm_g) @ w_ukv).reshape(B, S, MLA_HEADS, MLA_NOPE + MLA_V)
    k_nope, v = kv[..., :MLA_NOPE], kv[..., MLA_NOPE:]
    k_rope = rope(k_rope[:, :, None, :], pos)
    k = jnp.concatenate([k_nope, jnp.broadcast_to(k_rope, (B, S, MLA_HEADS, MLA_ROPE))], axis=-1)
    o = causal_block_attention(q, k, v).reshape(B, S, MLA_WIDTH)
    return (jax.nn.silu(g) * o) @ w_out

def first_inputs(seed: int = 0) -> dict:
    key = jax.random.key(seed)
    ks = jax.random.split(key, 18)

    def w(k, shape, fan_in, gain=1.0):
        return jax.random.normal(k, shape, jnp.float32) * (gain * fan_in ** -0.5)

    def gain(k, shape):
        return 1.0 + 0.05 * jax.random.normal(k, shape, jnp.float32)

    x = jax.random.normal(ks[0], (BATCH, SEQ, D_MODEL), jnp.float32)
    c = jax.random.normal(ks[1], (BATCH, D_MODEL), jnp.float32)
    start = jax.random.randint(ks[2], (BATCH, 1), 0, 1024, dtype=jnp.int32)
    positions = start + jnp.arange(SEQ, dtype=jnp.int32)[None, :]
    return {
        "x": x,
        "c": c,
        "positions": positions,
        "ada_w": w(ks[3], (DEPTH, D_MODEL, 3 * D_MODEL), D_MODEL, 0.5),
        "ada_b": 0.01 * jax.random.normal(ks[4], (DEPTH, 3 * D_MODEL), jnp.float32),
        "norm_g": gain(ks[5], (DEPTH, D_MODEL)),
        "ret_w_in": w(ks[6], (N_RET_LAYERS, D_MODEL, RET_IN), D_MODEL),
        "ret_gn_g": gain(ks[7], (N_RET_LAYERS, RET_WIDTH)),
        "ret_w_out": w(ks[8], (N_RET_LAYERS, RET_WIDTH, D_MODEL), RET_WIDTH),
        "mla_w_in": w(ks[9], (N_MLA_LAYERS, D_MODEL, MLA_IN), D_MODEL),
        "mla_q_norm_g": gain(ks[10], (N_MLA_LAYERS, MLA_Q_RANK)),
        "mla_w_uq": w(ks[11], (N_MLA_LAYERS, MLA_Q_RANK, MLA_HEADS * (MLA_NOPE + MLA_ROPE)), MLA_Q_RANK),
        "mla_kv_norm_g": gain(ks[12], (N_MLA_LAYERS, MLA_KV_RANK)),
        "mla_w_ukv": w(ks[13], (N_MLA_LAYERS, MLA_KV_RANK, MLA_HEADS * (MLA_NOPE + MLA_V)), MLA_KV_RANK),
        "mla_w_out": w(ks[14], (N_MLA_LAYERS, MLA_WIDTH, D_MODEL), MLA_WIDTH),
        "final_norm_g": gain(ks[15], (D_MODEL,)),
    }

def first_block(x, c, positions, ada_w, ada_b, norm_g, ret_w_in, ret_gn_g, ret_w_out,
              mla_w_in, mla_q_norm_g, mla_w_uq, mla_kv_norm_g, mla_w_ukv, mla_w_out,
              final_norm_g):
    c_act = jax.nn.silu(c)
    for i in range(DEPTH):
        mod = (c_act @ ada_w[i] + ada_b[i])[:, None, :]
        shift, scale, gate = jnp.split(mod, 3, axis=-1)
        h = rmsnorm(x, norm_g[i]) * (1.0 + scale) + shift
        j = i // N_MIXERS
        if i % N_MIXERS == 0:
            y = retention_branch(h, positions, ret_w_in[j], ret_gn_g[j], ret_w_out[j])
        else:
            y = mla_branch(h, positions, mla_w_in[j], mla_q_norm_g[j], mla_w_uq[j],
                           mla_kv_norm_g[j], mla_w_ukv[j], mla_w_out[j])
        x = x + gate * y
    return rmsnorm(x, final_norm_g)


DEPTH_2 = 1

HEAD_DIM = 64
N_FOX_HEADS = 16
N_DIL_HEADS = 16
FOX_WIDTH = N_FOX_HEADS * HEAD_DIM
DIL_WIDTH = N_DIL_HEADS * HEAD_DIM
MIX_WIDTH = FOX_WIDTH + DIL_WIDTH
ROPE_THETA = 500000.0
ROPE_DIM = HEAD_DIM // 4
DILATED_PAIRS = ((128, 1), (512, 4), (2048, 16))
Q_BLOCK = 128
PEER_HEADS = 8
PEER_N_KEYS = 128
PEER_N_EXPERTS = PEER_N_KEYS * PEER_N_KEYS
PEER_KEY_DIM = 256
PEER_HALF = PEER_KEY_DIM // 2
PEER_TOPK = 16
PEER_TOKEN_BLOCK = 128
RMS_EPS = 1e-6
IN_COLS = 3 * FOX_WIDTH + N_FOX_HEADS + 3 * DIL_WIDTH


def rms_norm(x, g):
    xf = x.astype(jnp.float32)
    y = xf * lax.rsqrt(jnp.mean(xf * xf, axis=-1, keepdims=True) + RMS_EPS)
    return y.astype(x.dtype) * g

def partial_rope(x, pos):
    inv = ROPE_THETA ** (-jnp.arange(0, ROPE_DIM, 2, dtype=jnp.float32) / ROPE_DIM)
    ang = pos.astype(jnp.float32)[:, None] * inv[None, :]
    cos = jnp.cos(ang)[None, :, None, :].astype(x.dtype)
    sin = jnp.sin(ang)[None, :, None, :].astype(x.dtype)
    xr, xp = x[..., :ROPE_DIM], x[..., ROPE_DIM:]
    x1, x2 = xr[..., :ROPE_DIM // 2], xr[..., ROPE_DIM // 2:]
    rot = jnp.concatenate([x1 * cos - x2 * sin, x2 * cos + x1 * sin], axis=-1)
    return jnp.concatenate([rot, xp], axis=-1)

def forgetting_attention(q, k, v, f_logit):
    B, S, H, hd = q.shape
    nb = S // Q_BLOCK
    log_f = jax.nn.log_sigmoid(f_logit.astype(jnp.float32))
    c = jnp.cumsum(log_f, axis=1).transpose(0, 2, 1)
    qh = q.transpose(0, 2, 1, 3) * (hd ** -0.5)
    kh = k.transpose(0, 2, 1, 3)
    vh = v.transpose(0, 2, 1, 3)
    q_blocks = qh.reshape(B, H, nb, Q_BLOCK, hd).transpose(2, 0, 1, 3, 4)
    c_blocks = c.reshape(B, H, nb, Q_BLOCK).transpose(2, 0, 1, 3)
    starts = jnp.arange(nb, dtype=jnp.int32) * Q_BLOCK
    k_pos = jnp.arange(S, dtype=jnp.int32)

    def block(args):
        qb, cb, s0 = args
        logits = jnp.einsum('bhqd,bhkd->bhqk', qb, kh).astype(jnp.float32)
        logits = logits + (cb[..., :, None] - c[..., None, :])
        q_pos = s0 + jnp.arange(Q_BLOCK, dtype=jnp.int32)
        mask = k_pos[None, :] <= q_pos[:, None]
        logits = jnp.where(mask, logits, -jnp.inf)
        p = jax.nn.softmax(logits, axis=-1).astype(vh.dtype)
        return jnp.einsum('bhqk,bhkd->bhqd', p, vh)

    o = lax.map(block, (q_blocks, c_blocks, starts))
    return o.transpose(1, 0, 3, 2, 4).reshape(B, S, H, hd)

def dilated_pattern(q, k, v, window, dilation):
    B, S, H, hd = q.shape
    span = window // dilation
    unit = dilation * Q_BLOCK
    s_pad = -(-S // unit) * unit
    L = s_pad // dilation
    nb = L // Q_BLOCK
    pad = ((0, 0), (0, s_pad - S), (0, 0), (0, 0))

    def to_sub(t):
        t = jnp.pad(t, pad).reshape(B, L, dilation, H, hd)
        return t.transpose(0, 2, 3, 1, 4).reshape(B, dilation, H, nb, Q_BLOCK, hd)

    def with_prev(t):
        prev = jnp.pad(t, ((0, 0), (0, 0), (0, 0), (1, 0), (0, 0), (0, 0)))[:, :, :, :-1]
        return jnp.concatenate([prev, t], axis=-2)

    qs = to_sub(q)
    kk = with_prev(to_sub(k))
    vv = with_prev(to_sub(v))
    logits = jnp.einsum('brhnqd,brhnkd->brhnqk', qs, kk).astype(jnp.float32) * (hd ** -0.5)
    qi = jnp.arange(Q_BLOCK)[:, None]
    kj = jnp.arange(2 * Q_BLOCK)[None, :]
    dist = qi + Q_BLOCK - kj
    band = (dist >= 0) & (dist <= span)
    has_prev = (jnp.arange(nb)[:, None, None] > 0) | (kj[None] >= Q_BLOCK)
    mask = band[None] & has_prev
    logits = jnp.where(mask, logits, -jnp.inf)
    m = jnp.max(logits, axis=-1, keepdims=True)
    e = jnp.exp(logits - m)
    den = jnp.sum(e, axis=-1, keepdims=True)
    o = jnp.einsum('brhnqk,brhnkd->brhnqd', (e / den).astype(v.dtype), vv)
    lse = (m + jnp.log(den))[..., 0]
    o = o.reshape(B, dilation, H, L, hd).transpose(0, 3, 1, 2, 4).reshape(B, s_pad, H, hd)[:, :S]
    lse = lse.reshape(B, dilation, H, L).transpose(0, 3, 1, 2).reshape(B, s_pad, H)[:, :S]
    return o, lse

def dilated_attention(q, k, v):
    outs = []
    lses = []
    for window, dilation in DILATED_PAIRS:
        o, lse = dilated_pattern(q, k, v, window, dilation)
        outs.append(o)
        lses.append(lse)
    wts = jax.nn.softmax(jnp.stack(lses, axis=0), axis=0)
    return jnp.sum(wts[..., None].astype(q.dtype) * jnp.stack(outs, axis=0), axis=0)

def peer(x, w_query, sub_keys, expert_down, expert_up):
    B, S, D = x.shape
    T = B * S
    xt = x.reshape(T, D)
    q = (xt @ w_query).reshape(T, PEER_HEADS, 2, PEER_HALF)
    scores = jnp.einsum('thpc,hpnc->thpn', q, sub_keys).astype(jnp.float32)
    vals, idx = lax.top_k(scores, PEER_TOPK)
    cand = (vals[..., 0, :, None] + vals[..., 1, None, :]).reshape(T, PEER_HEADS, PEER_TOPK * PEER_TOPK)
    top_vals, top_c = lax.top_k(cand, PEER_TOPK)
    i1 = jnp.take_along_axis(idx[..., 0, :], top_c // PEER_TOPK, axis=-1)
    i2 = jnp.take_along_axis(idx[..., 1, :], top_c % PEER_TOPK, axis=-1)
    experts = (i1 * PEER_N_KEYS + i2).reshape(T, PEER_HEADS * PEER_TOPK)
    gates = jax.nn.softmax(top_vals, axis=-1).reshape(T, PEER_HEADS * PEER_TOPK).astype(x.dtype)
    nc = T // PEER_TOKEN_BLOCK

    def block(args):
        xc, ec, gc = args
        u = jnp.take(expert_down, ec, axis=0)
        hdn = jax.nn.gelu(jnp.einsum('ted,td->te', u, xc))
        vsel = jnp.take(expert_up, ec, axis=0)
        return jnp.einsum('te,ted->td', gc * hdn, vsel)

    y = lax.map(block, (xt.reshape(nc, PEER_TOKEN_BLOCK, D),
                        experts.reshape(nc, PEER_TOKEN_BLOCK, PEER_HEADS * PEER_TOPK),
                        gates.reshape(nc, PEER_TOKEN_BLOCK, PEER_HEADS * PEER_TOPK)))
    return y.reshape(B, S, D)

def second_inputs(seed: int = 0) -> dict:
    key = jax.random.key(seed)
    ks = jax.random.split(key, 16)
    f32 = jnp.float32
    x = jax.random.normal(ks[0], (BATCH, SEQ, D_MODEL), f32)
    attn_norm_gain = 1.0 + 0.02 * jax.random.normal(ks[1], (DEPTH_2, D_MODEL), f32)
    w_in = jax.random.normal(ks[2], (DEPTH_2, D_MODEL, IN_COLS), f32) * D_MODEL ** -0.5
    forget_bias = jax.random.uniform(ks[3], (DEPTH_2, N_FOX_HEADS), f32, 1.0, 6.0)
    fox_out_gain = 1.0 + 0.02 * jax.random.normal(ks[4], (DEPTH_2, FOX_WIDTH), f32)
    dil_out_gain = 1.0 + 0.02 * jax.random.normal(ks[5], (DEPTH_2, DIL_WIDTH), f32)
    w_out = jax.random.normal(ks[6], (DEPTH_2, MIX_WIDTH, D_MODEL), f32) * MIX_WIDTH ** -0.5
    ffn_norm_gain = 1.0 + 0.02 * jax.random.normal(ks[7], (DEPTH_2, D_MODEL), f32)
    peer_query = jax.random.normal(ks[8], (DEPTH_2, D_MODEL, PEER_HEADS * PEER_KEY_DIM), f32) * D_MODEL ** -0.5
    peer_sub_keys = jax.random.normal(ks[9], (DEPTH_2, PEER_HEADS, 2, PEER_N_KEYS, PEER_HALF), f32) * PEER_HALF ** -0.5
    peer_down = jax.random.normal(ks[10], (DEPTH_2, PEER_N_EXPERTS, D_MODEL), f32) * D_MODEL ** -0.5
    peer_up = jax.random.normal(ks[11], (DEPTH_2, PEER_N_EXPERTS, D_MODEL), f32) * (PEER_HEADS * PEER_TOPK) ** -0.5
    final_norm_gain = 1.0 + 0.02 * jax.random.normal(ks[12], (D_MODEL,), f32)
    return {'x': x, 'attn_norm_gain': attn_norm_gain, 'w_in': w_in, 'forget_bias': forget_bias,
            'fox_out_gain': fox_out_gain, 'dil_out_gain': dil_out_gain, 'w_out': w_out,
            'ffn_norm_gain': ffn_norm_gain, 'peer_query': peer_query, 'peer_sub_keys': peer_sub_keys,
            'peer_down': peer_down, 'peer_up': peer_up, 'final_norm_gain': final_norm_gain}

def second_block(x, attn_norm_gain, w_in, forget_bias, fox_out_gain, dil_out_gain, w_out,
              ffn_norm_gain, peer_query, peer_sub_keys, peer_down, peer_up, final_norm_gain):
    B, S, _ = x.shape
    pos = jnp.arange(S, dtype=jnp.int32)
    splits = [FOX_WIDTH, 2 * FOX_WIDTH, 3 * FOX_WIDTH, 3 * FOX_WIDTH + N_FOX_HEADS,
              3 * FOX_WIDTH + N_FOX_HEADS + DIL_WIDTH, 3 * FOX_WIDTH + N_FOX_HEADS + 2 * DIL_WIDTH]
    h = x
    for layer in range(DEPTH_2):
        xn = rms_norm(h, attn_norm_gain[layer])
        proj = xn @ w_in[layer]
        fq, fk, fv, fg, dq, dk, dv = jnp.split(proj, splits, axis=-1)
        heads_f = (B, S, N_FOX_HEADS, HEAD_DIM)
        heads_d = (B, S, N_DIL_HEADS, HEAD_DIM)
        fox_o = forgetting_attention(fq.reshape(heads_f), fk.reshape(heads_f), fv.reshape(heads_f),
                                     fg + forget_bias[layer])
        dq = partial_rope(dq.reshape(heads_d), pos)
        dk = partial_rope(dk.reshape(heads_d), pos)
        dil_o = dilated_attention(dq, dk, dv.reshape(heads_d))
        mixed = jnp.concatenate([rms_norm(fox_o.reshape(B, S, FOX_WIDTH), fox_out_gain[layer]),
                                 rms_norm(dil_o.reshape(B, S, DIL_WIDTH), dil_out_gain[layer])], axis=-1)
        h = h + mixed @ w_out[layer]
        hn = rms_norm(h, ffn_norm_gain[layer])
        h = h + peer(hn, peer_query[layer], peer_sub_keys[layer], peer_down[layer], peer_up[layer])
    return rms_norm(h, final_norm_gain)


def setup_inputs(seed=0):
    out = dict(first_inputs(seed))
    for name, value in second_inputs(seed + 1).items():
        if name != "x":
            out[name + "_2"] = value
    return out


def reference(
    x, c, positions, ada_w, ada_b, norm_g, ret_w_in, ret_gn_g, ret_w_out, mla_w_in,
    mla_q_norm_g, mla_w_uq, mla_kv_norm_g, mla_w_ukv, mla_w_out, final_norm_g, attn_norm_gain_2,
    w_in_2, forget_bias_2, fox_out_gain_2, dil_out_gain_2, w_out_2, ffn_norm_gain_2,
    peer_query_2, peer_sub_keys_2, peer_down_2, peer_up_2, final_norm_gain_2,
):
    x = first_block(
        x, c, positions, ada_w, ada_b, norm_g, ret_w_in, ret_gn_g, ret_w_out, mla_w_in,
        mla_q_norm_g, mla_w_uq, mla_kv_norm_g, mla_w_ukv, mla_w_out, final_norm_g,
    )
    return second_block(
        x, attn_norm_gain_2, w_in_2, forget_bias_2, fox_out_gain_2, dil_out_gain_2, w_out_2,
        ffn_norm_gain_2, peer_query_2, peer_sub_keys_2, peer_down_2, peer_up_2,
        final_norm_gain_2,
    )


_drawn_inputs = setup_inputs


def setup_inputs(seed=0):
    import zlib

    import numpy as np

    out = dict(_drawn_inputs(seed))
    spreads = {}
    factors = {'ada_b': 3.973,
     'ret_gn_g': 4.089,
     'mla_q_norm_g': 8.0,
     'mla_kv_norm_g': 7.938,
     'fox_out_gain_2': 19.013,
     'dil_out_gain_2': 18.431,
     'ffn_norm_gain_2': 34.31,
     'final_norm_gain_2': 7.443}
    for name, (base, spread) in spreads.items():
        noise = np.random.default_rng([zlib.crc32(name.encode()), seed]).standard_normal(out[name].shape)
        drawn = base * np.exp(spread * noise) if base else spread * noise
        out[name] = jnp.asarray(drawn.astype(out[name].dtype))
    for name, factor in factors.items():
        out[name] = (out[name] * factor).astype(out[name].dtype)
    return out
```

```python
from contextlib import ExitStack

import numpy as np
import concourse.bass as bass
from concourse import mybir
from concourse.alu_op_type import AluOpType as ALU

F = mybir.dt.float32
I32 = mybir.dt.int32
U32 = mybir.dt.uint32
ACT = mybir.ActivationFunctionType
AX = mybir.AxisListType

D = 2048
R = 4
NB = 8
NG = 8
EPS = 1e-6
TWO_PI_INV = 0.15915494309189535
C1 = 6.28125
C2 = 0.0019350051879882812
C3 = 3.0199157663e-07
MAGIC = 12582912.0
PI_IN = 3.1415925

K_ID, K_ONE, K_PM, K_PD, K_TRI = 0, 128, 256, 384, 512
K_CM, K_INV, K_IOTA = 640, 1024, 1026
K_DM, K_DC, K_DS = 1042, 1426, 1682
K_END = 1938


def tables():
    t = np.zeros((128, K_END), np.float32)
    p = np.arange(128)
    t[:, K_ID:K_ID + 128] = np.eye(128)
    t[:, K_ONE:K_ONE + 128] = 1.0
    pm = np.zeros((128, 128), np.float32)
    pd = np.zeros((128, 128), np.float32)
    for b in (0, 64):
        for i in range(32):
            pm[b + 32 + i, b + i] = -1.0
            pm[b + i, b + 32 + i] = 1.0
        for i in range(8):
            pd[b + 8 + i, b + i] = -1.0
            pd[b + i, b + 8 + i] = 1.0
    t[:, K_PM:K_PM + 128] = pm
    t[:, K_PD:K_PD + 128] = pd
    t[:, K_TRI:K_TRI + 128] = p[:, None] <= p[None, :]

    def both(mask, add):
        full = np.where(mask, add, np.float32(-1e30)).astype(np.float32)
        return np.concatenate([full[0:128, 0:128], full[128:256, :]], axis=1)

    q = np.arange(256)[:, None]
    k = np.arange(256)[None, :]
    t[:, K_CM:K_CM + 384] = both(k <= q, np.zeros((256, 256), np.float32))
    count = ((q - k <= 128) & (k <= q)).astype(int) + ((k <= q) & ((q - k) % 4 == 0)) + ((k <= q) & ((q - k) % 16 == 0))
    t[:, K_DM:K_DM + 384] = both(count > 0, np.log(np.maximum(count, 1)).astype(np.float32))
    inv = (500000.0 ** (-np.arange(0, 16, 2) / 16)).astype(np.float32)
    ang = np.arange(256, dtype=np.float32)[None, :] * inv[:, None]
    for b in (0, 8, 64, 72):
        t[b:b + 8, K_DC:K_DC + 256] = np.cos(ang.astype(np.float64))
        t[b:b + 8, K_DS:K_DS + 256] = np.sin(ang.astype(np.float64))
    for b in (16, 80):
        t[b:b + 48, K_DC:K_DC + 256] = 1.0
    t[:, K_INV] = (10000.0 ** (-np.arange(0, 256, 2) / 256)).astype(np.float32)
    t[:, K_INV + 1] = (10000.0 ** (-np.arange(0, 64, 2) / 64)).astype(np.float32)[p % 32]
    t[:, K_IOTA:K_IOTA + 16] = np.arange(16)
    g = np.log1p(-np.exp2(-5.0 - np.arange(8)))
    n = np.arange(256)[None, :] - p[:, None]
    dec = np.stack([np.where(n >= 0, np.exp(a * np.maximum(n, 0)), 0.0) for a in g], axis=1) / 16.0
    return t, dec.astype(np.float32).reshape(128, 2048)


class Bank:
    def __init__(self, ap):
        self.ap = ap
        self.free = []


def build(nc, A, out):
    ctx = ExitStack()
    with ctx:
        def sem(name):
            return ctx.enter_context(nc.semaphore(name))

        class Eng:

            def __init__(self, name):
                self.name, self.q, self.n, self.seen = name, [], 0, {}
                self.sem = sem("s_" + name)

            def wait(self, *toks):
                for t in toks:
                    if t is None:
                        continue
                    if isinstance(t, list):
                        self.wait(*t)
                        continue
                    s, v = t
                    if self.seen.get(id(s), 0) < v:
                        self.seen[id(s)] = v
                        self.q.append(lambda e, s=s, v=v: e.wait_ge(s, v))

            def do(self, fn, *toks):
                self.wait(*toks)
                self.n += 1
                self.q.append(lambda e: fn(e).then_inc(self.sem, 1))
                return (self.sem, self.n)

            def mute(self, fn, *toks):
                self.wait(*toks)
                self.q.append(fn)

            def dma(self, dst, src, s, *toks, **kw):
                self.wait(*toks)
                self.q.append(lambda e: e.dma_start(dst, src, **kw).then_inc(s.sem, 16))
                s.n += 16
                return (s.sem, s.n)

            def run(self, e):
                for fn in self.q:
                    fn(e)

        class DSem:
            def __init__(self, name):
                self.sem, self.n = sem(name), 0

        PE, V, S, G, SP = (Eng(n) for n in ("pe", "dve", "act", "pool", "sp"))

        arena = ctx.enter_context(nc.sbuf_tensor("arena", [128, 52992], F))
        ps = ctx.enter_context(nc.psum_tensor("ps", [128, NB, 512], F))

        def at(off, *shape):
            n = int(np.prod(shape))
            a = arena[:, off:off + n]
            if len(shape) == 2:
                a = a.rearrange("p (a b) -> p a b", a=shape[0])
            if len(shape) == 3:
                a = a.rearrange("p (a b c) -> p a b c", a=shape[0], b=shape[1])
            return a

        KB = 256
        X = at(0, 2, D)
        HT = at(16 * KB, 16, 256)
        RING = 32 * KB
        YG = 96 * KB
        GBA = at(128 * KB, D)
        GBB = at(136 * KB, D)
        W = 144 * KB
        small = [192 * KB]

        def sm(*shape):
            off = small[0]
            small[0] += int(np.prod(shape))
            return at(off, *shape)

        cst = sm(K_DM)
        IDN = cst[:, K_ID:K_ID + 128]
        ONES = cst[:, K_ONE:K_ONE + 128]
        TRI = cst[:, K_TRI:K_TRI + 128]
        cosM, sinM = sm(256), sm(256)
        KR = sm(256)
        LB = [sm(384) for _ in range(2)]
        PTB = [sm(384) for _ in range(2)]
        colA, colB = sm(104), sm(128)
        cact, mod, gs = sm(16), sm(96), sm(16)
        st = sm(64)
        mn, sums, rinv = sm(2, 2), sm(2, 2), sm(3, 2)
        bst = sm(2, 6)
        mv = sm(2, 2)
        fb = sm(16)
        epsc = sm(1)
        assert small[0] <= 52992, small[0]

        banks = [Bank(ps[:, i, :]) for i in range(NB)]
        turn = [0]

        def bank():
            b = banks[turn[0] % NB]
            turn[0] += 1
            assert b.free is not None
            f, b.free = b.free, None
            return b, f

        plan = []
        slots = [(at(RING + i * 4096, 4096), DSem(f"w{i}")) for i in range(R)]
        sent, taken, freed = [0], [0], [0]

        def send(*toks):
            if sent[0] < len(plan):
                ap, ds = slots[sent[0] % R]
                for dst, src in plan[sent[0]](ap):
                    SP.dma(dst, src, ds, *toks)
                sent[0] += 1

        need = {}

        def take():
            i = taken[0]
            taken[0] += 1
            ap, ds = slots[i % R]
            return ap, (ds.sem, ds.n)

        def give(tok):
            freed[0] += 1
            send(tok)

        def block8(src, n0, n=512, k0=0):
            return lambda ap: [(ap[:, 0:8 * n].rearrange("p (k n) -> p k n", k=8),
                                src[k0:k0 + 1024, n0:n0 + n].rearrange("(k p) n -> p k n", p=128))]

        def pair(src, n0, n=512):
            plan.extend([block8(src, n0, n, 0), block8(src, n0, n, 1024)])

        ret_in, ret_out = A["ret_w_in"][0], A["ret_w_out"][0]
        mla_in, mla_out = A["mla_w_in"][0], A["mla_w_out"][0]
        uq, ukv = A["mla_w_uq"][0], A["mla_w_ukv"][0]
        w2, wo2, pq = A["w_in_2"][0], A["w_out_2"][0], A["peer_query_2"][0]

        def two(srcs, k0):
            def f(ap):
                v = ap.rearrange("p (k n) -> p k n", k=8)
                n = 512 // len(srcs)
                return [(v[:, :, i * n:(i + 1) * n], src[k0:k0 + 1024, c:c + n].rearrange("(k p) n -> p k n", p=128))
                        for i, (src, c) in enumerate(srcs)]
            return f

        def kr_pair(k0):
            def f(ap):
                v = ap[:, 0:1024].rearrange("p (k n) -> p k n", k=8)
                return [(v[:, :, j * 64:(j + 1) * 64],
                         mla_in[k0:k0 + 1024, 1024:1088].rearrange("(k p) n -> p k n", p=128)) for j in range(2)]
            return f

        def rows4(src, c, n):
            return lambda ap: [(ap[:, 0:4 * n].rearrange("p (k n) -> p k n", k=4),
                                src[:, c:c + n].rearrange("(k p) n -> p k n", p=128))]

        def uq_slot(c):
            def f(ap):
                v = ap[:, 0:3072].rearrange("p (k n) -> p k n", k=4)
                r = []
                for k in range(4):
                    s = uq[k * 128:(k + 1) * 128, c:c + 768].rearrange("p (h n) -> p h n", h=4)
                    r.append((v[:, k, 0:512].rearrange("p (h n) -> p h n", h=4), s[:, :, 0:128]))
                    r.append((v[:, k, 512:768].rearrange("p (h n) -> p h n", h=4), s[:, :, 128:192]))
                return r
            return f

        def out_slots(src, nk):
            for n in range(4):
                for k in range(nk // 8):
                    plan.append(block8(src, n * 512, 512, k * 1024))

        for g in range(8):
            pair(A["ada_w"][0], g * 512)
        for h in range(8):
            for k0 in (0, 1024):
                plan.append(two([(ret_in, h * 256), (ret_in, 2048 + h * 256)], k0))
            pair(ret_in, 4096 + h * 512)
            pair(ret_in, 8192 + h * 512)
            for g in range(2):
                n = 2 * h + g
                pair(A["ada_w"][0 if n < 4 else 1], (8 + n if n < 4 else n - 4) * 512)
        out_slots(ret_out, 32)
        pair(mla_in, 0)
        pair(mla_in, 512)
        plan.extend([kr_pair(0), kr_pair(1024)])
        for g in range(4):
            plan.append(uq_slot(g * 768))
            plan.append(rows4(ukv, g * 1024, 1024))
        for g in range(4):
            pair(mla_in, 1088 + g * 512)
        out_slots(mla_out, 16)
        plan.append(lambda ap: [(ap[:, 0:256].rearrange("p (k n) -> p k n", k=16),
                                 w2[:, 3072:3088].rearrange("(k p) n -> p k n", p=128))])
        for g in range(6):
            pair(w2, g * 512)
        for g in range(6):
            pair(w2, 3088 + g * 512)
        out_slots(wo2, 16)
        plan.append(lambda ap: [(ap[:, 0:2048].rearrange("p (h n) -> p h n", h=16),
                                 A["peer_sub_keys_2"][0].rearrange("h a n c -> n (h a) c"))])
        for g in range(4):
            pair(pq, g * 512)

        dc, dx, dr, dp, dg, dfb = (DSem(n) for n in ("dc", "dx", "dr", "dp", "dg", "dfb"))
        ROWA, ROWB = at(YG, 128), at(YG + 128, 128)
        PI, PF = at(YG + 256, 256), at(YG + 512, 256)
        t_c = SP.dma(cst, A["table"][:, 0:K_DM], dc)
        r0 = 0
        for name, n in (("c", 16), ("norm_g", 32), ("attn_norm_gain_2", 16), ("ffn_norm_gain_2", 16),
                        ("mla_q_norm_g", 4), ("mla_kv_norm_g", 4), ("fox_out_gain_2", 8), ("dil_out_gain_2", 8)):
            t_r = SP.dma(ROWA[r0:r0 + n, :], A[name].rearrange("a (n p) -> (a n) p", p=128), dr)
            r0 += n
        t_r = SP.dma(ROWB[0:96, :], A["ada_b"].rearrange("a (n p) -> (a n) p", p=128), dr)
        t_r = SP.dma(ROWB[96:128, :], A["ret_gn_g"].rearrange("a (n p) -> (a n) p", p=128), dr)
        for _ in range(R):
            send()
        t_x = G.dma(X, A["x"][0].rearrange("(t p) d -> p t d", p=128), dx)
        t_p = G.dma(PI.bitcast(I32), A["positions"][0].partition_broadcast(128), dp)
        DTAB = at(W, 8, 256)
        cosR, sinR = at(W + 8 * KB, 256), at(W + 9 * KB, 256)
        t_d = G.dma(DTAB.rearrange("p a b -> p (a b)"), A["decay"], dg)
        t_fb = G.dma(fb, A["forget_bias_2"][0].partition_broadcast(128), dfb)

        t_eps = V.do(lambda e: e.memset(epsc, EPS))

        def mm(o, l, r, start, stop):
            return lambda e: e.matmul(o, l, r, start=start, stop=stop)

        b, f = bank()
        PE.wait(t_c, t_r)
        PE.do(lambda e, b=b: e.transpose(b.ap[:, 0:104], ROWA[0:104, :], IDN[0:104, 0:104]), *f)
        t = PE.do(lambda e, b=b: e.transpose(b.ap[:, 128:256], ROWB, IDN))
        t_ca = V.do(lambda e, b=b: e.tensor_copy(colA, b.ap[:, 0:104]), t)
        t_cb = V.do(lambda e, b=b: e.tensor_copy(colB, b.ap[:, 128:256]), t)
        b.free = [t_cb]
        t_cact = S.do(lambda e: e.activation(cact, colA[:, 0:16], ACT.Silu), t_ca)

        t = V.do(lambda e: e.tensor_copy(PF, PI.bitcast(I32)), t_p)
        t_trig = []
        AN, KK, RR = (at(YG + (768 + 256 * i), 256) for i in range(3))
        RQ = [at(YG + 1536 + 256 * i, 256) for i in range(4)]
        k = 0
        for j, (co, si) in enumerate(((cosR, sinR), (cosM, sinM))):
            t = V.do(lambda e, j=j: e.tensor_scalar(AN, PF, cst[:, K_INV + j:K_INV + j + 1], None, ALU.mult), t, t_c)
            for dst, sh in ((co, 0.25), (si, 0.0)):
                q = RQ[k]
                k += 1
                t = V.do(lambda e, sh=sh: e.tensor_scalar(KK, AN, TWO_PI_INV, sh, ALU.mult, ALU.add), t)
                t = V.do(lambda e: e.tensor_scalar(KK, KK, MAGIC, None, ALU.add), t)
                t = V.do(lambda e: e.tensor_scalar(KK, KK, MAGIC, None, ALU.subtract), t)
                t = V.do(lambda e: e.scalar_tensor_tensor(out=RR, in0=KK, scalar=-C1, in1=AN, op0=ALU.mult, op1=ALU.add), t)
                t = V.do(lambda e: e.scalar_tensor_tensor(out=RR, in0=KK, scalar=-C2, in1=RR, op0=ALU.mult, op1=ALU.add), t)
                t = V.do(lambda e: e.scalar_tensor_tensor(out=RR, in0=KK, scalar=-C3, in1=RR, op0=ALU.mult, op1=ALU.add), t)
                if sh:
                    t = V.do(lambda e: e.tensor_scalar(RR, RR, 1.5707963267948966, None, ALU.add), t)
                t = V.do(lambda e, q=q: e.tensor_scalar(q, RR, PI_IN, -PI_IN, ALU.min, ALU.max), t)
                t_trig.append(S.do(lambda e, q=q, dst=dst: e.activation(dst, q, ACT.Sin), t))

        def ada(layer, g, *after):
            (w0, t0), (w1, t1) = take(), take()
            b, f = bank()
            PE.wait(t0, t1, t_cact, *f)
            for m in range(4):
                for kc in range(16):
                    w = (w0, w1)[kc // 8][:, (kc % 8) * 512 + m * 128:(kc % 8) * 512 + m * 128 + 128]
                    fn = mm(b.ap[:, m:m + 1], w, cact[:, kc:kc + 1], kc == 0, kc == 15)
                    if m == 3 and kc == 15:
                        t = PE.do(fn)
                    else:
                        PE.mute(fn)
            give(t)
            give(t)
            c = layer * 48 + g * 4
            r = V.do(lambda e, b=b, c=c: e.tensor_tensor(mod[:, c:c + 4], b.ap[:, 0:4], colB[:, c:c + 4], ALU.add), t, t_cb)
            b.free = [r]
            return r

        def gate_rows(layer, dst, t_gate, *after):
            toks = []
            DG = at(W + 46 * KB, 4, 128)
            prev = list(after)
            for g in range(4):
                ts = []
                for j in range(4):
                    c = layer * 48 + 32 + 4 * g + j
                    ts.append(V.do(lambda e, j=j, c=c: e.tensor_scalar(DG[:, j, :], IDN, mod[:, c:c + 1], None, ALU.mult),
                                   t_gate, *prev))
                b, f = bank()
                PE.wait(*f)
                t = PE.do(mm(b.ap, ONES, DG.rearrange("p a b -> p (a b)"), True, True), *ts)
                prev = [t]
                r = S.do(lambda e, b=b, g=g: e.copy(dst[:, g * 512:(g + 1) * 512], b.ap), t, *after)
                b.free = [r]
                toks.append(r)
            return toks[-1]

        for g in range(8):
            t_mod = ada(0, g)

        def stat_of(src, n, col, junk, *after):
            t = S.do(lambda e: e.activation(junk, src, ACT.Square, scale=float(n) ** -0.5, accum_out=st[:, col:col + 1]), *after)
            t = S.do(lambda e: e.activation(st[:, col:col + 1], st[:, col:col + 1], ACT.Sqrt, bias=epsc), t, t_eps)
            return V.do(lambda e: e.reciprocal(st[:, col:col + 1], st[:, col:col + 1]), t)

        def turn_over(src, nk, dst, scale, bias, waits, after):
            res = []
            for p in range(nk // 2):
                b, f = bank()
                PE.wait(*f)
                for t in range(2):
                    for j in range(2):
                        k = 2 * p + j
                        tt = PE.do(lambda e, b=b, j=j, t=t, k=k: e.transpose(
                            b.ap[:, j * 256 + t * 128:j * 256 + t * 128 + 128],
                            src[:, t, k * 128:(k + 1) * 128], IDN), waits[t])
                rs = []
                for j in range(2):
                    k = 2 * p + j
                    if p % 2 == 0:
                        if bias is None:
                            fn = lambda e, b=b, j=j, k=k: e.tensor_scalar(dst[:, k, :], b.ap[:, j * 256:j * 256 + 256],
                                                                          scale[:, k:k + 1], None, ALU.mult)
                        else:
                            fn = lambda e, b=b, j=j, k=k: e.tensor_scalar(dst[:, k, :], b.ap[:, j * 256:j * 256 + 256],
                                                                          scale[:, k:k + 1], bias[:, k:k + 1],
                                                                          ALU.mult, ALU.add)
                        rs.append(V.do(fn, tt, *after))
                    else:
                        if bias is None:
                            fn = lambda e, b=b, j=j, k=k: e.activation(dst[:, k, :], b.ap[:, j * 256:j * 256 + 256],
                                                                       ACT.Copy, scale=scale[:, k:k + 1])
                        else:
                            fn = lambda e, b=b, j=j, k=k: e.activation(dst[:, k, :], b.ap[:, j * 256:j * 256 + 256],
                                                                       ACT.Identity, scale=scale[:, k:k + 1],
                                                                       bias=bias[:, k:k + 1])
                        rs.append(S.do(fn, tt, *after))
                b.free = rs
                res = (res + rs)[-4:]
            return res

        def norm_T(t_X, scale, bias, after, stat0=0):
            XN = at(YG, 2, D)
            ws = []
            for t in range(2):
                r = stat_of(X[:, t, :], D, stat0 + t, XN[:, t, :], t_X, *after)
                ws.append(V.do(lambda e, t=t: e.tensor_scalar(XN[:, t, :], X[:, t, :], st[:, stat0 + t:stat0 + t + 1],
                                                              None, ALU.mult), r))
            return turn_over(XN, 16, HT, scale, bias, ws, after)

        def mod_scale(layer, t_mod, *after):
            c = layer * 48 + 16
            return V.do(lambda e: e.scalar_tensor_tensor(out=gs, in0=mod[:, c:c + 16], scalar=1.0,
                                                         in1=colA[:, 16 + 16 * layer:32 + 16 * layer],
                                                         op0=ALU.add, op1=ALU.mult), t_mod, t_ca, *after)

        t_gs = mod_scale(0, t_mod)
        t_ht = norm_T(t_x, gs, mod[:, 0:16], [t_gs, t_trig[-1]] + t_trig)

        def proj_T(ws, nk, cols, xT, o, t_w, per=8, width=512, pre=()):
            for kc in range(nk):
                w = cols(ws[kc // per], kc % per)
                fn = mm(o, w, xT[:, kc, :], kc == 0, kc == nk - 1)
                if kc == nk - 1:
                    t = PE.do(fn)
                else:
                    PE.mute(fn, *t_w)
            return t

        def col128(width, c):
            return lambda w, k: w[:, k * width + c:k * width + c + 128]

        def proj_tok(ws, nk, xT, t_w, waits, evac, per=8):
            for t in range(2):
                b, f = bank()
                PE.wait(*f)
                PE.wait(*t_w)
                PE.wait(*waits)
                for kc in range(nk):
                    w = ws[kc // per][:, (kc % per) * 512:(kc % per) * 512 + 512]
                    fn = mm(b.ap, xT[:, kc, t * 128:(t + 1) * 128], w, kc == 0, kc == nk - 1)
                    if kc == nk - 1:
                        tt = PE.do(fn)
                    else:
                        PE.mute(fn)
                b.free = evac(t, b, tt)
            return tt

        def take2():
            (w0, t0), (w1, t1) = take(), take()
            return [w0, w1], [t0, t1]

        o = W + 10 * KB
        QK = at(o, 4, 256)
        T1, T2 = at(o + 1024, 2, 256), at(o + 1536, 2, 256)
        VV = at(o + 2048, 2, 512)
        SD = at(o + 3072, 384)
        SG = at(o + 3456, 4, 256)
        YN = at(o + 4480, 2, 512)
        assert 10 * KB + 5504 <= 46 * KB
        YT = at(YG, 32, 256)

        def bc2(a):
            return a.unsqueeze(1).broadcast_to([128, 2, 256])

        state = {"sd": None, "yt": [], "gate": None, "t_y": None}
        PE.wait(*t_ht)

        def ret_back(h, ty):
            rs = []
            for p in range(2):
                b, f = bank()
                PE.wait(*f)
                for t in range(2):
                    for j in range(2):
                        k = 2 * p + j
                        tt = PE.do(lambda e, b=b, j=j, t=t, k=k: e.transpose(
                            b.ap[:, j * 256 + t * 128:j * 256 + t * 128 + 128],
                            YN[:, t, k * 128:(k + 1) * 128], IDN), ty[t])
                rr = []
                for j in range(2):
                    k = 2 * p + j
                    g = 96 + h * 4 + k
                    rr.append(V.do(lambda e, b=b, j=j, k=k, g=g: e.scalar_tensor_tensor(
                        out=YT[:, h * 4 + k, :], in0=b.ap[:, j * 256:j * 256 + 256], scalar=colB[:, g:g + 1],
                        in1=SG[:, k, :], op0=ALU.mult, op1=ALU.mult), tt, *state["sg"]))
                b.free = rr
                rs += rr
            state["yt"] = rs

        ty = None
        for h in range(8):
            ws, tw = take2()
            qs = []
            for part in range(2):
                b, f = bank()
                PE.wait(*f)
                for j in range(2):
                    tt = proj_T(ws, 16, col128(512, part * 256 + j * 128), HT, b.ap[:, j * 256:j * 256 + 256], tw)
                v = b.ap.rearrange("p (a b) -> p a b", a=2)
                a1 = V.do(lambda e, v=v: e.tensor_tensor(T1, v, bc2(cosR), ALU.mult), tt, *t_trig)
                a2 = V.do(lambda e, v=v: e.tensor_tensor(T2, v, bc2(sinR), ALU.mult), tt)
                b.free = [a2]
                q0 = V.do(lambda e, part=part: e.tensor_tensor(QK[:, 2 * part, :], T1[:, 0, :], T2[:, 1, :], ALU.subtract), a1, a2)
                q1 = V.do(lambda e, part=part: e.tensor_tensor(QK[:, 2 * part + 1, :], T1[:, 1, :], T2[:, 0, :], ALU.add))
                V.wait(q1)
                qs = [q1]
            give(tt)
            give(tt)
            if h:
                ret_back(h - 1, ty)
            ws, tw = take2()
            vs = []

            def ev(t, b, tt):
                vs.append(S.do(lambda e: e.copy(VV[:, t, :], b.ap), tt))
                return [vs[-1]]

            tt = proj_tok(ws, 16, HT, tw, [], ev)
            give(tt)
            give(tt)
            b, f = bank()
            PE.wait(*f)
            PE.wait(*qs)
            for j in range(2):
                PE.mute(mm(b.ap[:, 0:256], QK[:, 2 + j, 0:128], QK[:, j, :], j == 0, j == 1))
            for j in range(2):
                fn = mm(b.ap[:, 256:384], QK[:, 2 + j, 128:256], QK[:, j, 128:256], j == 0, j == 1)
                tt = PE.do(fn)
            a1 = V.do(lambda e, b=b, h=h: e.tensor_tensor(SD[:, 0:256], b.ap[:, 0:256], DTAB[:, h, :], ALU.mult), tt, t_d)
            a2 = V.do(lambda e, b=b, h=h: e.tensor_tensor(SD[:, 256:384], b.ap[:, 256:384], DTAB[:, h, 0:128], ALU.mult))
            b.free = [a2]
            ws, tw = take2()
            sg = []
            for p in range(2):
                b, f = bank()
                PE.wait(*f)
                for j in range(2):
                    tt = proj_T(ws, 16, col128(512, (2 * p + j) * 128), HT, b.ap[:, j * 256:j * 256 + 256], tw)
                sg.append(S.do(lambda e, b=b, p=p: e.activation(
                    SG[:, 2 * p:2 * p + 2, :].rearrange("p a b -> p (a b)"), b.ap, ACT.Silu), tt, *state["yt"]))
                b.free = [sg[-1]]
            state["sg"] = sg
            give(tt)
            give(tt)
            ty = []
            for t in range(2):
                b, f = bank()
                PE.wait(*f)
                PE.wait(a2, *vs)
                if t == 0:
                    tt = PE.do(mm(b.ap, SD[:, 0:128], VV[:, 0, :], True, True))
                else:
                    PE.mute(mm(b.ap, SD[:, 128:256], VV[:, 0, :], True, False))
                    tt = PE.do(mm(b.ap, SD[:, 256:384], VV[:, 1, :], False, True))
                r = V.do(lambda e, b=b, t=t: e.bn_stats(bst[:, t, :], b.ap), tt)
                r = V.do(lambda e, t=t: e.bn_aggr(mv[:, t, :], bst[:, t, :]), r)
                r = S.do(lambda e, t=t: e.activation(st[:, 8 + t:9 + t], mv[:, t, 1:2], ACT.Sqrt, bias=epsc), r, t_eps)
                r = V.do(lambda e, t=t: e.reciprocal(st[:, 8 + t:9 + t], st[:, 8 + t:9 + t]), r)
                r = V.do(lambda e, b=b, t=t: e.tensor_scalar(YN[:, t, :], b.ap, mv[:, t, 0:1], st[:, 8 + t:9 + t],
                                                             ALU.subtract, ALU.mult), r)
                b.free = [r]
                ty.append(r)
            for g in range(2):
                n = 2 * h + g
                t_mod = ada(0 if n < 4 else 1, 8 + n if n < 4 else n - 4)
                if n == 3:
                    t_g0 = t_mod
            if h == 2:
                t_gate = gate_rows(0, GBA, t_g0)
        ret_back(7, ty)

        def project_out(yT, nk, t_in, gate, t_gate, t_X):
            PE.wait(*t_in)
            OT = at(W + 40 * KB, 2, 512)
            last = [None, None]
            for n in range(4):
                bs = []
                for t in range(2):
                    b, f = bank()
                    PE.wait(*f)
                    bs.append(b)
                tk = [None, None]
                for s in range(nk // 8):
                    w, tw = take()
                    PE.wait(tw)
                    for t in range(2):
                        for k in range(8):
                            kc = s * 8 + k
                            fn = mm(bs[t].ap, yT[:, kc, t * 128:(t + 1) * 128], w[:, k * 512:(k + 1) * 512],
                                    kc == 0, kc == nk - 1)
                            if k == 7:
                                tk[t] = PE.do(fn)
                            else:
                                PE.mute(fn)
                    give(tk[1])
                for t in range(2):
                    b = bs[t]
                    xs = X[:, t, n * 512:(n + 1) * 512]
                    if gate is None:
                        r = V.do(lambda e, b=b, xs=xs: e.tensor_tensor(xs, b.ap, xs, ALU.add), tk[t], *t_X)
                        b.free = [r]
                    else:
                        gg = gate[:, n * 512:(n + 1) * 512]
                        r = V.do(lambda e, b=b, t=t, gg=gg: e.tensor_tensor(OT[:, t, :], b.ap, gg, ALU.mult),
                                 tk[t], t_gate, last[t])
                        b.free = [r]
                        r = V.do(lambda e, t=t, xs=xs: e.tensor_tensor(xs, OT[:, t, :], xs, ALU.add), r, *t_X)
                    last[t] = r
            return last[1]

        t_X = project_out(YT, 32, state["yt"], GBA, t_gate, [])
        t_w_end = t_X

        t_gs = mod_scale(1, t_mod, *t_ht)
        t_ht = norm_T(t_X, gs, mod[:, 48:64], [t_gs], 2)
        t_gate = gate_rows(1, GBB, t_mod, t_X)
        t_fg = G.dma(GBA, A["final_norm_g"].partition_broadcast(128), DSem("dfg"), t_X, t_gate)
        PE.wait(*t_ht)
        SGM = at(YG, 16, 256)
        QN = at(YG + 4096, 16, 256)
        KN = at(W, 16, 256)
        VM = at(W + 16 * KB, 2, D)
        QR = at(W + 32 * KB, 8, 256)
        CT = at(W + 40 * KB, 8, 256)
        CTOK = at(YG, 2, 1024)
        RAW = at(YG + 2048, 256)
        RT = [at(YG + 2304 + 256 * i, 256) for i in range(2)]

        for part in range(2):
            ws, tw = take2()
            cs = []

            def ev(t, b, tt, part=part):
                d = CTOK[:, t, part * 512:(part + 1) * 512]
                r = stat_of(b.ap, 512, 4 + 2 * part + t, d, tt, *t_ht)
                cs.append(V.do(lambda e: e.tensor_scalar(d, b.ap, st[:, 4 + 2 * part + t:5 + 2 * part + t], None, ALU.mult), r))
                return [cs[-1]]

            tt = proj_tok(ws, 16, HT, tw, [], ev)
            give(tt)
            give(tt)
            if part == 0:
                cs0 = cs
        ws, tw = take2()
        b, f = bank()
        PE.wait(*f)
        tt = proj_T(ws, 16, lambda w, k: w[:, k * 128:k * 128 + 128], HT, b.ap[:, 0:256], tw)
        give(tt)
        give(tt)

        def rotate(b, m, dst, perm, co, si, tt, raw, rt, sc, after):
            n = 256 * m

            def v(x):
                return x[:, 0:n].rearrange("p (a b) -> p a b", a=m)

            def bc(x):
                return x.unsqueeze(1).broadcast_to([128, m, 256])

            r = S.do(lambda e: e.copy(raw[:, 0:n], b.ap[:, 0:n]), tt, *after)
            p = PE.do(mm(b.ap[:, 0:n], perm, raw[:, 0:n], True, True), r)
            a = V.do(lambda e: e.tensor_tensor(v(rt[0]), v(raw), bc(co), ALU.mult), r, *after)
            c = V.do(lambda e: e.tensor_tensor(v(rt[1]), v(b.ap), bc(si), ALU.mult), p)
            if sc is None:
                return V.do(lambda e: e.tensor_tensor(dst, rt[0][:, 0:n], rt[1][:, 0:n], ALU.add), a, c)
            c = V.do(lambda e: e.tensor_tensor(rt[0][:, 0:n], rt[0][:, 0:n], rt[1][:, 0:n], ALU.add), a, c)
            return V.do(lambda e: e.tensor_scalar(dst, rt[0][:, 0:n], sc, None, ALU.mult), c)

        PMm = cst[:, K_PM:K_PM + 128]
        t_kr = rotate(b, 1, KR, PMm, cosM, sinM, tt, RAW, RT, None, [*t_ht])
        b.free = [t_kr]
        w1 = [cs0[0], cs[0]]
        t_ct = turn_over(CTOK, 8, CT, colA[:, 80:88], None, [cs[0], cs[1]], [t_w_end, t_gate, cs0[0], cs0[1]])
        PE.wait(*t_ct)
        outs = []
        prev = t_kr
        for g in range(4):
            (wq, tq), (wk, tk) = take(), take()
            PE.wait(tq, tk)
            for pr in range(2):
                b, f = bank()
                PE.wait(*f)
                for j in range(2):
                    hh = 2 * pr + j
                    tt = proj_T([wq], 4, lambda w, k, hh=hh: w[:, k * 768 + hh * 128:k * 768 + hh * 128 + 128],
                                CT, b.ap[:, j * 256:j * 256 + 256], [])
                h0 = 4 * g + 2 * pr
                r = S.do(lambda e, b=b, h0=h0: e.copy(QN[:, h0:h0 + 2, :].rearrange("p a b -> p (a b)"), b.ap), tt, *t_ct)
                b.free = [r]
                outs.append(r)
                b, f = bank()
                PE.wait(*f)
                tt = proj_T([wq], 4, lambda w, k, pr=pr: w[:, k * 768 + 512 + pr * 128:k * 768 + 640 + pr * 128], CT, b.ap[:, 0:256], [])
                prev = rotate(b, 1, QR[:, 2 * g + pr, :], PMm, cosM, sinM, tt, RAW, RT, None, [prev])
                b.free = [prev]
                outs.append(prev)
                b, f = bank()
                PE.wait(*f)
                for j in range(2):
                    hh = 2 * pr + j
                    tt = proj_T([wk], 4, lambda w, k, hh=hh: w[:, k * 1024 + hh * 256:k * 1024 + hh * 256 + 128],
                                CT[:, 4:8, :], b.ap[:, j * 256:j * 256 + 256], [])
                r = V.do(lambda e, b=b, h0=h0: e.tensor_copy(KN[:, h0:h0 + 2, :].rearrange("p a b -> p (a b)"), b.ap), tt)
                b.free = [r]
                outs.append(r)
            give(tt)
            for t in range(2):
                b, f = bank()
                PE.wait(*f)
                for kc in range(4):
                    w = wk[:, kc * 1024:(kc + 1) * 1024].rearrange("p (h c) -> p h c", h=4)[:, :, 128:256]
                    fn = mm(b.ap.rearrange("p (h c) -> p h c", h=4), CT[:, 4 + kc, t * 128:(t + 1) * 128], w, kc == 0, kc == 3)
                    if kc == 3:
                        tt = PE.do(fn)
                    else:
                        PE.mute(fn)
                r = S.do(lambda e, b=b, t=t, g=g: e.copy(VM[:, t, g * 512:(g + 1) * 512], b.ap), tt)
                b.free = [r]
                outs.append(r)
            give(tt)

        CM = cst[:, K_CM:K_CM + 384]

        def soft(i, b, tt, mask, scale, t_old):
            L = LB[i % 2]
            j = i % 2
            es = []
            rr = []
            for t, (c0, c1) in enumerate(((0, 128), (128, 384))):
                rr.append(V.do(lambda e, c0=c0, c1=c1, t=t: e.tensor_tensor_reduce(
                    L[:, c0:c1], b.ap[:, c0:c1], mask[:, c0:c1], -scale, 3e38, ALU.add, ALU.min,
                    mn[:, j, t:t + 1]), tt, *t_old))
            for t, (c0, c1) in enumerate(((0, 128), (128, 384))):
                es.append(S.do(lambda e, c0=c0, c1=c1, t=t: e.activation(
                    L[:, c0:c1], L[:, c0:c1], ACT.Exp, bias=mn[:, j, t:t + 1], scale=-1.0,
                    accum_out=sums[:, j, t:t + 1]), rr[t]))
            b.free = [rr[1]]
            r = V.do(lambda e: e.reciprocal(rinv[:, i % 3, :], sums[:, j, :]), es[0], es[1])
            return es, r

        def flip(i, waits, t_old):
            b, f = bank()
            PE.wait(*f)
            L = LB[i % 2]
            PE.wait(*waits)
            for c in range(3):
                tt = PE.do(lambda e, c=c, b=b: e.transpose(b.ap[:, c * 128:(c + 1) * 128], L[:, c * 128:(c + 1) * 128], IDN))
            r = S.do(lambda e, b=b: e.copy(PTB[i % 2], b.ap[:, 0:384]), tt, *t_old)
            b.free = [r]
            return tt, r

        PE.wait(*outs)
        gw = {}

        def gate_block(m):
            if m % 4 == 0:
                gw["w"], gw["t"] = take2()
            b, f = bank()
            PE.wait(*f)
            tt = proj_T(gw["w"], 16, col128(512, (m % 4) * 128), HT, b.ap[:, 0:256], gw["t"])
            if m % 4 == 3:
                give(tt)
                give(tt)
            r = S.do(lambda e, b=b, m=m: e.activation(SGM[:, m, :], b.ap[:, 0:256], ACT.Silu), tt, *t_ct, *outs)
            b.free = [r]
            return r

        sgt = {}
        fl = {}
        sm_ = {}
        og = {}
        ISQ = float(192 ** -0.5)
        for i in range(16 + 2):
            if i < 16:
                b, f = bank()
                PE.wait(*f)
                rb = 64 * (i % 2)
                q1, q2 = QN[:, i, :], QR[rb:rb + 64, i // 2, :]
                k1, k2 = KN[:, i, :], KR[rb:rb + 64, :]
                PE.mute(mm(b.ap[:, 0:128], q1[:, 0:128], k1[:, 0:128], True, False))
                PE.mute(mm(b.ap[:, 0:128], q2[:, 0:128], k2[:, 0:128], False, True))
                PE.mute(mm(b.ap[:, 128:384], q1[:, 128:256], k1, True, False))
                tt = PE.do(mm(b.ap[:, 128:384], q2[:, 128:256], k2, False, True))
                es, r = soft(i, b, tt, CM, ISQ, [fl[i - 2][0]] if i > 1 else [])
                ns = []
                for t, (c0, c1) in enumerate(((0, 128), (128, 384))):
                    ns.append(V.do(lambda e, c0=c0, c1=c1, t=t, i=i: e.tensor_scalar(
                        LB[i % 2][:, c0:c1], LB[i % 2][:, c0:c1], rinv[:, i % 3, t:t + 1], None, ALU.mult), r))
                sm_[i] = ns
                sgt[i] = gate_block(i)
            if 0 <= i - 1 < 16:
                fl[i - 1] = flip(i - 1, sm_[i - 1], [og[i - 3][0]] if i >= 3 else [])
            if i >= 2:
                h = i - 2
                b, f = bank()
                PE.wait(*f)
                PE.wait(fl[h][1])
                PT = PTB[h % 2]
                v0, v1 = VM[:, 0, h * 128:(h + 1) * 128], VM[:, 1, h * 128:(h + 1) * 128]
                PE.mute(mm(b.ap[:, 0:128], v0, PT[:, 0:128], True, True))
                PE.mute(mm(b.ap[:, 128:256], v0, PT[:, 128:256], True, False))
                tt = PE.do(mm(b.ap[:, 128:256], v1, PT[:, 256:384], False, True))
                r = V.do(lambda e, b=b, h=h: e.tensor_tensor(SGM[:, h, :], b.ap[:, 0:256], SGM[:, h, :], ALU.mult), tt, sgt[h])
                b.free = [r]
                og[h] = (tt, r)
        t_X = project_out(SGM, 16, [og[15][1]], GBB, t_gate, [t_X])

        JK = at(YG, D)
        ts = []
        for t in range(2):
            r = stat_of(X[:, t, :], D, 10 + t, at(YG + D * t, D), t_X)
            ts.append(V.do(lambda e, t=t: e.scalar_tensor_tensor(out=X[:, t, :], in0=X[:, t, :], scalar=st[:, 10 + t:11 + t],
                                                                 in1=GBA, op0=ALU.mult, op1=ALU.mult), r, t_fg))
        t_X = ts[1]

        t_ht = norm_T(t_X, colA[:, 48:64], None, [], 12)
        d2 = DSem("d2")
        DM, DC, DS = GBA[:, 0:384], GBA[:, 384:640], GBA[:, 640:896]
        t_d2 = G.dma(GBA[:, 0:896], A["table"][:, K_DM:K_END], d2, t_X)
        t_ff = G.dma(GBB, A["ffn_norm_gain_2"][0].partition_broadcast(128), DSem("dff"), t_X)
        PE.wait(*t_ht)
        O = at(YG, 2, D)
        FV, DV = at(YG + 4096, 2, 1024), at(YG + 6144, 2, 1024)
        FQ, FK, DQ, DK = (at(W + i * 2048, 8, 256) for i in range(4))
        RAW2 = at(W + 8192, 512)
        RT2 = [at(W + 8704 + 512 * i, 512) for i in range(2)]
        LF = at(W + 8192 + 1536, 2, 16)
        LA = at(W + 8192 + 1568, 2, 16)
        LM = at(W + 8192 + 1600, 2, 16)
        CTT = at(W + 8192 + 1632, 256)
        NCT = at(W + 8192 + 1888, 256)

        (wf, tf) = take()
        b, f = bank()
        PE.wait(*f)
        PE.wait(tf)
        for t in range(2):
            for kc in range(16):
                fn = mm(b.ap[:, t * 16:t * 16 + 16], HT[:, kc, t * 128:(t + 1) * 128], wf[:, kc * 16:(kc + 1) * 16],
                        kc == 0, kc == 15)
                if kc == 15:
                    tt = PE.do(fn)
                else:
                    PE.mute(fn)
        give(tt)
        r = V.do(lambda e, b=b: e.tensor_tensor(LF, b.ap[:, 0:32].rearrange("p (a b) -> p a b", a=2),
                                                fb.unsqueeze(1).broadcast_to([128, 2, 16]), ALU.add), tt, t_fb, t_X)
        b.free = [r]
        r2 = V.do(lambda e: e.scalar_tensor_tensor(out=LA, in0=LF, scalar=-1.0, in1=LF, op0=ALU.mult, op1=ALU.min), r)
        r3 = V.do(lambda e: e.tensor_scalar(LM, LF, 0.0, None, ALU.min), r)
        r2 = S.do(lambda e: e.activation(LA, LA, ACT.Exp), r2)
        r2 = S.do(lambda e: e.activation(LA, LA, ACT.Ln, bias=1.0), r2)
        t_lf = V.do(lambda e: e.tensor_tensor(LF, LM, LA, ALU.subtract), r2, r3)

        def work_T(dst, c, extra):
            def f(ws, tw):
                b, fr = bank()
                PE.wait(*fr)
                for j in range(2):
                    tt = proj_T(ws, 16, col128(512, (c % 4 + j) * 128), HT, b.ap[:, j * 256:j * 256 + 256], tw)
                b.free = extra(dst, c, b, tt)
                return tt
            return f

        fq_done, dq_done = [], []

        def fox_q(dst, c, b, tt):
            r = S.do(lambda e: e.mul(dst[:, c:c + 2, :].rearrange("p a b -> p (a b)"), b.ap, 0.125), tt, t_X)
            fq_done.append(r)
            return [r]

        def fox_k(dst, c, b, tt):
            r = S.do(lambda e: e.copy(dst[:, c:c + 2, :].rearrange("p a b -> p (a b)"), b.ap), tt, t_X)
            fq_done.append(r)
            return [r]

        ro = {0: t_X, 1: t_X}
        PDm = cst[:, K_PD:K_PD + 128]

        def dil_qk(sc):
            def f(dst, c, b, tt):
                ro[0] = rotate(b, 2, dst[:, c:c + 2, :].rearrange("p a b -> p (a b)"), PDm, DC, DS, tt, RAW2, RT2, sc,
                               [ro[0], t_d2])
                dq_done.append(ro[0])
                return [ro[0]]
            return f

        for dst, fn in ((FQ, fox_q), (FK, fox_k)):
            for g in range(2):
                ws, tw = take2()
                tt = work_T(dst, 4 * g, fn)(ws, tw)
                f2 = work_T(dst, 4 * g + 2, fn)
                tt = f2(ws, tw)
                give(tt)
                give(tt)

        def tok_pair(dst, g, done, acc):
            ws, tw = take2()

            def ev(t, b, tt):
                r = S.do(lambda e: e.copy(dst[:, t, g * 512:(g + 1) * 512], b.ap), tt, *t_ht)
                done.append(r)
                return [r]
            tt = proj_tok(ws, 16, HT, tw, [], ev)
            give(tt)
            give(tt)

        for g in range(2):
            tok_pair(FV, g, fq_done, None)

        b, f = bank()
        PE.wait(*f)
        PE.wait(t_lf)
        PE.mute(mm(b.ap[0:16, 0:128], LF[:, 0, :], TRI, True, True))
        PE.mute(mm(b.ap[0:16, 128:256], LF[:, 0, :], ONES, True, False))
        tt = PE.do(mm(b.ap[0:16, 128:256], LF[:, 1, :], TRI, False, True))
        r1 = V.do(lambda e, b=b: e.tensor_copy(CTT[0:16, :], b.ap[0:16, 0:256]), tt)
        r2 = V.do(lambda e, b=b: e.tensor_scalar(NCT[0:16, :], b.ap[0:16, 0:256], -1.0, None, ALU.mult), tt)
        b.free = [r2]
        PE.wait(r1, r2, *fq_done)

        items = []

        def pair_items(dst, g, fn):
            box = {}

            def a():
                box["w"], box["t"] = take2()
                work_T(dst, 4 * g, fn)(box["w"], box["t"])

            def c():
                tt = work_T(dst, 4 * g + 2, fn)(box["w"], box["t"])
                give(tt)
                give(tt)
            items.extend([a, c])

        for g in range(2):
            pair_items(DQ, g, dil_qk(0.125))
        for g in range(2):
            pair_items(DK, g, dil_qk(None))
        for g in range(2):
            items.append(lambda g=g: tok_pair(DV, g, dq_done, None))

        def heads(qT, kT, vt, col0, mask, fox, items, t_first):
            fl, sm_, pv = {}, {}, {}
            ob = None
            for i in range(16 + 2):
                if i < 16:
                    b, f = bank()
                    PE.wait(*f)
                    rb, c = 64 * (i % 2), i // 2
                    q, k = qT[rb:rb + 64, c, :], kT[rb:rb + 64, c, :]
                    one = IDN[0:16, i:i + 1]
                    for c0, q0, n in ((0, 0, 128), (128, 128, 256)):
                        o = b.ap[:, c0:c0 + n]
                        fn = mm(o, q[:, q0:q0 + 128], k[:, 0:n], True, not fox)
                        if fox:
                            PE.mute(fn)
                            PE.mute(mm(o, one.broadcast_to([16, 128]), NCT[0:16, 0:n], False, False))
                            fn = mm(o, CTT[0:16, q0:q0 + 128], one.broadcast_to([16, n]), False, True)
                        tt = PE.do(fn)
                    es, r = soft(i, b, tt, mask, 1.0, ([fl[i - 2][0]] if i > 1 else []) + t_first)
                    sm_[i] = (es, r)
                    if items:
                        items.pop(0)()
                if 0 <= i - 1 < 16:
                    fl[i - 1] = flip(i - 1, sm_[i - 1][0], [pv[i - 3][0]] if i >= 3 else [])
                if i >= 2:
                    h = i - 2
                    b, f = bank()
                    PE.wait(*f)
                    PE.wait(fl[h][1])
                    PT = PTB[h % 2]
                    v0, v1 = vt[:, 0, h * 64:(h + 1) * 64], vt[:, 1, h * 64:(h + 1) * 64]
                    PE.mute(mm(b.ap[:, 0:64], PT[:, 0:128], v0, True, True))
                    PE.mute(mm(b.ap[:, 64:128], PT[:, 128:256], v0, True, False))
                    tt = PE.do(mm(b.ap[:, 64:128], PT[:, 256:384], v1, False, True))
                    for t in range(2):
                        r = V.do(lambda e, b=b, h=h, t=t: e.tensor_scalar(
                            O[:, t, col0 + h * 64:col0 + h * 64 + 64], b.ap[:, t * 64:t * 64 + 64],
                            rinv[:, h % 3, t:t + 1], None, ALU.mult), tt, sm_[h][1])
                    b.free = [r]
                    pv[h] = (tt, r)
            return pv[15][1]

        t_o1 = heads(FQ, FK, FV, 0, CM, True, items, list(t_ht))
        while items:
            items.pop(0)()
        PE.wait(*dq_done)
        t_o2 = heads(DQ, DK, DV, 1024, DM, False, [], [t_d2])
        ns = []
        for t in range(2):
            for part, to in ((0, t_o1), (1, t_o2)):
                ap = O[:, t, part * 1024:(part + 1) * 1024]
                r = stat_of(ap, 1024, 16 + 2 * t + part, at(W + (2 * t + part) * 1024, 1024), to, t_o2)
                rr = V.do(lambda e, ap=ap, t=t, part=part: e.tensor_scalar(
                    ap, ap, st[:, 16 + 2 * t + part:17 + 2 * t + part], None, ALU.mult), r)
            ns.append(rr)
        MT = HT
        t_mt = turn_over(O, 16, MT, colA[:, 88:104], None, ns, [t_o2])
        t_X = project_out(MT, 16, t_mt, None, None, [])

        after = [t_X]
        HN = at(YG, 2, D)
        QT = at(YG + 4096, 16, 256)
        t_ht = norm_T(t_X, colA[:, 64:80], None, [], 20)
        t_hn = []
        for t in range(2):
            t_hn.append(V.do(lambda e, t=t: e.tensor_tensor(HN[:, t, :], HN[:, t, :], GBB, ALU.mult), *t_ht, t_ff))
        KT = at(W, 16, 128)
        SC = at(W + 2048, D)
        CA = at(W + 4096, 8, 256)
        EQ = at(W + 6144, 128, 16)
        JUNK = at(W + 8192, D)
        pz = [W + 10240]

        def pt(*shape):
            o = pz[0]
            pz[0] += int(np.prod(shape))
            return at(o, *shape)

        VAL, IDX, IDF = pt(16, 16), pt(16, 16), GBA[:, 0:256].rearrange("p (a b) -> p a b", a=16)
        WK = pt(256)
        TV, TC = pt(8, 16), pt(128)
        II = [GBA[:, 256 + 128 * i:384 + 128 * i] for i in range(2)]
        IF = [GBA[:, 512 + 128 * i:640 + 128 * i] for i in range(2)]
        EF = [GBA[:, 768 + 128 * i:896 + 128 * i] for i in range(2)]
        EI = [pt(128) for _ in range(2)]
        GT = [pt(8, 16) for _ in range(2)]
        HD = [pt(128) for _ in range(2)]
        GS = pt(8)
        assert pz[0] <= 192 * KB, pz[0]

        wk_, tk_ = take()
        PE.wait(tk_, *t_ht)
        kt = []
        for g in range(4):
            b, f = bank()
            PE.wait(*f)
            for j in range(4):
                tt = PE.do(lambda e, b=b, g=g, j=j: e.transpose(
                    b.ap[:, j * 128:(j + 1) * 128], wk_[:, (4 * g + j) * 128:(4 * g + j + 1) * 128], IDN))
            r = V.do(lambda e, b=b, g=g: e.tensor_copy(KT[:, 4 * g:4 * g + 4, :].rearrange("p a b -> p (a b)"), b.ap), tt, t_o2, *t_mt)
            b.free = [r]
            kt.append(r)
        give(tt)
        for g in range(4):
            ws, tw = take2()
            for p in range(2):
                b, f = bank()
                PE.wait(*f)
                for j in range(2):
                    tt = proj_T(ws, 16, col128(512, (2 * p + j) * 128), HT, b.ap[:, j * 256:j * 256 + 256], tw)
                r = S.do(lambda e, b=b, c=4 * g + 2 * p: e.copy(QT[:, c:c + 2, :].rearrange("p a b -> p (a b)"), b.ap), tt, *t_ht)
                b.free = [r]
                kt.append(r)
            give(tt)
            give(tt)
        t_ring = tt
        PE.wait(*kt)
        IOTA = cst[:, K_IOTA:K_IOTA + 16]
        t_sel = [None, None]
        t_old = []
        for t in range(2):
            sc = []
            for g in range(4):
                b, f = bank()
                PE.wait(*f)
                for j in range(4):
                    tt = PE.do(mm(b.ap[:, j * 128:(j + 1) * 128], QT[:, 4 * g + j, t * 128:(t + 1) * 128], KT[:, 4 * g + j, :], True, True))
                r = S.do(lambda e, b=b, g=g: e.copy(SC[:, g * 512:(g + 1) * 512], b.ap), tt, *t_old)
                b.free = [r]
                sc.append(r)

            def top16(src, val, idx, wk, r):
                r = V.do(lambda e: e.max(val[:, 0:8], src), r)
                r = V.do(lambda e: e.max_index(idx[:, 0:8], val[:, 0:8], src), r)
                r = V.do(lambda e: e.match_replace(wk, val[:, 0:8], src, -3.0e38), r)
                r = V.do(lambda e: e.max(val[:, 8:16], wk), r)
                return V.do(lambda e: e.max_index(idx[:, 8:16], val[:, 8:16], wk), r)

            r = None
            for hp in range(16):
                r = top16(SC[:, hp * 128:(hp + 1) * 128], VAL[:, hp, :], IDX[:, hp, :].bitcast(U32), WK[:, 0:128],
                          [sc[hp // 4], r])
            t_old = [r]
            V2 = VAL.rearrange("p (h a) k -> p h a k", a=2)
            I2 = IDF.rearrange("p (h a) k -> p h a k", a=2)
            r = V.do(lambda e: e.tensor_copy(IDF, IDX.bitcast(U32)), r)
            r = V.do(lambda e: e.tensor_tensor(CA.rearrange("p h (i j) -> p h i j", i=16),
                                               V2[:, :, 0, :].unsqueeze(3).broadcast_to([128, 8, 16, 16]),
                                               V2[:, :, 1, :].unsqueeze(2).broadcast_to([128, 8, 16, 16]), ALU.add), r)
            for h in range(8):
                r = top16(CA[:, h, :], TV[:, h, :], TC[:, h * 16:(h + 1) * 16].bitcast(U32), WK, r)
            ra = V.do(lambda e: e.tensor_scalar(II[0].bitcast(U32), TC.bitcast(U32), 4, None, ALU.logical_shift_right), r)
            rb = V.do(lambda e: e.tensor_scalar(II[1].bitcast(U32), TC.bitcast(U32), 15, None, ALU.bitwise_and), r)
            for p in range(2):
                r = V.do(lambda e, p=p: e.tensor_copy(IF[p], II[p].bitcast(U32)), ra, rb)
                r = V.do(lambda e, p=p: e.tensor_tensor(EQ, IF[p].unsqueeze(2).broadcast_to([128, 128, 16]),
                                                        IOTA.unsqueeze(1).broadcast_to([128, 128, 16]), ALU.is_equal), r)
                E4 = EQ.rearrange("p (h k) i -> p h k i", h=8)
                r = V.do(lambda e, p=p, E4=E4: e.tensor_tensor(E4, E4, I2[:, :, p, :].unsqueeze(2).broadcast_to([128, 8, 16, 16]), ALU.mult), r)
                r = V.do(lambda e, p=p: e.tensor_reduce(EF[p], EQ, AX.X, ALU.add), r)
            t_sel[t] = V.do(lambda e, t=t: e.scalar_tensor_tensor(out=EI[t].bitcast(U32), in0=EF[0], scalar=128.0, in1=EF[1],
                                                                  op0=ALU.mult, op1=ALU.add), r)
            r = V.do(lambda e, t=t: e.tensor_tensor(GT[t], TV, TV[:, :, 0:1].broadcast_to([128, 8, 16]), ALU.subtract), t_sel[t])
            r = S.do(lambda e, t=t: e.activation(GT[t], GT[t], ACT.Exp), r)
            r = V.do(lambda e, t=t: e.tensor_reduce(GS, GT[t], AX.X, ALU.add), r)
            r = V.do(lambda e: e.reciprocal(GS, GS), r)
            t_gt = V.do(lambda e, t=t: e.tensor_tensor(GT[t], GT[t], GS.unsqueeze(2).broadcast_to([128, 8, 16]), ALU.mult), r)
        gsem = [DSem(f"g{i}") for i in range(NG)]
        gbuf = [at(RING + i * 2048, D) for i in range(NG)]
        last = [t_ring] * NG
        cnt = [0]
        t_f2 = G.dma(GBB, A["final_norm_gain_2"].partition_broadcast(128), DSem("df2"), *t_hn)

        def gather(tab, t, j):
            i = cnt[0] % NG
            cnt[0] += 1
            ds = gsem[i]
            G.wait(t_sel[t], last[i], t_ring)
            G.q.append(lambda e: e.indirect_dma_start(
                out=gbuf[i], out_offset=None, in_=tab,
                in_offset=bass.IndirectOffsetOnAxis(ap=EI[t][:, j:j + 1].bitcast(U32), axis=0)).then_inc(ds.sem, 16))
            ds.n += 16
            return i, (ds.sem, ds.n)

        down, up = A["peer_down_2"][0], A["peer_up_2"][0]
        todo = [(down, t, j) for t in range(2) for j in range(128)] + [(up, t, j) for t in range(2) for j in range(128)]
        co = [None, None]
        rprev = None
        for n, (tab, t, j) in enumerate(todo):
            i, tg = gather(tab, t, j)
            if tab is down:
                rprev = V.do(lambda e, i=i, t=t, j=j: e.tensor_tensor_reduce(
                    JUNK, gbuf[i], HN[:, t, :], 1.0, 0.0, ALU.mult, ALU.add, HD[t][:, j:j + 1]), tg, rprev)
                if j == 127:
                    r = S.do(lambda e, t=t: e.activation(HD[t], HD[t], ACT.Gelu_apprx_tanh), rprev)
                    co[t] = (r, t)
            else:
                if j == 0:
                    rprev = V.do(lambda e, t=t: e.tensor_tensor(HD[t], HD[t], GT[t].rearrange("p a b -> p (a b)"), ALU.mult),
                                 co[t][0], rprev)
                rprev = V.do(lambda e, i=i, t=t, j=j: e.scalar_tensor_tensor(
                    out=X[:, t, :], in0=gbuf[i], scalar=HD[t][:, j:j + 1], in1=X[:, t, :], op0=ALU.mult, op1=ALU.add),
                    tg, rprev)
                if j == 127:
                    r = stat_of(X[:, t, :], D, 24 + t, SC, rprev)
                    r = V.do(lambda e, t=t: e.scalar_tensor_tensor(out=X[:, t, :], in0=X[:, t, :], scalar=st[:, 24 + t:25 + t],
                                                                   in1=GBB, op0=ALU.mult, op1=ALU.mult), r, t_f2)
                    if t == 0:
                        dout = DSem("dout")
                    t_out = SP.dma(out[0][t * 128:(t + 1) * 128, :], X[:, t, :], dout, r)
                    rprev = r
            last[i] = rprev
        SP.wait(t_out)
        assert taken[0] == len(plan) == sent[0], (taken, len(plan), sent)

        block = ctx.enter_context(nc.Block())
        block.sync(SP.run)
        block.gpsimd(G.run)
        block.scalar(S.run)
        block.vector(V.run)
        block.tensor(PE.run)


_INS = ["x", "c", "positions", "ada_w", "ada_b", "norm_g", "ret_w_in", "ret_gn_g", "ret_w_out", "mla_w_in",
        "mla_q_norm_g", "mla_w_uq", "mla_kv_norm_g", "mla_w_ukv", "mla_w_out", "final_norm_g", "attn_norm_gain_2",
        "w_in_2", "forget_bias_2", "fox_out_gain_2", "dil_out_gain_2", "w_out_2", "ffn_norm_gain_2",
        "peer_query_2", "peer_sub_keys_2", "peer_down_2", "peer_up_2", "final_norm_gain_2"]


def kernel(**inputs):
    import concourse.bacc as _bacc
    from concourse.bass_utils import run_bass_kernel_spmd as _run

    nc = _bacc.Bacc("TRN2", target_bir_lowering=False, num_devices=1)
    arrays, A = {}, {}
    table, decay = tables()
    every = {n: np.ascontiguousarray(inputs[n]) for n in _INS}
    every["table"], every["decay"] = table, decay
    for name, a in every.items():
        arrays[f"in_{name}"] = a
        A[name] = nc.dram_tensor(f"in_{name}", a.shape, mybir.dt.from_np(a.dtype), kind="ExternalInput").ap()
    out = nc.dram_tensor("out_0", (1, 256, D), F, kind="ExternalOutput").ap()
    build(nc, A, out)
    r = _run(nc, [arrays], core_ids=[0])
    return r.results[0]["out_0"]
```

```python
from contextlib import ExitStack

import numpy as np
import concourse.bass as bass
from concourse import mybir
from concourse.alu_op_type import AluOpType as ALU

F = mybir.dt.float32
FR = mybir.dt.float32r
I32 = mybir.dt.int32
U32 = mybir.dt.uint32
ACT = mybir.ActivationFunctionType
AX = mybir.AxisListType

D = 2048
R = 4
NB = 8
NG = 8
EPS = 1e-6
TWO_PI_INV = 0.15915494309189535
C1 = 6.28125
C2 = 0.0019350051879882812
C3 = 3.0199157663e-07
MAGIC = 12582912.0
PI_IN = 3.1415925

K_ID, K_ONE, K_PM, K_PD, K_TRI = 0, 128, 256, 384, 512
K_CM, K_INV, K_IOTA = 640, 1024, 1026
K_DM, K_DC, K_DS = 1042, 1426, 1682
K_END = 1938


def tables():
    t = np.zeros((128, K_END), np.float32)
    p = np.arange(128)
    t[:, K_ID:K_ID + 128] = np.eye(128)
    t[:, K_ONE:K_ONE + 128] = 1.0
    pm = np.zeros((128, 128), np.float32)
    pd = np.zeros((128, 128), np.float32)
    for b in (0, 64):
        for i in range(32):
            pm[b + 32 + i, b + i] = -1.0
            pm[b + i, b + 32 + i] = 1.0
        for i in range(8):
            pd[b + 8 + i, b + i] = -1.0
            pd[b + i, b + 8 + i] = 1.0
    t[:, K_PM:K_PM + 128] = pm
    t[:, K_PD:K_PD + 128] = pd
    t[:, K_TRI:K_TRI + 128] = p[:, None] <= p[None, :]

    def both(mask, add):
        full = np.where(mask, add, np.float32(-1e30)).astype(np.float32)
        return np.concatenate([full[0:128, 0:128], full[128:256, :]], axis=1)

    q = np.arange(256)[:, None]
    k = np.arange(256)[None, :]
    t[:, K_CM:K_CM + 384] = both(k <= q, np.zeros((256, 256), np.float32))
    count = ((q - k <= 128) & (k <= q)).astype(int) + ((k <= q) & ((q - k) % 4 == 0)) + ((k <= q) & ((q - k) % 16 == 0))
    t[:, K_DM:K_DM + 384] = both(count > 0, np.log(np.maximum(count, 1)).astype(np.float32))
    inv = (500000.0 ** (-np.arange(0, 16, 2) / 16)).astype(np.float32)
    ang = np.arange(256, dtype=np.float32)[None, :] * inv[:, None]
    for b in (0, 8, 64, 72):
        t[b:b + 8, K_DC:K_DC + 256] = np.cos(ang.astype(np.float64))
        t[b:b + 8, K_DS:K_DS + 256] = np.sin(ang.astype(np.float64))
    for b in (16, 80):
        t[b:b + 48, K_DC:K_DC + 256] = 1.0
    t[:, K_INV] = (10000.0 ** (-np.arange(0, 256, 2) / 256)).astype(np.float32)
    t[:, K_INV + 1] = (10000.0 ** (-np.arange(0, 64, 2) / 64)).astype(np.float32)[p % 32]
    t[:, K_IOTA:K_IOTA + 16] = np.arange(16)
    g = np.log1p(-np.exp2(-5.0 - np.arange(8)))
    n = np.arange(256)[None, :] - p[:, None]
    dec = np.stack([np.where(n >= 0, np.exp(a * np.maximum(n, 0)), 0.0) for a in g], axis=1) / 16.0
    return t, dec.astype(np.float32).reshape(128, 2048)


class Bank:
    def __init__(self, ap):
        self.ap = ap
        self.free = []


def build(nc, A, out):
    ctx = ExitStack()
    with ctx:
        def sem(name):
            return ctx.enter_context(nc.semaphore(name))

        class Eng:

            def __init__(self, name):
                self.name, self.q, self.n, self.seen = name, [], 0, {}
                self.sem = sem("s_" + name)

            def wait(self, *toks):
                for t in toks:
                    if t is None:
                        continue
                    if isinstance(t, list):
                        self.wait(*t)
                        continue
                    s, v = t
                    if self.seen.get(id(s), 0) < v:
                        self.seen[id(s)] = v
                        self.q.append(lambda e, s=s, v=v: e.wait_ge(s, v))

            def do(self, fn, *toks):
                self.wait(*toks)
                self.n += 1
                self.q.append(lambda e: fn(e).then_inc(self.sem, 1))
                return (self.sem, self.n)

            def mute(self, fn, *toks):
                self.wait(*toks)
                self.q.append(fn)

            def dma(self, dst, src, s, *toks, **kw):
                self.wait(*toks)
                self.q.append(lambda e: e.dma_start(dst, src, **kw).then_inc(s.sem, 16))
                s.n += 16
                return (s.sem, s.n)

            def run(self, e):
                for fn in self.q:
                    fn(e)

        class DSem:
            def __init__(self, name):
                self.sem, self.n = sem(name), 0

        PE, V, S, G, SP = (Eng(n) for n in ("pe", "dve", "act", "pool", "sp"))

        base = (nc.sbuf_base + 63) // 64 * 64
        bounds = [0, 16, 48, 80, 112, 144, 160, 192, 207]
        arena, arena_r = {}, {}
        for a, z in zip(bounds, bounds[1:]):
            n = (z - a) * 256
            arena[a * 256, z * 256] = nc.alloc_sbuf_tensor_at(f"s{a}", [128, n], F, offset=base + a * 1024)
            if a in (16, 80, 112, 160):
                arena_r[a * 256, z * 256] = nc.alloc_sbuf_tensor_at(f"r{a}", [128, n], FR, offset=base + a * 1024)
        ps = ctx.enter_context(nc.psum_tensor("ps", [128, NB, 512], F))

        def at(off, *shape, of=arena):
            n = int(np.prod(shape))
            (lo, _), seg = next((k, v) for k, v in of.items() if k[0] <= off and off + n <= k[1])
            a = seg[:, off - lo:off - lo + n]
            if len(shape) == 2:
                a = a.rearrange("p (a b) -> p a b", a=shape[0])
            if len(shape) == 3:
                a = a.rearrange("p (a b c) -> p a b c", a=shape[0], b=shape[1])
            return a

        KB = 256
        X = at(0, 2, D)
        HT = (at(16 * KB, 16, 256, of=arena_r), at(32 * KB, 16, 256, of=arena_r))
        RAWS = 48 * KB
        HLS = 80 * KB
        YG = 112 * KB
        GBA = at(144 * KB, D)
        GBB = at(152 * KB, D)
        W = 160 * KB
        small = [192 * KB]

        def sm(*shape):
            off = small[0]
            small[0] += int(np.prod(shape))
            return at(off, *shape)

        cst = sm(K_DM)
        IDN = cst[:, K_ID:K_ID + 128]
        ONES = cst[:, K_ONE:K_ONE + 128]
        TRI = cst[:, K_TRI:K_TRI + 128]
        cosM, sinM = sm(256), sm(256)
        KR = sm(256)
        LB = [sm(384) for _ in range(2)]
        PTB = [sm(384) for _ in range(2)]
        colA, colB = sm(104), sm(128)
        cact, mod, gs = sm(16), sm(96), sm(16)
        st = sm(64)
        mn, sums, rinv = sm(2, 2), sm(2, 2), sm(3, 2)
        bst = sm(2, 6)
        mv = sm(2, 2)
        fb = sm(16)
        epsc = sm(1)
        assert small[0] <= 52992, small[0]

        banks = [Bank(ps[:, i, :]) for i in range(NB)]
        turn = [0]

        def bank():
            b = banks[turn[0] % NB]
            turn[0] += 1
            assert b.free is not None
            f, b.free = b.free, None
            return b, f

        plan = []
        raws = [(at(RAWS + i * 2048, 2048), DSem(f"w{i}")) for i in range(4)]
        parts = [(at(HLS + i * 4096, 2048, of=arena_r), at(HLS + i * 4096 + 2048, 2048, of=arena_r)) for i in range(2)]
        landed, raw_free, sent = {}, {}, [0]
        pos, conv, hl_free, hl_turn, split_of = [0], [0], [[], []], [0], {}

        def send():
            while sent[0] < len(plan) and (sent[0] < 4 or sent[0] - 4 in raw_free):
                i = sent[0]
                ap, ds = raws[i % 4]
                for dst, src in plan[i][2](ap):
                    t = SP.dma(dst, src, ds, *(raw_free[i - 4] if i >= 4 else []))
                landed[i] = t
                sent[0] += 1

        def free_raw(i, *toks):
            raw_free[i] = list(toks)
            send()

        def split_next():
            while conv[0] < len(plan) and plan[conv[0]][0] != "w":
                conv[0] += 1
            i = conv[0]
            if i >= len(plan) or i not in landed:
                return
            n = plan[i][1]
            raw = raws[i % 4][0][:, 0:n]
            j = hl_turn[0] % 2
            assert hl_free[j] is not None
            hi, lo = parts[j][0][:, 0:n], parts[j][1][:, 0:n]
            r = S.do(lambda e: e.copy(hi, raw), landed[i], *hl_free[j])
            q = V.do(lambda e: e.tensor_tensor(lo, raw, hi.bitcast(F), ALU.subtract), r)
            hl_free[j] = None
            hl_turn[0] += 1
            split_of[i] = (hi, lo, [r, q], j)
            conv[0] += 1
            free_raw(i, q)

        def take_w():
            ada_units()
            i = pos[0]
            assert plan[i][0] == "w"
            if i not in split_of:
                split_next()
            hi, lo, toks, j = split_of[i]
            pos[0] += 1
            PE.wait(*toks)
            return hi, lo, j

        def give_w(j, tok):
            hl_free[j] = [tok]
            split_next()
            ada_units()

        def ada_units():
            while pos[0] < len(plan) and plan[pos[0]][0] == "ada":
                ada_unit(pos[0], *plan[pos[0]][3])
                pos[0] += 1

        def rows(src, k0, nk, c, n):
            return src[k0:k0 + nk * 128, c:c + n].rearrange("(k p) n -> p k n", p=128)

        def unit(src, k0, c, n=512, nk=4):
            return lambda ap: [(ap[:, 0:nk * n].rearrange("p (k n) -> p k n", k=nk), rows(src, k0, nk, c, n))]

        ticks = []

        def addw(fn, n=2048):
            plan.append(("w", n, fn, None))
            if ticks and sum(p[0] == "w" for p in plan) % 2 == 0:
                plan.append(ticks.pop(0))

        def ada_entry(layer, g, u):
            return ("ada", 2048, unit(A["ada_w"][layer], u * 512, g * 512), (layer, g, u))

        def cols512(src, c, nu=4):
            for u in range(nu):
                addw(unit(src, u * 512, c))

        ret_in, ret_out = A["ret_w_in"][0], A["ret_w_out"][0]
        mla_in, mla_out = A["mla_w_in"][0], A["mla_w_out"][0]
        uq, ukv = A["mla_w_uq"][0], A["mla_w_ukv"][0]
        w2, wo2, pq = A["w_in_2"][0], A["w_out_2"][0], A["peer_query_2"][0]

        def qk_unit(h, u):
            def f(ap):
                v = ap.rearrange("p (k n) -> p k n", k=4)
                return [(v[:, :, 0:256], rows(ret_in, u * 512, 4, h * 256, 256)),
                        (v[:, :, 256:512], rows(ret_in, u * 512, 4, 2048 + h * 256, 256))]
            return f

        def head_unit(src, c, hw, o, n):
            def f(ap):
                v = ap[:, 0:16 * n].rearrange("p (k h n) -> p k h n", k=4, h=4)
                return [(v[:, k], src[k * 128:(k + 1) * 128, c:c + 4 * hw].rearrange(
                    "p (h n) -> p h n", h=4)[:, :, o:o + n]) for k in range(4)]
            return f

        def kr_unit(ap):
            v = ap.rearrange("p (k n) -> p k n", k=16)
            return [(v[:, :, j * 64:(j + 1) * 64], rows(mla_in, 0, 16, 1024, 64)) for j in range(2)]

        for g in range(8):
            for u in range(4):
                plan.append(ada_entry(0, g, u))
        for n in range(16):
            for u in range(4):
                ticks.append(ada_entry(0, 8 + n, u) if n < 4 else ada_entry(1, n - 4, u))
        for h in range(8):
            for u in range(4):
                addw(qk_unit(h, u))
            cols512(ret_in, 4096 + h * 512)
            cols512(ret_in, 8192 + h * 512)
        for n in range(4):
            cols512(ret_out, n * 512, 8)
        assert not ticks
        cols512(mla_in, 0)
        cols512(mla_in, 512)
        cols512(mla_in, 1088)
        addw(kr_unit)
        for g in range(1, 4):
            cols512(mla_in, 1088 + g * 512)
        for g in range(4):
            addw(head_unit(uq, g * 768, 192, 0, 128))
            addw(head_unit(uq, g * 768, 192, 128, 64), 1024)
            addw(head_unit(ukv, g * 1024, 256, 0, 128))
            addw(head_unit(ukv, g * 1024, 256, 128, 128))
        for n in range(4):
            cols512(mla_out, n * 512)
        addw(unit(w2, 0, 3072, 16, 16), 256)
        for g in range(6):
            cols512(w2, g * 512)
        for g in range(6):
            cols512(w2, 3088 + g * 512)
        for n in range(4):
            cols512(wo2, n * 512)
        plan.append(("raw", 2048, lambda ap: [(ap.rearrange("p (h n) -> p h n", h=16),
                                               A["peer_sub_keys_2"][0].rearrange("h a n c -> n (h a) c"))], None))
        for g in range(4):
            cols512(pq, g * 512)

        dc, dx, dr, dp, dg, dfb = (DSem(n) for n in ("dc", "dx", "dr", "dp", "dg", "dfb"))
        ROWA, ROWB = at(YG, 128), at(YG + 128, 128)
        PI, PF = at(YG + 256, 256), at(YG + 512, 256)
        t_c = SP.dma(cst, A["table"][:, 0:K_DM], dc)
        r0 = 0
        for name, n in (("c", 16), ("norm_g", 32), ("attn_norm_gain_2", 16), ("ffn_norm_gain_2", 16),
                        ("mla_q_norm_g", 4), ("mla_kv_norm_g", 4), ("fox_out_gain_2", 8), ("dil_out_gain_2", 8)):
            t_r = SP.dma(ROWA[r0:r0 + n, :], A[name].rearrange("a (n p) -> (a n) p", p=128), dr)
            r0 += n
        t_r = SP.dma(ROWB[0:96, :], A["ada_b"].rearrange("a (n p) -> (a n) p", p=128), dr)
        t_r = SP.dma(ROWB[96:128, :], A["ret_gn_g"].rearrange("a (n p) -> (a n) p", p=128), dr)
        send()
        t_x = G.dma(X, A["x"][0].rearrange("(t p) d -> p t d", p=128), dx)
        t_p = G.dma(PI.bitcast(I32), A["positions"][0].partition_broadcast(128), dp)
        DTAB = at(W, 8, 256)
        cosR, sinR = at(W + 2048, 256), at(W + 2304, 256)
        t_d = G.dma(DTAB.rearrange("p a b -> p (a b)"), A["decay"], dg)
        t_fb = G.dma(fb, A["forget_bias_2"][0].partition_broadcast(128), dfb)

        t_eps = V.do(lambda e: e.memset(epsc, EPS))

        def mm(o, l, r, start, stop):
            return lambda e: e.matmul(o, l, r, start=start, stop=stop)

        b, f = bank()
        PE.wait(t_c, t_r)
        PE.do(lambda e, b=b: e.transpose(b.ap[:, 0:104], ROWA[0:104, :], IDN[0:104, 0:104]), *f)
        t = PE.do(lambda e, b=b: e.transpose(b.ap[:, 128:256], ROWB, IDN))
        t_ca = V.do(lambda e, b=b: e.tensor_copy(colA, b.ap[:, 0:104]), t)
        t_cb = V.do(lambda e, b=b: e.tensor_copy(colB, b.ap[:, 128:256]), t)
        b.free = [t_cb]
        t_cact = S.do(lambda e: e.activation(cact, colA[:, 0:16], ACT.Silu), t_ca)

        t = V.do(lambda e: e.tensor_copy(PF, PI.bitcast(I32)), t_p)
        t_trig = []
        AN, KK, RR = (at(YG + (768 + 256 * i), 256) for i in range(3))
        RQ = [at(YG + 1536 + 256 * i, 256) for i in range(4)]
        k = 0
        for j, (co, si) in enumerate(((cosR, sinR), (cosM, sinM))):
            t = V.do(lambda e, j=j: e.tensor_scalar(AN, PF, cst[:, K_INV + j:K_INV + j + 1], None, ALU.mult), t, t_c)
            for dst, sh in ((co, 0.25), (si, 0.0)):
                q = RQ[k]
                k += 1
                t = V.do(lambda e, sh=sh: e.tensor_scalar(KK, AN, TWO_PI_INV, sh, ALU.mult, ALU.add), t)
                t = V.do(lambda e: e.tensor_scalar(KK, KK, MAGIC, None, ALU.add), t)
                t = V.do(lambda e: e.tensor_scalar(KK, KK, MAGIC, None, ALU.subtract), t)
                t = V.do(lambda e: e.scalar_tensor_tensor(out=RR, in0=KK, scalar=-C1, in1=AN, op0=ALU.mult, op1=ALU.add), t)
                t = V.do(lambda e: e.scalar_tensor_tensor(out=RR, in0=KK, scalar=-C2, in1=RR, op0=ALU.mult, op1=ALU.add), t)
                t = V.do(lambda e: e.scalar_tensor_tensor(out=RR, in0=KK, scalar=-C3, in1=RR, op0=ALU.mult, op1=ALU.add), t)
                if sh:
                    t = V.do(lambda e: e.tensor_scalar(RR, RR, 1.5707963267948966, None, ALU.add), t)
                t = V.do(lambda e, q=q: e.tensor_scalar(q, RR, PI_IN, -PI_IN, ALU.min, ALU.max), t)
                t_trig.append(S.do(lambda e, q=q, dst=dst: e.activation(dst, q, ACT.Sin), t))

        acc_free, fin = [[], []], []
        t_mods = {}

        def ada_unit(i, layer, g, u):
            j = (layer * 12 + g) % 2
            acc = GBB[:, j * 512:(j + 1) * 512]
            ada_finish()
            r = acc_free[j] if u == 0 else fin_prev[j]
            for kc in range(4):
                k = u * 4 + kc
                w = raws[i % 4][0][:, kc * 512:(kc + 1) * 512]
                if k == 0:
                    r = V.do(lambda e, w=w: e.tensor_scalar(acc, w, cact[:, 0:1], None, ALU.mult), r, landed[i], t_cact)
                else:
                    r = V.do(lambda e, w=w, k=k: e.scalar_tensor_tensor(out=acc, in0=w, scalar=cact[:, k:k + 1], in1=acc,
                                                                        op0=ALU.mult, op1=ALU.add), r, landed[i])
            fin_prev[j] = r
            free_raw(i, r)
            if u == 3:
                b, f = bank()
                PE.wait(*f)
                PE.wait(r)
                for m in range(4):
                    t = PE.do(mm(b.ap[:, m:m + 1], acc[:, m * 128:(m + 1) * 128], ONES[:, 0:1], True, True))
                acc_free[j] = t
                b.free = []
                fin.append((layer, g, b, t))

        fin_prev = [None, None]

        def ada_finish():
            while fin:
                layer, g, b, t = fin.pop(0)
                c = layer * 48 + g * 4
                r = V.do(lambda e, b=b, c=c: e.tensor_tensor(mod[:, c:c + 4], b.ap[:, 0:4], colB[:, c:c + 4], ALU.add), t, t_cb)
                b.free = [r]
                t_mods[(layer, g)] = r

        def gate_rows(layer, dst, t_gate, DG, *after):
            toks = []
            prev = list(after)
            for g in range(4):
                ts = []
                for j in range(4):
                    c = layer * 48 + 32 + 4 * g + j
                    ts.append(V.do(lambda e, j=j, c=c: e.tensor_scalar(DG[:, j, :], IDN, mod[:, c:c + 1], None, ALU.mult),
                                   t_gate, *prev))
                b, f = bank()
                PE.wait(*f)
                t = PE.do(mm(b.ap, ONES, DG.rearrange("p a b -> p (a b)"), True, True), *ts)
                prev = [t]
                r = S.do(lambda e, b=b, g=g: e.copy(dst[:, g * 512:(g + 1) * 512], b.ap), t, *after)
                b.free = [r]
                toks.append(r)
            return toks[-1]

        ada_units()
        ada_finish()
        t_mod = t_mods[(0, 7)]

        def stat_of(src, n, col, junk, *after):
            t = S.do(lambda e: e.activation(junk, src, ACT.Square, scale=float(n) ** -0.5, accum_out=st[:, col:col + 1]), *after)
            t = S.do(lambda e: e.activation(st[:, col:col + 1], st[:, col:col + 1], ACT.Sqrt, bias=epsc), t, t_eps)
            return V.do(lambda e: e.reciprocal(st[:, col:col + 1], st[:, col:col + 1]), t)

        def turn_over(src, nk, dst, scale, bias, waits, after, tmp):
            res = []
            used = [list(after), list(after)]
            for p in range(nk // 2):
                b, f = bank()
                PE.wait(*f)
                for t in range(2):
                    for j in range(2):
                        k = 2 * p + j
                        tt = PE.do(lambda e, b=b, j=j, t=t, k=k: e.transpose(
                            b.ap[:, j * 256 + t * 128:j * 256 + t * 128 + 128],
                            src[:, t, k * 128:(k + 1) * 128], IDN), waits[t])
                rs = []
                T = at(tmp + 512 * (p % 2), 512)
                for j in range(2):
                    k = 2 * p + j
                    o, i_ = T[:, j * 256:(j + 1) * 256], b.ap[:, j * 256:j * 256 + 256]
                    sc = scale[:, k:k + 1]
                    if p % 2 == 0:
                        if bias is None:
                            fn = lambda e, o=o, i_=i_, sc=sc: e.tensor_scalar(o, i_, sc, None, ALU.mult)
                        else:
                            fn = lambda e, o=o, i_=i_, sc=sc, bi=bias[:, k:k + 1]: e.tensor_scalar(
                                o, i_, sc, bi, ALU.mult, ALU.add)
                        rs.append(V.do(fn, tt, *used[0]))
                    else:
                        if bias is None:
                            fn = lambda e, o=o, i_=i_, sc=sc: e.activation(o, i_, ACT.Copy, scale=sc)
                        else:
                            fn = lambda e, o=o, i_=i_, sc=sc, bi=bias[:, k:k + 1]: e.activation(
                                o, i_, ACT.Identity, scale=sc, bias=bi)
                        rs.append(S.do(fn, tt, *used[1]))
                b.free = rs
                h, lo = (x[:, 2 * p:2 * p + 2, :].rearrange("p a b -> p (a b)") for x in dst)
                r = S.do(lambda e, h=h, T=T: e.copy(h, T), *rs, *after)
                q = V.do(lambda e, h=h, lo=lo, T=T: e.tensor_tensor(lo, T, h.bitcast(F), ALU.subtract), r, *rs)
                used[p % 2] = [q]
                res = [r, q]
            return res

        def split(src, hi, lo, n, after):
            res = []
            for i in range(0, n, 1024):
                r = S.do(lambda e, i=i: e.copy(hi[:, i:i + 1024], src[:, i:i + 1024]), *after)
                q = V.do(lambda e, i=i: e.tensor_tensor(lo[:, i:i + 1024], src[:, i:i + 1024],
                                                        hi[:, i:i + 1024].bitcast(F), ALU.subtract), r, *after)
                res.append([r, q])
            return res

        def norm_T(t_X, scale, bias, after, stat0=0):
            XN = at(YG, 2, D)
            ws = []
            for t in range(2):
                r = stat_of(X[:, t, :], D, stat0 + t, XN[:, t, :], t_X, *after)
                ws.append(V.do(lambda e, t=t: e.tensor_scalar(XN[:, t, :], X[:, t, :], st[:, stat0 + t:stat0 + t + 1],
                                                              None, ALU.mult), r))
            return turn_over(XN, 16, HT, scale, bias, ws, after, YG + 4096)

        def mod_scale(layer, t_mod, *after):
            c = layer * 48 + 16
            return V.do(lambda e: e.scalar_tensor_tensor(out=gs, in0=mod[:, c:c + 16], scalar=1.0,
                                                         in1=colA[:, 16 + 16 * layer:32 + 16 * layer],
                                                         op0=ALU.add, op1=ALU.mult), t_mod, t_ca, *after)

        t_gs = mod_scale(0, t_mod)
        t_ht = norm_T(t_x, gs, mod[:, 0:16], [t_gs, t_trig[-1]] + t_trig)

        def three(o, l, r, start, stop):
            (lh, ll), (rh, rl) = l, r
            ops = ((lh, rh), (lh, rl), (ll, rh))
            for i, (a, c) in enumerate(ops):
                fn = (lambda e, a=a, c=c, i=i: e.matmul(o, a, c, start=start and i == 0, stop=stop and i == 2,
                                                        skip_group_check=True))
                if stop and i == 2:
                    return PE.do(fn)
                PE.mute(fn)

        def g_proj_T(x, evac, units=4, nk=4, ms=4, m_per=2):
            bs = []
            for p in range((ms + 1) // 2):
                b, f = bank()
                PE.wait(*f)
                bs.append(b)
            wd = ms * 128
            for u in range(units):
                hi, lo, j = take_w()
                for m in range(ms):
                    o = bs[m // 2].ap[:, (m % 2) * 256:(m % 2) * 256 + 256]
                    for k in range(nk):
                        c = k * wd + m * 128
                        kc = u * nk + k
                        last = u == units - 1 and k == nk - 1
                        tt = three(o, (hi[:, c:c + 128], lo[:, c:c + 128]), (x[0][:, kc, :], x[1][:, kc, :]),
                                   m % 2 == 0 and kc == 0, last)
                        if k == nk - 1 and m == ms - 1 and not last:
                            tt = mark()
                give_w(j, tt)
                if u < units - 1:
                    yield
            for p, b in enumerate(bs):
                b.free = evac(p, b, tt)
            yield

        def mark():
            fn = PE.q.pop()
            return PE.do(fn)

        def g_proj_tok(x, evac, units=4):
            bs = []
            for t in range(2):
                b, f = bank()
                PE.wait(*f)
                bs.append(b)
            for u in range(units):
                hi, lo, j = take_w()
                for t in range(2):
                    for k in range(4):
                        kc = u * 4 + k
                        ts_ = slice(t * 128, (t + 1) * 128)
                        last = u == units - 1 and k == 3
                        tt = three(bs[t].ap, (x[0][:, kc, ts_], x[1][:, kc, ts_]),
                                   (hi[:, k * 512:(k + 1) * 512], lo[:, k * 512:(k + 1) * 512]), kc == 0, last)
                        if last and t == 0:
                            t0 = tt
                        if k == 3 and t == 1 and not last:
                            tt = mark()
                give_w(j, tt)
                if u < units - 1:
                    yield
            bs[0].free = evac(0, bs[0], t0)
            bs[1].free = evac(1, bs[1], tt)
            yield

        def run(g):
            for _ in g:
                pass

        o = W + 2560
        QK = at(o, 4, 256)
        T1, T2 = at(o + 1024, 2, 256), at(o + 1536, 2, 256)
        VV = at(o + 2048, 2, 512)
        SD = at(o + 3072, 384)
        SG = at(o + 3456, 4, 256)
        YN = at(o + 4480, 2, 512)
        assert 2560 + 5504 <= 32 * KB
        YT = at(YG, 32, 256)

        def bc2(a):
            return a.unsqueeze(1).broadcast_to([128, 2, 256])

        state = {"sd": None, "yt": [], "gate": None, "t_y": None}
        PE.wait(*t_ht)

        def ret_back(h, ty):
            rs = []
            for p in range(2):
                b, f = bank()
                PE.wait(*f)
                for t in range(2):
                    for j in range(2):
                        k = 2 * p + j
                        tt = PE.do(lambda e, b=b, j=j, t=t, k=k: e.transpose(
                            b.ap[:, j * 256 + t * 128:j * 256 + t * 128 + 128],
                            YN[:, t, k * 128:(k + 1) * 128], IDN), ty[t])
                rr = []
                for j in range(2):
                    k = 2 * p + j
                    g = 96 + h * 4 + k
                    rr.append(V.do(lambda e, b=b, j=j, k=k, g=g: e.scalar_tensor_tensor(
                        out=YT[:, h * 4 + k, :], in0=b.ap[:, j * 256:j * 256 + 256], scalar=colB[:, g:g + 1],
                        in1=SG[:, k, :], op0=ALU.mult, op1=ALU.mult), tt, *state["sg"]))
                b.free = rr
                rs += rr
            state["yt"] = rs

        ty = None
        for h in range(8):
            qs = []

            def ev_qk(part, b, tt):
                v = b.ap.rearrange("p (a b) -> p a b", a=2)
                a1 = V.do(lambda e: e.tensor_tensor(T1, v, bc2(cosR), ALU.mult), tt, *t_trig)
                a2 = V.do(lambda e: e.tensor_tensor(T2, v, bc2(sinR), ALU.mult), tt)
                V.do(lambda e: e.tensor_tensor(QK[:, 2 * part, :], T1[:, 0, :], T2[:, 1, :], ALU.subtract), a1, a2)
                qs.append(V.do(lambda e: e.tensor_tensor(QK[:, 2 * part + 1, :], T1[:, 1, :], T2[:, 0, :], ALU.add)))
                V.wait(qs[-1])
                return [a2]

            run(g_proj_T(HT, ev_qk))
            if h:
                ret_back(h - 1, ty)
            vs = []

            def ev(t, b, tt):
                vs.append(S.do(lambda e: e.copy(VV[:, t, :], b.ap), tt))
                return [vs[-1]]

            run(g_proj_tok(HT, ev))
            b, f = bank()
            PE.wait(*f)
            PE.wait(*qs)
            for j in range(2):
                PE.mute(mm(b.ap[:, 0:256], QK[:, 2 + j, 0:128], QK[:, j, :], j == 0, j == 1))
            for j in range(2):
                fn = mm(b.ap[:, 256:384], QK[:, 2 + j, 128:256], QK[:, j, 128:256], j == 0, j == 1)
                tt = PE.do(fn)
            a1 = V.do(lambda e, b=b, h=h: e.tensor_tensor(SD[:, 0:256], b.ap[:, 0:256], DTAB[:, h, :], ALU.mult), tt, t_d)
            a2 = V.do(lambda e, b=b, h=h: e.tensor_tensor(SD[:, 256:384], b.ap[:, 256:384], DTAB[:, h, 0:128], ALU.mult))
            b.free = [a2]
            sg = []

            def ev_g(p, b, tt):
                sg.append(S.do(lambda e: e.activation(
                    SG[:, 2 * p:2 * p + 2, :].rearrange("p a b -> p (a b)"), b.ap, ACT.Silu), tt, *state["yt"]))
                return [sg[-1]]

            run(g_proj_T(HT, ev_g))
            state["sg"] = sg
            ty = []
            for t in range(2):
                b, f = bank()
                PE.wait(*f)
                PE.wait(a2, *vs)
                if t == 0:
                    tt = PE.do(mm(b.ap, SD[:, 0:128], VV[:, 0, :], True, True))
                else:
                    PE.mute(mm(b.ap, SD[:, 128:256], VV[:, 0, :], True, False))
                    tt = PE.do(mm(b.ap, SD[:, 256:384], VV[:, 1, :], False, True))
                r = V.do(lambda e, b=b, t=t: e.bn_stats(bst[:, t, :], b.ap), tt)
                r = V.do(lambda e, t=t: e.bn_aggr(mv[:, t, :], bst[:, t, :]), r)
                r = S.do(lambda e, t=t: e.activation(st[:, 8 + t:9 + t], mv[:, t, 1:2], ACT.Sqrt, bias=epsc), r, t_eps)
                r = V.do(lambda e, t=t: e.reciprocal(st[:, 8 + t:9 + t], st[:, 8 + t:9 + t]), r)
                r = V.do(lambda e, b=b, t=t: e.tensor_scalar(YN[:, t, :], b.ap, mv[:, t, 0:1], st[:, 8 + t:9 + t],
                                                             ALU.subtract, ALU.mult), r)
                b.free = [r]
                ty.append(r)
            if h == 4:
                t_gate = gate_rows(0, GBA, t_mods[(0, 11)], at(152 * KB + 1024, 4, 128))
        ret_back(7, ty)
        YS = (at(16 * KB, 32, 256, of=arena_r), at(W, 32, 256, of=arena_r))

        def flat(x):
            return x.rearrange("p a b -> p (a b)")

        t_sp = split(flat(YT), flat(YS[0]), flat(YS[1]), 8192, state["yt"])

        def project_out(yT, nk, t_in, gate, t_gate, t_X):
            OT = at(YG, 2, 512)
            last = [None, None]
            for n in range(4):
                done = []

                def ev(t, b, tt, n=n):
                    xs = X[:, t, n * 512:(n + 1) * 512]
                    if gate is None:
                        r = V.do(lambda e: e.tensor_tensor(xs, b.ap, xs, ALU.add), tt, *t_X)
                        last[t] = r
                        return [r]
                    gg = gate[:, n * 512:(n + 1) * 512]
                    q = V.do(lambda e: e.tensor_tensor(OT[:, t, :], b.ap, gg, ALU.mult), tt, t_gate, last[t], *t_X)
                    r = V.do(lambda e: e.tensor_tensor(xs, OT[:, t, :], xs, ALU.add), q)
                    last[t] = r
                    return [q]

                g = g_proj_tok(yT, ev, nk // 4)
                for u in range(nk // 4):
                    if n == 0:
                        PE.wait(*t_in[u])
                    next(g)
            return last[1]

        t_X = project_out(YS, 32, t_sp, GBA, t_gate, t_sp[-1])
        t_w_end = t_X
        ada_finish()
        t_mod = t_mods[(1, 11)]

        t_gs = mod_scale(1, t_mod, *t_ht)
        t_ht = norm_T(t_X, gs, mod[:, 48:64], [t_gs], 2)
        t_gate = gate_rows(1, GBB, t_mod, at(W, 4, 128), t_X)
        PE.wait(*t_ht)
        SGM = at(YG, 16, 256)
        CT = (at(YG + 4096, 8, 256, of=arena_r), at(YG + 6144, 8, 256, of=arena_r))
        QN = [at(W + 1024 * i, 4, 256) for i in range(2)]
        KN = [at(W + 2048 + 1024 * i, 4, 256) for i in range(2)]
        VM = [at(W + 4096 + 1024 * i, 2, 512) for i in range(2)]
        QR = [at(W + 6144 + 512 * i, 2, 256) for i in range(2)]
        CTOK = GBA.rearrange("p (t n) -> p t n", t=2)
        RAW = at(144 * KB, 512)
        RT = [at(144 * KB + 512 + 512 * i, 512) for i in range(2)]
        cs = []
        for part in range(2):
            def ev(t, b, tt, part=part):
                d = CTOK[:, t, part * 512:(part + 1) * 512]
                c = 4 + 2 * part + t
                r = stat_of(b.ap, 512, c, d, tt, t_w_end)
                cs.append(V.do(lambda e: e.tensor_scalar(d, b.ap, st[:, c:c + 1], None, ALU.mult), r))
                return [cs[-1]]

            run(g_proj_tok(HT, ev))

        sgt = {}

        def gate_ev(g):
            def ev(p, b, tt):
                m = 4 * g + 2 * p
                r = S.do(lambda e: e.activation(flat(SGM[:, m:m + 2, :]), b.ap, ACT.Silu), tt)
                sgt[m] = sgt[m + 1] = r
                return [r]
            return ev

        run(g_proj_T(HT, gate_ev(0)))

        def rotate(b, m, dst, perm, co, si, tt, raw, rt, sc, after):
            n = 256 * m

            def v(x):
                return x[:, 0:n].rearrange("p (a b) -> p a b", a=m)

            def bc(x):
                return x.unsqueeze(1).broadcast_to([128, m, 256])

            r = S.do(lambda e: e.copy(raw[:, 0:n], b.ap[:, 0:n]), tt, *after)
            p = PE.do(mm(b.ap[:, 0:n], perm, raw[:, 0:n], True, True), r)
            a = V.do(lambda e: e.tensor_tensor(v(rt[0]), v(raw), bc(co), ALU.mult), r, *after)
            c = V.do(lambda e: e.tensor_tensor(v(rt[1]), v(b.ap), bc(si), ALU.mult), p)
            if sc is None:
                return V.do(lambda e: e.tensor_tensor(dst, rt[0][:, 0:n], rt[1][:, 0:n], ALU.add), a, c)
            c = V.do(lambda e: e.tensor_tensor(rt[0][:, 0:n], rt[0][:, 0:n], rt[1][:, 0:n], ALU.add), a, c)
            return V.do(lambda e: e.tensor_scalar(dst, rt[0][:, 0:n], sc, None, ALU.mult), c)

        PMm = cst[:, K_PM:K_PM + 128]
        t_ct = turn_over(CTOK, 8, CT, colA[:, 80:88], None, [cs[2], cs[3]], [t_w_end, t_gate] + cs, W)

        def ev(p, b, tt):
            t_krs.append(rotate(b, 1, KR, PMm, cosM, sinM, tt, RAW, RT, None, t_ct))
            return [t_krs[-1]]

        t_krs = []
        run(g_proj_T(HT, ev, units=1, nk=16, ms=1))
        for g in range(1, 4):
            run(g_proj_T(HT, gate_ev(g)))
        rot = [t_krs[0]]
        got = {}

        def group(g, free):
            a = g % 2
            ts = got[g] = []

            def e_q(p, b, tt):
                ts.append(S.do(lambda e: e.copy(flat(QN[a][:, 2 * p:2 * p + 2, :]), b.ap), tt, *free, *t_ct))
                return [ts[-1]]

            def e_r(p, b, tt):
                rot[0] = rotate(b, 2, flat(QR[a]), PMm, cosM, sinM, tt, RAW, RT, None, [rot[0], *free])
                ts.append(rot[0])
                return [rot[0]]

            def e_k(p, b, tt):
                ts.append(V.do(lambda e: e.tensor_copy(flat(KN[a][:, 2 * p:2 * p + 2, :]), b.ap), tt, *free))
                return [ts[-1]]

            def e_v(t, b, tt):
                ts.append(S.do(lambda e: e.copy(VM[a][:, t, :], b.ap), tt, *free))
                return [ts[-1]]

            PE.wait(*t_ct)
            ck = (CT[0][:, 4:8, :], CT[1][:, 4:8, :])
            yield from g_proj_T(CT, e_q, units=1)
            yield from g_proj_T(CT, e_r, units=1, ms=2)
            yield from g_proj_T(ck, e_k, units=1)
            yield from g_proj_tok(ck, e_v, units=1)

        run(group(0, []))

        CM = cst[:, K_CM:K_CM + 384]

        def soft(i, b, tt, mask, scale, t_old):
            L = LB[i % 2]
            j = i % 2
            es = []
            rr = []
            for t, (c0, c1) in enumerate(((0, 128), (128, 384))):
                rr.append(V.do(lambda e, c0=c0, c1=c1, t=t: e.tensor_tensor_reduce(
                    L[:, c0:c1], b.ap[:, c0:c1], mask[:, c0:c1], -scale, 3e38, ALU.add, ALU.min,
                    mn[:, j, t:t + 1]), tt, *t_old))
            for t, (c0, c1) in enumerate(((0, 128), (128, 384))):
                es.append(S.do(lambda e, c0=c0, c1=c1, t=t: e.activation(
                    L[:, c0:c1], L[:, c0:c1], ACT.Exp, bias=mn[:, j, t:t + 1], scale=-1.0,
                    accum_out=sums[:, j, t:t + 1]), rr[t]))
            b.free = [rr[1]]
            r = V.do(lambda e: e.reciprocal(rinv[:, i % 3, :], sums[:, j, :]), es[0], es[1])
            return es, r

        def flip(i, waits, t_old):
            b, f = bank()
            PE.wait(*f)
            L = LB[i % 2]
            PE.wait(*waits)
            for c in range(3):
                tt = PE.do(lambda e, c=c, b=b: e.transpose(b.ap[:, c * 128:(c + 1) * 128], L[:, c * 128:(c + 1) * 128], IDN))
            r = S.do(lambda e, b=b: e.copy(PTB[i % 2], b.ap[:, 0:384]), tt, *t_old)
            b.free = [r]
            return tt, r

        fl = {}
        sm_ = {}
        og = {}
        ISQ = float(192 ** -0.5)
        nxt = None
        for i in range(16 + 2):
            if i < 16:
                g = i // 4
                if i % 4 == 0:
                    PE.wait(*got[g])
                b, f = bank()
                PE.wait(*f)
                rb = 64 * (i % 2)
                q1, q2 = QN[g % 2][:, i % 4, :], QR[g % 2][rb:rb + 64, (i % 4) // 2, :]
                k1, k2 = KN[g % 2][:, i % 4, :], KR[rb:rb + 64, :]
                PE.mute(mm(b.ap[:, 0:128], q1[:, 0:128], k1[:, 0:128], True, False))
                PE.mute(mm(b.ap[:, 0:128], q2[:, 0:128], k2[:, 0:128], False, True))
                PE.mute(mm(b.ap[:, 128:384], q1[:, 128:256], k1, True, False))
                tt = PE.do(mm(b.ap[:, 128:384], q2[:, 128:256], k2, False, True))
                es, r = soft(i, b, tt, CM, ISQ, [fl[i - 2][0]] if i > 1 else [])
                ns = []
                for t, (c0, c1) in enumerate(((0, 128), (128, 384))):
                    ns.append(V.do(lambda e, c0=c0, c1=c1, t=t, i=i: e.tensor_scalar(
                        LB[i % 2][:, c0:c1], LB[i % 2][:, c0:c1], rinv[:, i % 3, t:t + 1], None, ALU.mult), r))
                sm_[i] = ns
            if 0 <= i - 1 < 16:
                fl[i - 1] = flip(i - 1, sm_[i - 1], [og[i - 3][0]] if i >= 3 else [])
            if i >= 2:
                h = i - 2
                b, f = bank()
                PE.wait(*f)
                PE.wait(fl[h][1])
                PT = PTB[h % 2]
                vm = VM[(h // 4) % 2]
                v0, v1 = (vm[:, t, (h % 4) * 128:(h % 4 + 1) * 128] for t in range(2))
                PE.mute(mm(b.ap[:, 0:128], v0, PT[:, 0:128], True, True))
                PE.mute(mm(b.ap[:, 128:256], v0, PT[:, 128:256], True, False))
                tt = PE.do(mm(b.ap[:, 128:256], v1, PT[:, 256:384], False, True))
                r = V.do(lambda e, b=b, h=h: e.tensor_tensor(SGM[:, h, :], b.ap[:, 0:256], SGM[:, h, :], ALU.mult), tt, sgt[h])
                b.free = [r]
                og[h] = (tt, r)
            if i % 4 == 1 and 1 <= i and i // 4 + 1 < 4:
                nxt = group(i // 4 + 1, [og[i - 2][0]] if i >= 4 else [])
                next(nxt)
            elif nxt is not None and i < 16:
                for _ in range(2):
                    next(nxt, None)
                if i % 4 == 3:
                    run(nxt)
                    nxt = None
        OS = (at(16 * KB, 16, 256, of=arena_r), at(32 * KB, 16, 256, of=arena_r))
        t_sp = split(flat(SGM), flat(OS[0]), flat(OS[1]), 4096, [og[15][1]])
        t_fg = G.dma(GBA, A["final_norm_g"].partition_broadcast(128), DSem("dfg"), og[15][1], rot[0])
        t_X = project_out(OS, 16, t_sp, GBB, t_gate, [t_X, *t_sp[-1]])

        ts = []
        for t in range(2):
            r = stat_of(X[:, t, :], D, 10 + t, at(YG + D * t, D), t_X)
            ts.append(V.do(lambda e, t=t: e.scalar_tensor_tensor(out=X[:, t, :], in0=X[:, t, :], scalar=st[:, 10 + t:11 + t],
                                                                 in1=GBA, op0=ALU.mult, op1=ALU.mult), r, t_fg))
        t_X = ts[1]

        t_ht = norm_T(t_X, colA[:, 48:64], None, [], 12)
        d2 = DSem("d2")
        DM, DC, DS = GBA[:, 0:384], GBA[:, 384:640], GBA[:, 640:896]
        t_d2 = G.dma(GBA[:, 0:896], A["table"][:, K_DM:K_END], d2, t_X)
        PE.wait(*t_ht)
        O = at(YG, 2, D)
        FV, DV = at(YG + 4096, 2, 1024), at(YG + 6144, 2, 1024)
        FQ, FK, DQ, DK = (at(W + i * 2048, 8, 256) for i in range(4))
        RAW2 = at(152 * KB, 512)
        RT2 = [at(152 * KB + 512 + 512 * i, 512) for i in range(2)]
        LF, LA, LM = (at(152 * KB + 1536 + 32 * i, 2, 16) for i in range(3))
        CTT, NCT = at(144 * KB + 896, 256), at(144 * KB + 1152, 256)

        b, f = bank()
        PE.wait(*f)
        hi, lo, j = take_w()
        for t in range(2):
            for kc in range(16):
                ts_ = slice(t * 128, (t + 1) * 128)
                tt = three(b.ap[:, t * 16:t * 16 + 16], (HT[0][:, kc, ts_], HT[1][:, kc, ts_]),
                           (hi[:, kc * 16:(kc + 1) * 16], lo[:, kc * 16:(kc + 1) * 16]), kc == 0, kc == 15)
        give_w(j, tt)
        r = V.do(lambda e, b=b: e.tensor_tensor(LF, b.ap[:, 0:32].rearrange("p (a b) -> p a b", a=2),
                                                fb.unsqueeze(1).broadcast_to([128, 2, 16]), ALU.add), tt, t_fb, t_X)
        b.free = [r]
        r2 = V.do(lambda e: e.scalar_tensor_tensor(out=LA, in0=LF, scalar=-1.0, in1=LF, op0=ALU.mult, op1=ALU.min), r)
        r3 = V.do(lambda e: e.tensor_scalar(LM, LF, 0.0, None, ALU.min), r)
        r2 = S.do(lambda e: e.activation(LA, LA, ACT.Exp), r2)
        r2 = S.do(lambda e: e.activation(LA, LA, ACT.Ln, bias=1.0), r2)
        t_lf = V.do(lambda e: e.tensor_tensor(LF, LM, LA, ALU.subtract), r2, r3)

        fq_done, dq_done = [], []

        def copy_T(dst, g, sc, done):
            def f(p, b, tt):
                c = 4 * g + 2 * p
                d = flat(dst[:, c:c + 2, :])
                done.append(S.do(lambda e: e.mul(d, b.ap, sc) if sc else e.copy(d, b.ap), tt, t_X, *t_ht))
                return [done[-1]]
            return f

        ro = [t_X]
        PDm = cst[:, K_PD:K_PD + 128]

        def dil_T(dst, g, sc):
            def f(p, b, tt):
                c = 4 * g + 2 * p
                ro[0] = rotate(b, 2, flat(dst[:, c:c + 2, :]), PDm, DC, DS, tt, RAW2, RT2, sc, [ro[0], t_d2])
                dq_done.append(ro[0])
                return [ro[0]]
            return f

        def copy_tok(dst, g, done):
            def f(t, b, tt):
                done.append(S.do(lambda e: e.copy(dst[:, t, g * 512:(g + 1) * 512], b.ap), tt, *t_ht))
                return [done[-1]]
            return f

        for g in range(2):
            run(g_proj_T(HT, copy_T(FQ, g, 0.125, fq_done)))
        for g in range(2):
            run(g_proj_T(HT, copy_T(FK, g, None, fq_done)))
        for g in range(2):
            run(g_proj_tok(HT, copy_tok(FV, g, fq_done)))

        b, f = bank()
        PE.wait(*f)
        PE.wait(t_lf)
        PE.mute(mm(b.ap[0:16, 0:128], LF[:, 0, :], TRI, True, True))
        PE.mute(mm(b.ap[0:16, 128:256], LF[:, 0, :], ONES, True, False))
        tt = PE.do(mm(b.ap[0:16, 128:256], LF[:, 1, :], TRI, False, True))
        r1 = V.do(lambda e, b=b: e.tensor_copy(CTT[0:16, :], b.ap[0:16, 0:256]), tt)
        r2 = V.do(lambda e, b=b: e.tensor_scalar(NCT[0:16, :], b.ap[0:16, 0:256], -1.0, None, ALU.mult), tt)
        b.free = [r2]
        PE.wait(r1, r2, *fq_done)

        def dil_work():
            for g in range(2):
                yield from g_proj_T(HT, dil_T(DQ, g, 0.125))
            for g in range(2):
                yield from g_proj_T(HT, dil_T(DK, g, None))
            for g in range(2):
                yield from g_proj_tok(HT, copy_tok(DV, g, dq_done))

        def heads(qT, kT, vt, col0, mask, fox, items, t_first):
            fl, sm_, pv = {}, {}, {}
            ob = None
            for i in range(16 + 2):
                if i < 16:
                    b, f = bank()
                    PE.wait(*f)
                    rb, c = 64 * (i % 2), i // 2
                    q, k = qT[rb:rb + 64, c, :], kT[rb:rb + 64, c, :]
                    one = IDN[0:16, i:i + 1]
                    for c0, q0, n in ((0, 0, 128), (128, 128, 256)):
                        o = b.ap[:, c0:c0 + n]
                        fn = mm(o, q[:, q0:q0 + 128], k[:, 0:n], True, not fox)
                        if fox:
                            PE.mute(fn)
                            PE.mute(mm(o, one.broadcast_to([16, 128]), NCT[0:16, 0:n], False, False))
                            fn = mm(o, CTT[0:16, q0:q0 + 128], one.broadcast_to([16, n]), False, True)
                        tt = PE.do(fn)
                    es, r = soft(i, b, tt, mask, 1.0, ([fl[i - 2][0]] if i > 1 else []) + t_first)
                    sm_[i] = (es, r)
                    next(items, None)
                if 0 <= i - 1 < 16:
                    fl[i - 1] = flip(i - 1, sm_[i - 1][0], [pv[i - 3][0]] if i >= 3 else [])
                if i < 16 and i % 2:
                    next(items, None)
                if i >= 2:
                    h = i - 2
                    b, f = bank()
                    PE.wait(*f)
                    PE.wait(fl[h][1])
                    PT = PTB[h % 2]
                    v0, v1 = vt[:, 0, h * 64:(h + 1) * 64], vt[:, 1, h * 64:(h + 1) * 64]
                    PE.mute(mm(b.ap[:, 0:64], PT[:, 0:128], v0, True, True))
                    PE.mute(mm(b.ap[:, 64:128], PT[:, 128:256], v0, True, False))
                    tt = PE.do(mm(b.ap[:, 64:128], PT[:, 256:384], v1, False, True))
                    for t in range(2):
                        r = V.do(lambda e, b=b, h=h, t=t: e.tensor_scalar(
                            O[:, t, col0 + h * 64:col0 + h * 64 + 64], b.ap[:, t * 64:t * 64 + 64],
                            rinv[:, h % 3, t:t + 1], None, ALU.mult), tt, sm_[h][1])
                    b.free = [r]
                    pv[h] = (tt, r)
            return pv[15][1]

        items = dil_work()
        t_o1 = heads(FQ, FK, FV, 0, CM, True, items, list(t_ht))
        run(items)
        PE.wait(*dq_done)
        t_o2 = heads(DQ, DK, DV, 1024, DM, False, iter(()), [t_d2])
        ns = []
        for t in range(2):
            for part, to in ((0, t_o1), (1, t_o2)):
                ap = O[:, t, part * 1024:(part + 1) * 1024]
                r = stat_of(ap, 1024, 16 + 2 * t + part, at(W + (2 * t + part) * 1024, 1024), to, t_o2)
                rr = V.do(lambda e, ap=ap, t=t, part=part: e.tensor_scalar(
                    ap, ap, st[:, 16 + 2 * t + part:17 + 2 * t + part], None, ALU.mult), r)
            ns.append(rr)
        t_ff = G.dma(GBB, A["ffn_norm_gain_2"][0].partition_broadcast(128), DSem("dff"), t_o2)
        t_mt = turn_over(O, 16, HT, colA[:, 88:104], None, ns, [t_o2], YG + 4096)
        t_X = project_out(HT, 16, [t_mt] * 4, None, None, t_mt)

        after = [t_X]
        HN = at(YG, 2, D)
        QT = at(YG + 4096, 16, 256)
        t_ht = norm_T(t_X, colA[:, 64:80], None, [], 20)
        t_hn = []
        for t in range(2):
            t_hn.append(V.do(lambda e, t=t: e.tensor_tensor(HN[:, t, :], HN[:, t, :], GBB, ALU.mult), *t_ht, t_ff))
        KT = at(W, 16, 128)
        SC, CA, EQ, JUNK = at(16 * KB, D), at(16 * KB + 2048, 8, 256), at(16 * KB + 4096, 128, 16), at(16 * KB + 6144, D)
        pz = [W + 2048]

        def pt(*shape):
            o = pz[0]
            pz[0] += int(np.prod(shape))
            return at(o, *shape)

        VAL, IDX, IDF = pt(16, 16), pt(16, 16), pt(16, 16)
        WK = pt(256)
        TV, TC = pt(8, 16), pt(128)
        II = [pt(128) for i in range(2)]
        IF = [pt(128) for i in range(2)]
        EF = [pt(128) for i in range(2)]
        EI = [pt(128) for _ in range(2)]
        GT = [pt(8, 16) for _ in range(2)]
        HD = [pt(128) for _ in range(2)]
        GS = pt(8)
        assert pz[0] <= 192 * KB, pz[0]

        ki = pos[0]
        pos[0] += 1
        assert plan[ki][0] == "raw"
        wk_ = raws[ki % 4][0]
        PE.wait(landed[ki], *t_ht)
        kt = []
        for g in range(4):
            b, f = bank()
            PE.wait(*f)
            for j in range(4):
                tt = PE.do(lambda e, b=b, g=g, j=j: e.transpose(
                    b.ap[:, j * 128:(j + 1) * 128], wk_[:, (4 * g + j) * 128:(4 * g + j + 1) * 128], IDN))
            r = V.do(lambda e, b=b, g=g: e.tensor_copy(KT[:, 4 * g:4 * g + 4, :].rearrange("p a b -> p (a b)"), b.ap), tt, t_o2, *t_mt)
            b.free = [r]
            kt.append(r)
        free_raw(ki, tt)
        for g in range(4):
            def ev(p, b, tt, g=g):
                c = 4 * g + 2 * p
                kt.append(S.do(lambda e: e.copy(flat(QT[:, c:c + 2, :]), b.ap), tt, *t_ht))
                return [kt[-1]]
            run(g_proj_T(HT, ev))
        t_ring = kt[-1]
        PE.wait(*kt)
        IOTA = cst[:, K_IOTA:K_IOTA + 16]
        t_sel = {}

        def top16(src, val, idx, wk, r):
            r = V.do(lambda e: e.max(val[:, 0:8], src), r)
            yield r
            r = V.do(lambda e: e.max_index(idx[:, 0:8], val[:, 0:8], src), r)
            yield r
            r = V.do(lambda e: e.match_replace(wk, val[:, 0:8], src, -3.0e38), r)
            yield r
            r = V.do(lambda e: e.max(val[:, 8:16], wk), r)
            yield r
            r = V.do(lambda e: e.max_index(idx[:, 8:16], val[:, 8:16], wk), r)
            yield r

        def select(t, r):
            sc = []
            for g in range(4):
                b, f = bank()
                PE.wait(*f)
                for j in range(4):
                    tt = PE.do(mm(b.ap[:, j * 128:(j + 1) * 128], QT[:, 4 * g + j, t * 128:(t + 1) * 128],
                                  KT[:, 4 * g + j, :], True, True))
                q = S.do(lambda e, b=b, g=g: e.copy(SC[:, g * 512:(g + 1) * 512], b.ap), tt, r, *kt)
                b.free = [q]
                sc.append(q)
            for hf in range(2):
                a, h4 = slice(8 * hf, 8 * hf + 8), slice(4 * hf, 4 * hf + 4)
                for hp in range(8 * hf, 8 * hf + 8):
                    for r in top16(SC[:, hp * 128:(hp + 1) * 128], VAL[:, hp, :], IDX[:, hp, :].bitcast(U32),
                                   WK[:, 0:128], [sc[hp // 4], r]):
                        yield
                V2 = VAL[:, a, :].rearrange("p (h a) k -> p h a k", a=2)
                I2 = IDF[:, a, :].rearrange("p (h a) k -> p h a k", a=2)
                r = V.do(lambda e, a=a: e.tensor_copy(IDF[:, a, :], IDX[:, a, :].bitcast(U32)), r)
                yield
                r = V.do(lambda e, h4=h4, V2=V2: e.tensor_tensor(
                    CA[:, h4, :].rearrange("p h (i j) -> p h i j", i=16),
                    V2[:, :, 0, :].unsqueeze(3).broadcast_to([128, 4, 16, 16]),
                    V2[:, :, 1, :].unsqueeze(2).broadcast_to([128, 4, 16, 16]), ALU.add), r)
                yield
                for h in range(4 * hf, 4 * hf + 4):
                    for r in top16(CA[:, h, :], TV[:, h, :], TC[:, h * 16:(h + 1) * 16].bitcast(U32), WK, r):
                        yield
                s6 = slice(64 * hf, 64 * hf + 64)
                ra = V.do(lambda e, s6=s6: e.tensor_scalar(II[0][:, s6].bitcast(U32), TC[:, s6].bitcast(U32), 4, None,
                                                           ALU.logical_shift_right), r)
                yield
                rb = V.do(lambda e, s6=s6: e.tensor_scalar(II[1][:, s6].bitcast(U32), TC[:, s6].bitcast(U32), 15, None,
                                                           ALU.bitwise_and), r)
                yield
                E3 = EQ[:, s6, :]
                E4 = E3.rearrange("p (h k) i -> p h k i", h=4)
                for p in range(2):
                    r = V.do(lambda e, p=p, s6=s6: e.tensor_copy(IF[p][:, s6], II[p][:, s6].bitcast(U32)), ra, rb)
                    yield
                    r = V.do(lambda e, p=p, s6=s6, E3=E3: e.tensor_tensor(
                        E3, IF[p][:, s6].unsqueeze(2).broadcast_to([128, 64, 16]),
                        IOTA.unsqueeze(1).broadcast_to([128, 64, 16]), ALU.is_equal), r)
                    yield
                    r = V.do(lambda e, p=p, E4=E4, I2=I2: e.tensor_tensor(
                        E4, E4, I2[:, :, p, :].unsqueeze(2).broadcast_to([128, 4, 16, 16]), ALU.mult), r)
                    yield
                    r = V.do(lambda e, p=p, s6=s6, E3=E3: e.tensor_reduce(EF[p][:, s6], E3, AX.X, ALU.add), r)
                    yield
                r = V.do(lambda e, s6=s6: e.scalar_tensor_tensor(out=EI[t][:, s6].bitcast(U32), in0=EF[0][:, s6], scalar=128.0,
                                                                 in1=EF[1][:, s6], op0=ALU.mult, op1=ALU.add), r)
                t_sel[(t, hf)] = r
                yield
            r = V.do(lambda e: e.tensor_tensor(GT[t], TV, TV[:, :, 0:1].broadcast_to([128, 8, 16]), ALU.subtract), r)
            yield
            r = S.do(lambda e: e.activation(GT[t], GT[t], ACT.Exp), r)
            yield
            r = V.do(lambda e: e.tensor_reduce(GS, GT[t], AX.X, ALU.add), r)
            yield
            r = V.do(lambda e: e.reciprocal(GS, GS), r)
            yield
            t_gt[t] = V.do(lambda e: e.tensor_tensor(GT[t], GT[t], GS.unsqueeze(2).broadcast_to([128, 8, 16]), ALU.mult), r)
            yield

        t_gt = {}

        def selects():
            yield from select(0, None)
            yield from select(1, t_gt[0])

        sel = selects()
        while (0, 0) not in t_sel:
            next(sel)
        gsem = [DSem(f"g{i}") for i in range(NG)]
        gbuf = [at(RAWS + i * 2048, D) for i in range(NG)]
        last = [t_ring] * NG
        cnt = [0]
        t_f2 = G.dma(GBB, A["final_norm_gain_2"].partition_broadcast(128), DSem("df2"), *t_hn)

        def gather(tab, t, j):
            i = cnt[0] % NG
            cnt[0] += 1
            ds = gsem[i]
            G.wait(t_sel[(t, j // 64)], last[i], t_ring)
            G.q.append(lambda e: e.indirect_dma_start(
                out=gbuf[i], out_offset=None, in_=tab,
                in_offset=bass.IndirectOffsetOnAxis(ap=EI[t][:, j:j + 1].bitcast(U32), axis=0)).then_inc(ds.sem, 16))
            ds.n += 16
            return i, (ds.sem, ds.n)

        down, up = A["peer_down_2"][0], A["peer_up_2"][0]
        todo = [(down, t, j) for t in range(2) for j in range(128)] + [(up, t, j) for t in range(2) for j in range(128)]
        co = [None, None]
        rprev = None
        for n, (tab, t, j) in enumerate(todo):
            if n:
                next(sel, None)
                next(sel, None)
            i, tg = gather(tab, t, j)
            if tab is down:
                rprev = V.do(lambda e, i=i, t=t, j=j: e.tensor_tensor_reduce(
                    JUNK, gbuf[i], HN[:, t, :], 1.0, 0.0, ALU.mult, ALU.add, HD[t][:, j:j + 1]), tg, rprev)
                if j == 127:
                    r = S.do(lambda e, t=t: e.activation(HD[t], HD[t], ACT.Gelu_apprx_tanh), rprev)
                    co[t] = (r, t)
            else:
                if j == 0:
                    rprev = V.do(lambda e, t=t: e.tensor_tensor(HD[t], HD[t], GT[t].rearrange("p a b -> p (a b)"), ALU.mult),
                                 co[t][0], rprev, t_gt[t])
                rprev = V.do(lambda e, i=i, t=t, j=j: e.scalar_tensor_tensor(
                    out=X[:, t, :], in0=gbuf[i], scalar=HD[t][:, j:j + 1], in1=X[:, t, :], op0=ALU.mult, op1=ALU.add),
                    tg, rprev)
                if j == 127:
                    r = stat_of(X[:, t, :], D, 24 + t, SC, rprev)
                    r = V.do(lambda e, t=t: e.scalar_tensor_tensor(out=X[:, t, :], in0=X[:, t, :], scalar=st[:, 24 + t:25 + t],
                                                                   in1=GBB, op0=ALU.mult, op1=ALU.mult), r, t_f2)
                    if t == 0:
                        dout = DSem("dout")
                    t_out = SP.dma(out[0][t * 128:(t + 1) * 128, :], X[:, t, :], dout, r)
                    rprev = r
            last[i] = rprev
        SP.wait(t_out)
        assert pos[0] == len(plan) == sent[0], (pos, len(plan), sent)

        block = ctx.enter_context(nc.Block())
        block.sync(SP.run)
        block.gpsimd(G.run)
        block.scalar(S.run)
        block.vector(V.run)
        block.tensor(PE.run)


_INS = ["x", "c", "positions", "ada_w", "ada_b", "norm_g", "ret_w_in", "ret_gn_g", "ret_w_out", "mla_w_in",
        "mla_q_norm_g", "mla_w_uq", "mla_kv_norm_g", "mla_w_ukv", "mla_w_out", "final_norm_g", "attn_norm_gain_2",
        "w_in_2", "forget_bias_2", "fox_out_gain_2", "dil_out_gain_2", "w_out_2", "ffn_norm_gain_2",
        "peer_query_2", "peer_sub_keys_2", "peer_down_2", "peer_up_2", "final_norm_gain_2"]


def kernel(**inputs):
    import concourse.bacc as _bacc
    from concourse.bass_utils import run_bass_kernel_spmd as _run

    nc = _bacc.Bacc("TRN2", target_bir_lowering=False, num_devices=1)
    arrays, A = {}, {}
    table, decay = tables()
    every = {n: np.ascontiguousarray(inputs[n]) for n in _INS}
    every["table"], every["decay"] = table, decay
    for name, a in every.items():
        arrays[f"in_{name}"] = a
        A[name] = nc.dram_tensor(f"in_{name}", a.shape, mybir.dt.from_np(a.dtype), kind="ExternalInput").ap()
    out = nc.dram_tensor("out_0", (1, 256, D), F, kind="ExternalOutput").ap()
    build(nc, A, out)
    r = _run(nc, [arrays], core_ids=[0])
    return r.results[0]["out_0"]
```

```python
from contextlib import ExitStack

import numpy as np
import concourse.bass as bass
from concourse import mybir
from concourse.alu_op_type import AluOpType as ALU

F = mybir.dt.float32
FR = mybir.dt.float32r
I32 = mybir.dt.int32
U32 = mybir.dt.uint32
ACT = mybir.ActivationFunctionType
AX = mybir.AxisListType

D = 2048
R = 4
NB = 8
NG = 8
EPS = 1e-6
TWO_PI_INV = 0.15915494309189535
C1 = 6.28125
C2 = 0.0019350051879882812
C3 = 3.0199157663e-07
MAGIC = 12582912.0
PI_IN = 3.1415925

K_ID, K_ONE, K_PM, K_PD, K_TRI = 0, 128, 256, 384, 512
K_CM, K_INV, K_IOTA = 640, 1024, 1026
K_DM, K_DC, K_DS = 1042, 1426, 1682
K_END = 1938


def tables():
    t = np.zeros((128, K_END), np.float32)
    p = np.arange(128)
    t[:, K_ID:K_ID + 128] = np.eye(128)
    t[:, K_ONE:K_ONE + 128] = 1.0
    pm = np.zeros((128, 128), np.float32)
    pd = np.zeros((128, 128), np.float32)
    for b in (0, 64):
        for i in range(32):
            pm[b + 32 + i, b + i] = -1.0
            pm[b + i, b + 32 + i] = 1.0
        for i in range(8):
            pd[b + 8 + i, b + i] = -1.0
            pd[b + i, b + 8 + i] = 1.0
    t[:, K_PM:K_PM + 128] = pm
    t[:, K_PD:K_PD + 128] = pd
    t[:, K_TRI:K_TRI + 128] = p[:, None] <= p[None, :]

    def both(mask, add):
        full = np.where(mask, add, np.float32(-1e30)).astype(np.float32)
        return np.concatenate([full[0:128, 0:128], full[128:256, :]], axis=1)

    q = np.arange(256)[:, None]
    k = np.arange(256)[None, :]
    t[:, K_CM:K_CM + 384] = both(k <= q, np.zeros((256, 256), np.float32))
    count = ((q - k <= 128) & (k <= q)).astype(int) + ((k <= q) & ((q - k) % 4 == 0)) + ((k <= q) & ((q - k) % 16 == 0))
    t[:, K_DM:K_DM + 384] = both(count > 0, np.log(np.maximum(count, 1)).astype(np.float32))
    inv = (500000.0 ** (-np.arange(0, 16, 2) / 16)).astype(np.float32)
    ang = np.arange(256, dtype=np.float32)[None, :] * inv[:, None]
    for b in (0, 8, 64, 72):
        t[b:b + 8, K_DC:K_DC + 256] = np.cos(ang.astype(np.float64))
        t[b:b + 8, K_DS:K_DS + 256] = np.sin(ang.astype(np.float64))
    for b in (16, 80):
        t[b:b + 48, K_DC:K_DC + 256] = 1.0
    t[:, K_INV] = (10000.0 ** (-np.arange(0, 256, 2) / 256)).astype(np.float32)
    t[:, K_INV + 1] = (10000.0 ** (-np.arange(0, 64, 2) / 64)).astype(np.float32)[p % 32]
    t[:, K_IOTA:K_IOTA + 16] = np.arange(16)
    g = np.log1p(-np.exp2(-5.0 - np.arange(8)))
    n = np.arange(256)[None, :] - p[:, None]
    dec = np.stack([np.where(n >= 0, np.exp(a * np.maximum(n, 0)), 0.0) for a in g], axis=1) / 16.0
    return t, dec.astype(np.float32).reshape(128, 2048)


class Bank:
    def __init__(self, ap):
        self.ap = ap
        self.free = []


def build(nc, A, out):
    ctx = ExitStack()
    with ctx:
        def sem(name):
            return ctx.enter_context(nc.semaphore(name))

        class Eng:

            def __init__(self, name):
                self.name, self.q, self.n, self.seen = name, [], 0, {}
                self.sem = sem("s_" + name)

            def wait(self, *toks):
                for t in toks:
                    if t is None:
                        continue
                    if isinstance(t, list):
                        self.wait(*t)
                        continue
                    s, v = t
                    if self.seen.get(id(s), 0) < v:
                        self.seen[id(s)] = v
                        self.q.append(lambda e, s=s, v=v: e.wait_ge(s, v))

            def do(self, fn, *toks):
                self.wait(*toks)
                self.n += 1
                self.q.append(lambda e: fn(e).then_inc(self.sem, 1))
                return (self.sem, self.n)

            def mute(self, fn, *toks):
                self.wait(*toks)
                self.q.append(fn)

            def dma(self, dst, src, s, *toks, **kw):
                self.wait(*toks)
                self.q.append(lambda e: e.dma_start(dst, src, **kw).then_inc(s.sem, 16))
                s.n += 16
                return (s.sem, s.n)

            def run(self, e):
                for fn in self.q:
                    fn(e)

        class DSem:
            def __init__(self, name):
                self.sem, self.n = sem(name), 0

        PE, V, S, G, SP = (Eng(n) for n in ("pe", "dve", "act", "pool", "sp"))

        base = (nc.sbuf_base + 63) // 64 * 64
        bounds = [0, 16, 48, 80, 112, 144, 160, 192, 207]
        arena, arena_r = {}, {}
        for a, z in zip(bounds, bounds[1:]):
            n = (z - a) * 256
            arena[a * 256, z * 256] = nc.alloc_sbuf_tensor_at(f"s{a}", [128, n], F, offset=base + a * 1024)
            if a in (16, 80, 112, 160):
                arena_r[a * 256, z * 256] = nc.alloc_sbuf_tensor_at(f"r{a}", [128, n], FR, offset=base + a * 1024)
        ps = ctx.enter_context(nc.psum_tensor("ps", [128, NB, 512], F))

        def at(off, *shape, of=arena):
            n = int(np.prod(shape))
            (lo, _), seg = next((k, v) for k, v in of.items() if k[0] <= off and off + n <= k[1])
            a = seg[:, off - lo:off - lo + n]
            if len(shape) == 2:
                a = a.rearrange("p (a b) -> p a b", a=shape[0])
            if len(shape) == 3:
                a = a.rearrange("p (a b c) -> p a b c", a=shape[0], b=shape[1])
            return a

        KB = 256
        X = at(0, 2, D)
        HT = (at(16 * KB, 16, 256, of=arena_r), at(32 * KB, 16, 256, of=arena_r))
        RAWS = 48 * KB
        HLS = 80 * KB
        YG = 112 * KB
        GBA = at(144 * KB, D)
        GBB = at(152 * KB, D)
        W = 160 * KB
        small = [192 * KB]

        def sm(*shape):
            off = small[0]
            small[0] += int(np.prod(shape))
            return at(off, *shape)

        cst = sm(K_DM)
        IDN = cst[:, K_ID:K_ID + 128]
        ONES = cst[:, K_ONE:K_ONE + 128]
        TRI = cst[:, K_TRI:K_TRI + 128]
        cosM, sinM = sm(256), sm(256)
        KR = sm(256)
        LBO = small[0]
        LB = [sm(384) for _ in range(2)]
        PTB = [sm(384) for _ in range(2)]
        colA, colB = sm(104), sm(128)
        cact, mod, gs = sm(16), sm(96), sm(16)
        st = sm(64)
        mn, sums, rinv = sm(2, 2), sm(2, 2), sm(3, 2)
        bst = sm(2, 6)
        mv = sm(2, 2)
        fb = sm(16)
        epsc = sm(1)
        SQ = sm(2, 4)
        assert small[0] <= 52992, small[0]

        banks = [Bank(ps[:, i, :]) for i in range(NB)]
        turn = [0]

        def bank():
            n = 0
            while banks[turn[0] % NB].free is None:
                turn[0] += 1
                n += 1
                assert n < NB
            b = banks[turn[0] % NB]
            turn[0] += 1
            f, b.free = b.free, None
            return b, f

        plan = []
        raws = [(at(RAWS + i * 1024, 1024), DSem(f"w{i}")) for i in range(8)]
        parts = [(at(HLS + i * 2048, 1024, of=arena_r), at(HLS + i * 2048 + 1024, 1024, of=arena_r)) for i in range(4)]
        landed, raw_free, sent, limit = {}, {}, [0], [0]
        pos, conv, hl_free, hl_turn, split_of = [0], [0], [[], [], [], []], [0], {}

        def send():
            while sent[0] < len(plan) and (sent[0] < 8 or sent[0] - 8 in raw_free):
                i = sent[0]
                ap, ds = raws[i % 8]
                for dst, src in plan[i][2](ap):
                    t = SP.dma(dst, src, ds, *(raw_free[i - 8] if i >= 8 else []))
                landed[i] = t
                sent[0] += 1

        def free_raw(i, *toks):
            raw_free[i] = list(toks)
            send()

        def split_next():
            while conv[0] < limit[0] and plan[conv[0]][0] != "w" and conv[0] in landed:
                if plan[conv[0]][0] == "ada":
                    ada_unit(conv[0], *plan[conv[0]][3])
                conv[0] += 1
            i = conv[0]
            j = hl_turn[0] % 4
            if i >= limit[0] or i not in landed or hl_free[j] is None:
                return False
            n = plan[i][1]
            raw = raws[i % 8][0][:, 0:n]
            hi, lo = parts[j][0][:, 0:n], parts[j][1][:, 0:n]
            r = S.do(lambda e: e.copy(hi, raw), landed[i], *hl_free[j])
            q = V.do(lambda e: e.tensor_tensor(lo, raw, hi.bitcast(F), ALU.subtract), r)
            hl_free[j] = None
            hl_turn[0] += 1
            split_of[i] = (hi, lo, [r, q], j)
            conv[0] += 1
            free_raw(i, q)
            return True

        def take_w():
            while plan[pos[0]][0] == "ada":
                pos[0] += 1
            i = pos[0]
            assert plan[i][0] == "w"
            while i not in split_of:
                assert split_next()
            hi, lo, toks, j = split_of[i]
            pos[0] += 1
            PE.wait(*toks)
            return hi, lo, j

        late = []

        def flush():
            while late:
                late.pop(0)()

        def give_w(j, tok):
            flush()
            hl_free[j] = [tok]
            while split_next():
                pass
            given[0] += 1
            ada_sum(False)

        def rows(src, k0, nk, c, n):
            return src[k0:k0 + nk * 128, c:c + n].rearrange("(k p) n -> p k n", p=128)

        def unit(src, k0, c, n=512, nk=2):
            return lambda ap: [(ap[:, 0:nk * n].rearrange("p (k n) -> p k n", k=nk), rows(src, k0, nk, c, n))]

        ticks = []

        def addw(fns, n=1024):
            for fn in fns:
                plan.append(("w", n, fn, None))
                if ticks and sum(p[0] == "w" for p in plan) % 9 in (1, 3, 5, 7, 8):
                    plan.append(ticks.pop(0))

        def ada_entry(layer, g, u):
            return ("ada", 1024, unit(A["ada_w"][layer], u * 256, g * 512), (layer, g, u))

        def cols512(src, c, nu=8):
            for u in range(nu):
                addw([unit(src, u * 256, c)])

        ret_in, ret_out = A["ret_w_in"][0], A["ret_w_out"][0]
        mla_in, mla_out = A["mla_w_in"][0], A["mla_w_out"][0]
        uq, ukv = A["mla_w_uq"][0], A["mla_w_ukv"][0]
        w2, wo2, pq = A["w_in_2"][0], A["w_out_2"][0], A["peer_query_2"][0]

        def qk_unit(h, u):
            def f(ap):
                v = ap.rearrange("p (k n) -> p k n", k=2)
                return [(v[:, :, 0:256], rows(ret_in, u * 256, 2, h * 256, 256)),
                        (v[:, :, 256:512], rows(ret_in, u * 256, 2, 2048 + h * 256, 256))]
            return f

        def head_units(src, c, hw, o, n):
            def part(a):
                def f(ap):
                    v = ap[:, 0:8 * n].rearrange("p (k h n) -> p k h n", k=2, h=4)
                    return [(v[:, k], src[(2 * a + k) * 128:(2 * a + k + 1) * 128, c:c + 4 * hw].rearrange(
                        "p (h n) -> p h n", h=4)[:, :, o:o + n]) for k in range(2)]
                return f
            return [part(0), part(1)]

        def kr_unit(a):
            def f(ap):
                v = ap.rearrange("p (k n) -> p k n", k=8)
                return [(v[:, :, j * 64:(j + 1) * 64], rows(mla_in, a * 1024, 8, 1024, 64)) for j in range(2)]
            return f

        marks = []
        for q in range(5):
            ada = [ada_entry(0, g, u) for g in (q, 4 + q) for u in range(8)] if q < 4 else []
            if q == 0:
                plan += ada
            else:
                us = (2 * q - 2, 2 * q - 1)
                ws = [qk_unit(0, u) for u in us] + [unit(ret_in, u * 256, c) for c in (4096, 8192) for u in us]
                at_ = []
                for i, w in enumerate(ws):
                    plan += ada[0:3 if i == 0 else 2]
                    ada = ada[3 if i == 0 else 2:]
                    at_.append(len(plan))
                    plan.append(("w", 1024, w, None))
                plan += ada
                marks.append([at_[2] + 1, at_[4] + 1, len(plan)])
        for n in range(16):
            for u in range(8):
                ticks.append(ada_entry(0, 8 + n, u) if n < 4 else ada_entry(1, n - 4, u))
        for h in range(1, 8):
            addw([qk_unit(h, u) for u in range(8)])
            cols512(ret_in, 4096 + h * 512)
            cols512(ret_in, 8192 + h * 512)
        for n in range(4):
            cols512(ret_out, n * 512, 16)
        assert not ticks
        cols512(mla_in, 0)
        cols512(mla_in, 512)
        cols512(mla_in, 1088)
        addw([kr_unit(0), kr_unit(1)])
        for g in range(1, 4):
            cols512(mla_in, 1088 + g * 512)
        for g in range(4):
            addw(head_units(uq, g * 768, 192, 0, 128))
            addw(head_units(uq, g * 768, 192, 128, 64), 512)
            addw(head_units(ukv, g * 1024, 256, 0, 128))
            addw(head_units(ukv, g * 1024, 256, 128, 128))
        for n in range(4):
            cols512(mla_out, n * 512)
        addw([unit(w2, a * 1024, 3072, 16, 8) for a in range(2)], 128)
        for g in range(6):
            cols512(w2, g * 512)
        for g in range(6):
            cols512(w2, 3088 + g * 512)
        for n in range(4):
            cols512(wo2, n * 512)
        keys = A["peer_sub_keys_2"][0].rearrange("h a n c -> n (h a) c")
        for a in range(2):
            plan.append(("raw", 1024, lambda ap, a=a: [(ap.rearrange("p (h n) -> p h n", h=8),
                                                        keys[:, 8 * a:8 * a + 8, :])], None))
        for g in range(4):
            cols512(pq, g * 512)

        dc, dx, dr, dp, dg, dfb = (DSem(n) for n in ("dc", "dx", "dr", "dp", "dg", "dfb"))
        ROWA, ROWB = at(YG, 128), at(YG + 128, 128)
        PI, PF = at(W + 2560, 256), at(W + 2816, 256)
        t_c = SP.dma(cst, A["table"][:, 0:K_DM], dc)
        r0 = 0
        for name, n in (("c", 16), ("norm_g", 32), ("attn_norm_gain_2", 16), ("ffn_norm_gain_2", 16),
                        ("mla_q_norm_g", 4), ("mla_kv_norm_g", 4), ("fox_out_gain_2", 8), ("dil_out_gain_2", 8)):
            t_r = SP.dma(ROWA[r0:r0 + n, :], A[name].rearrange("a (n p) -> (a n) p", p=128), dr)
            r0 += n
        t_r = SP.dma(ROWB[0:96, :], A["ada_b"].rearrange("a (n p) -> (a n) p", p=128), dr)
        t_r = SP.dma(ROWB[96:128, :], A["ret_gn_g"].rearrange("a (n p) -> (a n) p", p=128), dr)
        send()
        t_x = G.dma(X, A["x"][0].rearrange("(t p) d -> p t d", p=128), dx)
        t_p = G.dma(PI.bitcast(I32), A["positions"][0].partition_broadcast(128), dp)
        DTAB = at(W, 8, 256)
        cosR, sinR = at(W + 2048, 256), at(W + 2304, 256)
        t_d = G.dma(DTAB.rearrange("p a b -> p (a b)"), A["decay"], dg)
        t_fb = G.dma(fb, A["forget_bias_2"][0].partition_broadcast(128), dfb)

        t_eps = V.do(lambda e: e.memset(epsc, EPS))

        def mm(o, l, r, start, stop):
            return lambda e: e.matmul(o, l, r, start=start, stop=stop)

        b, f = bank()
        PE.wait(t_c, t_r)
        PE.do(lambda e, b=b: e.transpose(b.ap[:, 0:104], ROWA[0:104, :], IDN[0:104, 0:104]), *f)
        t = PE.do(lambda e, b=b: e.transpose(b.ap[:, 128:256], ROWB, IDN))
        t_ca = V.do(lambda e, b=b: e.tensor_copy(colA, b.ap[:, 0:104]), t)
        t_cb = V.do(lambda e, b=b: e.tensor_copy(colB, b.ap[:, 128:256]), t)
        b.free = [t_cb]
        t_cact = S.do(lambda e: e.activation(cact, colA[:, 0:16], ACT.Silu), t_ca)

        t_trig = []

        def trig():
            t = V.do(lambda e: e.tensor_copy(PF, PI.bitcast(I32)), t_p)
            AN, KK, RR = (at(W + 3072 + 256 * i, 256) for i in range(3))
            RQ = [at(W + 3840 + 256 * i, 256) for i in range(4)]
            k = 0
            for j, (co, si) in enumerate(((cosR, sinR), (cosM, sinM))):
                t = V.do(lambda e, j=j: e.tensor_scalar(AN, PF, cst[:, K_INV + j:K_INV + j + 1], None, ALU.mult), t, t_c)
                yield
                for dst, sh in ((co, 0.25), (si, 0.0)):
                    q = RQ[k]
                    k += 1
                    t = V.do(lambda e, sh=sh: e.tensor_scalar(KK, AN, TWO_PI_INV, sh, ALU.mult, ALU.add), t)
                    yield
                    t = V.do(lambda e: e.tensor_scalar(KK, KK, MAGIC, None, ALU.add), t)
                    yield
                    t = V.do(lambda e: e.tensor_scalar(KK, KK, MAGIC, None, ALU.subtract), t)
                    yield
                    t = V.do(lambda e: e.scalar_tensor_tensor(out=RR, in0=KK, scalar=-C1, in1=AN, op0=ALU.mult, op1=ALU.add), t)
                    yield
                    t = V.do(lambda e: e.scalar_tensor_tensor(out=RR, in0=KK, scalar=-C2, in1=RR, op0=ALU.mult, op1=ALU.add), t)
                    yield
                    t = V.do(lambda e: e.scalar_tensor_tensor(out=RR, in0=KK, scalar=-C3, in1=RR, op0=ALU.mult, op1=ALU.add), t)
                    yield
                    if sh:
                        t = V.do(lambda e: e.tensor_scalar(RR, RR, 1.5707963267948966, None, ALU.add), t)
                        yield
                    t = V.do(lambda e, q=q: e.tensor_scalar(q, RR, PI_IN, -PI_IN, ALU.min, ALU.max), t)
                    yield
                    t_trig.append(S.do(lambda e, q=q, dst=dst: e.activation(dst, q, ACT.Sin), t))
                    yield

        acc_free, fin = [None, None], []
        t_mods = {}

        def turn_of(layer, g):
            return g // 4 if layer == 0 and g < 8 else g % 2

        def ada_unit(i, layer, g, u):
            j = turn_of(layer, g)
            first = layer == 0 and g < 8
            acc = [GBB[:, j * 512 + h * 1024:(j + 1) * 512 + h * 1024] for h in range(2)] + [GBA[:, j * 512:(j + 1) * 512]]
            ada_finish()
            if u == 0:
                if len(whole) > 1:
                    ada_sum(True)
                fin_prev[j] = [acc_free[j]] * 3
                used[j] = set()
            rs = fin_prev[j]
            for kc in range(2):
                k = u * 2 + kc
                w = raws[i % 8][0][:, kc * 512:(kc + 1) * 512]
                if first and k % 4 == 3:
                    o = acc[2] if k == 3 else GBA[:, 1024:1536]
                    r = G.do(lambda e, w=w, k=k, o=o: e.tensor_scalar(o, w, cact[:, k:k + 1], None, ALU.mult),
                             rs[2], landed[i], t_cact)
                    if k > 3:
                        r = G.do(lambda e, o=o: e.tensor_tensor(acc[2], acc[2], o, ALU.add), r)
                    rs[2] = r
                    continue
                h = k % 2
                if h not in used[j]:
                    used[j].add(h)
                    rs[h] = V.do(lambda e, w=w, k=k, h=h: e.tensor_scalar(acc[h], w, cact[:, k:k + 1], None, ALU.mult),
                                 rs[h], landed[i], t_cact)
                else:
                    rs[h] = V.do(lambda e, w=w, k=k, h=h: e.scalar_tensor_tensor(
                        out=acc[h], in0=w, scalar=cact[:, k:k + 1], in1=acc[h], op0=ALU.mult, op1=ALU.add), rs[h], landed[i])
            free_raw(i, *rs)
            if u == 7:
                whole.append((given[0], layer, g, acc, rs))

        def ada_sum(now):
            if whole and (now or given[0] >= whole[0][0] + 3):
                _, layer, g, acc, rs = whole.pop(0)
                j = turn_of(layer, g)
                b, f = bank()
                PE.wait(*f)
                PE.wait(*rs)
                for m in range(4):
                    ms_ = slice(m * 128, (m + 1) * 128)
                    PE.mute(mm(b.ap[:, m:m + 1], acc[0][:, ms_], ONES[:, 0:1], True, False))
                    if layer == 0 and g < 8:
                        PE.mute(mm(b.ap[:, m:m + 1], acc[2][:, ms_], ONES[:, 0:1], False, False))
                    t = PE.do(mm(b.ap[:, m:m + 1], acc[1][:, ms_], ONES[:, 0:1], False, True))
                acc_free[j] = t
                fin.append((layer, g, b, t))

        used, whole, given = {}, [], [0]
        fin_prev = [None, None]

        def ada_finish():
            while fin:
                layer, g, b, t = fin.pop(0)
                c = layer * 48 + g * 4
                r = V.do(lambda e, b=b, c=c: e.tensor_tensor(mod[:, c:c + 4], b.ap[:, 0:4], colB[:, c:c + 4], ALU.add), t, t_cb)
                b.free = [r]
                t_mods[(layer, g)] = r

        def gate_rows(layer, dst, DG, toks, *after):
            t = None
            for g in range(4):
                ts = []
                for j in range(4):
                    c = layer * 48 + 32 + 4 * g + j
                    ts.append(V.do(lambda e, j=j, c=c: e.tensor_scalar(DG[:, j, :], IDN, mod[:, c:c + 1], None, ALU.mult),
                                   t_mods[(layer, 8 + g)], t, *after))
                yield
                b, f = bank()
                PE.wait(*f)
                t = PE.do(mm(b.ap, ONES, DG.rearrange("p a b -> p (a b)"), True, True), *ts)
                r = S.do(lambda e, b=b, g=g: e.copy(dst[:, g * 512:(g + 1) * 512], b.ap), t, *after)
                b.free = [r]
            toks.append(r)

        def stat_of(src, n, col, junk, *after):
            t = S.do(lambda e: e.activation(junk, src, ACT.Square, scale=float(n) ** -0.5, accum_out=st[:, col:col + 1]), *after)
            t = S.do(lambda e: e.activation(st[:, col:col + 1], st[:, col:col + 1], ACT.Sqrt, bias=epsc), t, t_eps)
            return V.do(lambda e: e.reciprocal(st[:, col:col + 1], st[:, col:col + 1]), t)

        def turn_over(src, ks, dst, scale, bias, waits, after, tmp):
            res = {}
            used = [list(after), list(after)]
            for p in range(ks[0] // 2, ks[1] // 2):
                b, f = bank()
                PE.wait(*f)
                for t in range(2):
                    for j in range(2):
                        k = 2 * p + j
                        tt = PE.do(lambda e, b=b, j=j, t=t, k=k: e.transpose(
                            b.ap[:, j * 256 + t * 128:j * 256 + t * 128 + 128],
                            src[:, t, k * 128:(k + 1) * 128], IDN), waits(t, k))
                rs = []
                T = at(tmp + 512 * (p % 2), 512)
                for j in range(2):
                    k = 2 * p + j
                    o, i_ = T[:, j * 256:(j + 1) * 256], b.ap[:, j * 256:j * 256 + 256]
                    sc = scale[:, k:k + 1]
                    if p % 2 == 0:
                        if bias is None:
                            fn = lambda e, o=o, i_=i_, sc=sc: e.tensor_scalar(o, i_, sc, None, ALU.mult)
                        else:
                            fn = lambda e, o=o, i_=i_, sc=sc, bi=bias[:, k:k + 1]: e.tensor_scalar(
                                o, i_, sc, bi, ALU.mult, ALU.add)
                        rs.append(V.do(fn, tt, *used[0]))
                    else:
                        if bias is None:
                            fn = lambda e, o=o, i_=i_, sc=sc: e.activation(o, i_, ACT.Copy, scale=sc)
                        else:
                            fn = lambda e, o=o, i_=i_, sc=sc, bi=bias[:, k:k + 1]: e.activation(
                                o, i_, ACT.Identity, scale=sc, bias=bi)
                        rs.append(S.do(fn, tt, *used[1]))
                b.free = rs
                h, lo = (x[:, 2 * p:2 * p + 2, :].rearrange("p a b -> p (a b)") for x in dst)
                r = S.do(lambda e, h=h, T=T: e.copy(h, T), *rs, *after)
                q = V.do(lambda e, h=h, lo=lo, T=T: e.tensor_tensor(lo, T, h.bitcast(F), ALU.subtract), r, *rs)
                used[p % 2] = [q]
                res[2 * p] = res[2 * p + 1] = [r, q]
            return res

        def split(src, hi, lo, n, after):
            res = {}
            for i in range(0, n, 1024):
                r = S.do(lambda e, i=i: e.copy(hi[:, i:i + 1024], src[:, i:i + 1024]), *after)
                q = V.do(lambda e, i=i: e.tensor_tensor(lo[:, i:i + 1024], src[:, i:i + 1024],
                                                        hi[:, i:i + 1024].bitcast(F), ALU.subtract), r, *after)
                for k in range(4):
                    res[i // 256 + k] = [r, q]
            return res

        def norm(t_X, after, stat0=0, sums4=None):
            XN = at(YG, 2, D)
            rs = []
            for t in range(2):
                c = stat0 + t
                if sums4:
                    r = V.do(lambda e, t=t, c=c: e.tensor_reduce(st[:, c:c + 1], SQ[:, t, :], AX.X, ALU.add), *sums4)
                elif t == 0:
                    r = S.do(lambda e, t=t, c=c: e.activation(XN[:, t, :], X[:, t, :], ACT.Square, scale=float(D) ** -0.5,
                                                              accum_out=st[:, c:c + 1]), t_X, *after)
                else:
                    r = V.do(lambda e, t=t, c=c: e.tensor_tensor_reduce(XN[:, t, :], X[:, t, :], X[:, t, :], 1.0 / D, 0.0,
                                                                        ALU.mult, ALU.add, st[:, c:c + 1]), t_X, *after)
                rs.append(r)
            r = S.do(lambda e: e.activation(st[:, stat0:stat0 + 2], st[:, stat0:stat0 + 2], ACT.Sqrt, bias=epsc), *rs, t_eps)
            r = V.do(lambda e: e.reciprocal(st[:, stat0:stat0 + 2], st[:, stat0:stat0 + 2]), r)
            ws = {}
            for n in range(4):
                for t in range(2):
                    sl = slice(n * 512, (n + 1) * 512)
                    if t == 0:
                        ws[t, n] = V.do(lambda e, t=t, sl=sl: e.tensor_scalar(
                            XN[:, t, sl], X[:, t, sl], st[:, stat0 + t:stat0 + t + 1], None, ALU.mult), r, t_X)
                    else:
                        ws[t, n] = S.do(lambda e, t=t, sl=sl: e.activation(
                            XN[:, t, sl], X[:, t, sl], ACT.Copy, scale=st[:, stat0 + t:stat0 + t + 1]), r, t_X)
            return XN, lambda t, k: ws[t, k // 4]

        def norm_T(t_X, scale, bias, after, stat0=0, sums4=None):
            XN, ws = norm(t_X, after, stat0, sums4)
            return turn_over(XN, (0, 16), HT, scale, bias, ws, after, YG + 4096)

        def mod_scale(layer, t_mod, *after):
            c = layer * 48 + 16
            return V.do(lambda e: e.scalar_tensor_tensor(out=gs, in0=mod[:, c:c + 16], scalar=1.0,
                                                         in1=colA[:, 16 + 16 * layer:32 + 16 * layer],
                                                         op0=ALU.add, op1=ALU.mult), t_mod, t_ca, *after)

        t_ht = {}
        HX = (*HT, t_ht)

        def advance(i):
            limit[0] = i
            while split_next():
                pass

        def first_head(gens):
            advance(8)
            XN, ws = norm(t_x, [t_ca, t_cb])
            tg = trig()
            advance(16)
            prev = []
            for q in range(4):
                ada_sum(True)
                ada_sum(True)
                ada_finish()
                c = slice(4 * q, 4 * q + 4)
                t_gs = V.do(lambda e, c=c, q=q: e.scalar_tensor_tensor(
                    out=gs[:, c], in0=mod[:, 16 + 4 * q:20 + 4 * q], scalar=1.0, in1=colA[:, 16 + 4 * q:20 + 4 * q],
                    op0=ALU.add, op1=ALU.mult), t_mods[(0, q)], t_mods[(0, 4 + q)], t_ca)
                r = turn_over(XN, (4 * q, 4 * q + 4), HT, gs, mod[:, 0:16], ws, [t_gs, *prev], YG + 4096)
                t_ht.update(r)
                prev = r[4 * q] + r[4 * q + 2]
                if q == 3:
                    for _ in tg:
                        pass
                if q < 3:
                    for i, g in enumerate(gens):
                        advance(marks[q][i])
                        next(g)
                        for _ in range(4):
                            next(tg, None)
            limit[0] = len(plan)

        def three(o, l, r, start, stop):
            (lh, ll), (rh, rl) = l, r
            ops = ((lh, rh), (lh, rl), (ll, rh))
            for i, (a, c) in enumerate(ops):
                fn = (lambda e, a=a, c=c, i=i: e.matmul(o, a, c, start=start and i == 0, stop=stop and i == 2,
                                                        skip_group_check=True))
                if stop and i == 2:
                    return PE.do(fn)
                PE.mute(fn)

        def chunk(x, kc):
            if len(x) > 2:
                PE.wait(*x[2][kc])

        def g_proj_T(x, evac, units=4, nk=4, ms=4):
            bs = []
            for p in range((ms + 1) // 2):
                b, f = bank()
                PE.wait(*f)
                bs.append(b)
            wd, nk = ms * 128, nk // 2
            for u in range(2 * units):
                hi, lo, j = take_w()
                for k in range(nk):
                    chunk(x, u * nk + k)
                for m in range(ms):
                    o = bs[m // 2].ap[:, (m % 2) * 256:(m % 2) * 256 + 256]
                    for k in range(nk):
                        c = k * wd + m * 128
                        kc = u * nk + k
                        last = u == 2 * units - 1 and k == nk - 1
                        tt = three(o, (hi[:, c:c + 128], lo[:, c:c + 128]), (x[0][:, kc, :], x[1][:, kc, :]),
                                   m % 2 == 0 and kc == 0, last)
                        if last and m == 1:
                            t0 = tt
                        if k == nk - 1 and m == ms - 1 and not last:
                            tt = mark()
                give_w(j, tt)
                if u % 2 and u < 2 * units - 1:
                    yield
            for p, b in enumerate(bs):
                b.free = evac(p, b, t0 if p == 0 and ms > 2 else tt)
            yield

        def mark():
            fn = PE.q.pop()
            return PE.do(fn)

        def g_proj_tok(x, evac, units=4):
            bs = []
            for t in range(2):
                b, f = bank()
                PE.wait(*f)
                bs.append(b)
            for u in range(2 * units):
                hi, lo, j = take_w()
                for t in range(2):
                    for k in range(2):
                        kc = u * 2 + k
                        chunk(x, kc)
                        ts_ = slice(t * 128, (t + 1) * 128)
                        last = u == 2 * units - 1 and k == 1
                        tt = three(bs[t].ap, (x[0][:, kc, ts_], x[1][:, kc, ts_]),
                                   (hi[:, k * 512:(k + 1) * 512], lo[:, k * 512:(k + 1) * 512]), kc == 0, last)
                        if last and t == 0:
                            t0 = tt
                        if k == 1 and t == 1 and not last:
                            tt = mark()
                give_w(j, tt)
                if u % 2 and u < 2 * units - 1:
                    yield
            bs[0].free = evac(0, bs[0], t0)
            bs[1].free = evac(1, bs[1], tt)
            yield

        def run(g):
            for _ in g:
                pass

        o = W + 2560
        QK = at(o, 4, 256)
        T1, T2 = at(o + 1024, 2, 256), at(o + 1536, 2, 256)
        VV = at(o + 2048, 2, 512)
        SD = at(o + 3072, 384)
        SG = at(o + 3456, 4, 256)
        YN = at(o + 4480, 2, 512)
        assert 2560 + 5504 <= 32 * KB
        YT = at(YG, 32, 256)

        def bc2(a):
            return a.unsqueeze(1).broadcast_to([128, 2, 256])

        state = {"sd": None, "yt": [], "gate": None, "t_y": None}

        def ret_back(h, ty):
            rs = []
            for p in range(2):
                b, f = bank()
                PE.wait(*f)
                for t in range(2):
                    for j in range(2):
                        k = 2 * p + j
                        tt = PE.do(lambda e, b=b, j=j, t=t, k=k: e.transpose(
                            b.ap[:, j * 256 + t * 128:j * 256 + t * 128 + 128],
                            YN[:, t, k * 128:(k + 1) * 128], IDN), ty[t])
                rr = []
                for j in range(2):
                    k = 2 * p + j
                    g = 96 + h * 4 + k
                    rr.append(V.do(lambda e, b=b, j=j, k=k, g=g: e.scalar_tensor_tensor(
                        out=YT[:, h * 4 + k, :], in0=b.ap[:, j * 256:j * 256 + 256], scalar=colB[:, g:g + 1],
                        in1=SG[:, k, :], op0=ALU.mult, op1=ALU.mult), tt, *state["sg"]))
                b.free = rr
                rs += rr
            state["yt"] = rs

        ty = None
        t_gate0, t_gate1 = [], []
        for h in range(8):
            qs = []

            def ev_qk(part, b, tt):
                v = b.ap.rearrange("p (a b) -> p a b", a=2)
                a1 = V.do(lambda e: e.tensor_tensor(T1, v, bc2(cosR), ALU.mult), tt, *t_trig)
                a2 = V.do(lambda e: e.tensor_tensor(T2, v, bc2(sinR), ALU.mult), tt)
                V.do(lambda e: e.tensor_tensor(QK[:, 2 * part, :], T1[:, 0, :], T2[:, 1, :], ALU.subtract), a1, a2)
                qs.append(V.do(lambda e: e.tensor_tensor(QK[:, 2 * part + 1, :], T1[:, 1, :], T2[:, 0, :], ALU.add)))
                V.wait(qs[-1])
                return [a2]

            gq = g_proj_T(HX, ev_qk)
            vs, sg = [], []

            def ev(t, b, tt):
                vs.append(S.do(lambda e: e.copy(VV[:, t, :], b.ap), tt))
                return [vs[-1]]

            def ev_g(p, b, tt):
                sg.append(S.do(lambda e: e.activation(
                    SG[:, 2 * p:2 * p + 2, :].rearrange("p a b -> p (a b)"), b.ap, ACT.Silu), tt, *state["yt"]))
                return [sg[-1]]

            gv, gg = g_proj_tok(HX, ev), g_proj_T(HX, ev_g)
            if h == 0:
                first_head((gq, gv, gg))
            if h >= 4:
                if h == 4:
                    gates = gate_rows(0, GBA, at(LBO, 4, 128), t_gate0)
                next(gates)
            run(gq)
            if h:
                ret_back(h - 1, ty)
            run(gv)
            b, f = bank()
            PE.wait(*f)
            PE.wait(*qs)
            for j in range(2):
                PE.mute(mm(b.ap[:, 0:256], QK[:, 2 + j, 0:128], QK[:, j, :], j == 0, j == 1))
            for j in range(2):
                fn = mm(b.ap[:, 256:384], QK[:, 2 + j, 128:256], QK[:, j, 128:256], j == 0, j == 1)
                tt = PE.do(fn)
            a1 = V.do(lambda e, b=b, h=h: e.tensor_tensor(SD[:, 0:256], b.ap[:, 0:256], DTAB[:, h, :], ALU.mult), tt, t_d)
            a2 = V.do(lambda e, b=b, h=h: e.tensor_tensor(SD[:, 256:384], b.ap[:, 256:384], DTAB[:, h, 0:128], ALU.mult))
            b.free = [a2]
            run(gg)
            state["sg"] = sg
            ty = []
            for t in range(2):
                b, f = bank()
                PE.wait(*f)
                PE.wait(a2, *vs)
                if t == 0:
                    tt = PE.do(mm(b.ap, SD[:, 0:128], VV[:, 0, :], True, True))
                else:
                    PE.mute(mm(b.ap, SD[:, 128:256], VV[:, 0, :], True, False))
                    tt = PE.do(mm(b.ap, SD[:, 256:384], VV[:, 1, :], False, True))
                r = V.do(lambda e, b=b, t=t: e.bn_stats(bst[:, t, :], b.ap), tt)
                r = V.do(lambda e, t=t: e.bn_aggr(mv[:, t, :], bst[:, t, :]), r)
                r = S.do(lambda e, t=t: e.activation(st[:, 8 + t:9 + t], mv[:, t, 1:2], ACT.Sqrt, bias=epsc), r, t_eps)
                r = V.do(lambda e, t=t: e.reciprocal(st[:, 8 + t:9 + t], st[:, 8 + t:9 + t]), r)
                r = V.do(lambda e, b=b, t=t: e.tensor_scalar(YN[:, t, :], b.ap, mv[:, t, 0:1], st[:, 8 + t:9 + t],
                                                             ALU.subtract, ALU.mult), r)
                b.free = [r]
                ty.append(r)
        run(gates)
        t_gate = t_gate0[0]
        ret_back(7, ty)
        YS = (at(16 * KB, 32, 256, of=arena_r), at(W, 32, 256, of=arena_r))

        def flat(x):
            return x.rearrange("p a b -> p (a b)")

        t_sp = split(flat(YT), flat(YS[0]), flat(YS[1]), 8192, state["yt"])

        def project_out(y, nk, gate, t_gate, t_X):
            OT = at(YG, 2, 512)
            last, sq = [None, None], []
            for n in range(4):
                def ev(t, b, tt, n=n):
                    xs = X[:, t, n * 512:(n + 1) * 512]
                    if gate is None:
                        q = r = V.do(lambda e: e.tensor_tensor(xs, b.ap, xs, ALU.add), tt, *t_X)
                    else:
                        gg = gate[:, n * 512:(n + 1) * 512]
                        q = V.do(lambda e: e.tensor_tensor(OT[:, t, :], b.ap, gg, ALU.mult), tt, t_gate, last[t], *t_X)
                        r = V.do(lambda e: e.tensor_tensor(xs, OT[:, t, :], xs, ALU.add), q)
                    sq.append(S.do(lambda e: e.activation(at(YG + 1024 + 512 * t, 512), xs, ACT.Square, scale=float(D) ** -0.5,
                                                          accum_out=SQ[:, t, n:n + 1]), r, *t_X))
                    last[t] = r
                    return [q]

                run(g_proj_tok(y, ev, nk // 4))
            return last[1], sq

        t_X, sq = project_out((*YS, t_sp), 32, GBA, t_gate, t_sp[31])
        t_w_end = t_X
        ada_finish()
        ada_sum(True)
        ada_finish()
        t_mod = t_mods[(1, 11)]

        t_gs = mod_scale(1, t_mod)
        t_ht = norm_T(t_X, gs, mod[:, 48:64], [t_gs, *sq], 2, sq)
        HX = (*HT, t_ht)
        gates = gate_rows(1, GBB, at(W, 4, 128), t_gate1, t_X)
        SGM = at(YG, 16, 256)
        CT = (at(YG + 4096, 8, 256, of=arena_r), at(YG + 6144, 8, 256, of=arena_r))
        QN = [at(W + 1024 * i, 4, 256) for i in range(2)]
        KN = [at(W + 2048 + 1024 * i, 4, 256) for i in range(2)]
        VM = [at(W + 4096 + 1024 * i, 2, 512) for i in range(2)]
        QR = [at(W + 6144 + 512 * i, 2, 256) for i in range(2)]
        CTOK = GBA.rearrange("p (t n) -> p t n", t=2)
        RAW = at(144 * KB, 512)
        RT = [at(144 * KB + 512 + 512 * i, 512) for i in range(2)]
        cs = []
        for part in range(2):
            def ev(t, b, tt, part=part):
                d = CTOK[:, t, part * 512:(part + 1) * 512]
                c = 4 + 2 * part + t
                r = stat_of(b.ap, 512, c, d, tt, t_w_end)
                cs.append(V.do(lambda e: e.tensor_scalar(d, b.ap, st[:, c:c + 1], None, ALU.mult), r))
                return [cs[-1]]

            for i, _ in enumerate(g_proj_tok(HX, ev)):
                if part or i == 2:
                    next(gates, None)

        sgt = {}

        def gate_ev(g):
            def ev(p, b, tt):
                m = 4 * g + 2 * p
                r = S.do(lambda e: e.activation(flat(SGM[:, m:m + 2, :]), b.ap, ACT.Silu), tt)
                sgt[m] = sgt[m + 1] = r
                return [r]
            return ev

        run(gates)
        t_gate, = t_gate1
        run(g_proj_T(HX, gate_ev(0)))

        def rotate(b, m, dst, perm, co, si, tt, raw, rt, sc, t_raw, after, done):
            n = 256 * m

            def v(x):
                return x[:, 0:n].rearrange("p (a b) -> p a b", a=m)

            def bc(x):
                return x.unsqueeze(1).broadcast_to([128, m, 256])

            r = S.do(lambda e: e.copy(raw[:, 0:n], b.ap[:, 0:n]), tt, *t_raw)

            def rest():
                w = after()
                p = PE.do(mm(b.ap[:, 0:n], perm, raw[:, 0:n], True, True), r)
                a = V.do(lambda e: e.tensor_tensor(v(rt[0]), v(raw), bc(co), ALU.mult), r, *w)
                c = V.do(lambda e: e.tensor_tensor(v(rt[1]), v(b.ap), bc(si), ALU.mult), p)
                if sc is None:
                    t = V.do(lambda e: e.tensor_tensor(dst, rt[0][:, 0:n], rt[1][:, 0:n], ALU.add), a, c)
                else:
                    c = V.do(lambda e: e.tensor_tensor(rt[0][:, 0:n], rt[0][:, 0:n], rt[1][:, 0:n], ALU.add), a, c)
                    t = V.do(lambda e: e.tensor_scalar(dst, rt[0][:, 0:n], sc, None, ALU.mult), c)
                b.free = [t]
                done(t)

            late.append(rest)
            return None

        PMm = cst[:, K_PM:K_PM + 128]
        t_ct = turn_over(CTOK, (0, 8), CT, colA[:, 80:88], None, lambda t, k: cs[2 * (k // 4) + t], [t_w_end, t_gate], W)

        def ev(p, b, tt):
            return rotate(b, 1, KR, PMm, cosM, sinM, tt, RAW, RT, None, t_ct[7], lambda: t_ct[7], t_krs.append)

        t_krs = []
        run(g_proj_T(HX, ev, units=1, nk=16, ms=1))
        for g in range(1, 4):
            run(g_proj_T(HX, gate_ev(g)))
        rot = [t_krs[0]]
        got = {}

        def group(g, free):
            a = g % 2
            ts = got[g] = []

            def e_q(p, b, tt):
                ts.append(S.do(lambda e: e.copy(flat(QN[a][:, 2 * p:2 * p + 2, :]), b.ap), tt, *free, *t_ct[7]))
                return [ts[-1]]

            def e_r(p, b, tt):
                def done(t):
                    rot[0] = t
                    ts.append(t)

                return rotate(b, 2, flat(QR[a]), PMm, cosM, sinM, tt, RAW, RT, None, [rot[0], *free],
                              lambda: [rot[0], *free], done)

            def e_k(p, b, tt):
                ts.append(V.do(lambda e: e.tensor_copy(flat(KN[a][:, 2 * p:2 * p + 2, :]), b.ap), tt, *free))
                return [ts[-1]]

            def e_v(t, b, tt):
                ts.append(S.do(lambda e: e.copy(VM[a][:, t, :], b.ap), tt, *free))
                return [ts[-1]]

            PE.wait(*t_ct[5], *t_ct[7])
            ck = (CT[0][:, 4:8, :], CT[1][:, 4:8, :])
            yield from g_proj_T(CT, e_q, units=1)
            yield from g_proj_T(CT, e_r, units=1, ms=2)
            yield from g_proj_T(ck, e_k, units=1)
            yield from g_proj_tok(ck, e_v, units=1)

        run(group(0, []))

        CM = cst[:, K_CM:K_CM + 384]

        def soft(i, b, tt, mask, scale, t_old):
            L = LB[i % 2]
            j = i % 2
            es = []
            rr = []
            for t, (c0, c1) in enumerate(((0, 128), (128, 384))):
                rr.append(V.do(lambda e, c0=c0, c1=c1, t=t: e.tensor_tensor_reduce(
                    L[:, c0:c1], b.ap[:, c0:c1], mask[:, c0:c1], -scale, 3e38, ALU.add, ALU.min,
                    mn[:, j, t:t + 1]), tt, *t_old))
            for t, (c0, c1) in enumerate(((0, 128), (128, 384))):
                es.append(S.do(lambda e, c0=c0, c1=c1, t=t: e.activation(
                    L[:, c0:c1], L[:, c0:c1], ACT.Exp, bias=mn[:, j, t:t + 1], scale=-1.0,
                    accum_out=sums[:, j, t:t + 1]), rr[t]))
            b.free = [rr[1]]
            r = V.do(lambda e: e.reciprocal(rinv[:, i % 3, :], sums[:, j, :]), es[0], es[1])
            return es, r

        def flip(i, waits, t_old):
            b, f = bank()
            PE.wait(*f)
            L = LB[i % 2]
            PE.wait(*waits)
            for c in range(3):
                tt = PE.do(lambda e, c=c, b=b: e.transpose(b.ap[:, c * 128:(c + 1) * 128], L[:, c * 128:(c + 1) * 128], IDN))
            r = S.do(lambda e, b=b: e.copy(PTB[i % 2], b.ap[:, 0:384]), tt, *t_old)
            b.free = [r]
            return tt, r

        fl = {}
        sm_ = {}
        og = {}
        ISQ = float(192 ** -0.5)
        nxt = None
        for i in range(16 + 2):
            if i < 16:
                g = i // 4
                if i % 4 == 0:
                    PE.wait(*got[g])
                b, f = bank()
                PE.wait(*f)
                rb = 64 * (i % 2)
                q1, q2 = QN[g % 2][:, i % 4, :], QR[g % 2][rb:rb + 64, (i % 4) // 2, :]
                k1, k2 = KN[g % 2][:, i % 4, :], KR[rb:rb + 64, :]
                PE.mute(mm(b.ap[:, 0:128], q1[:, 0:128], k1[:, 0:128], True, False))
                PE.mute(mm(b.ap[:, 0:128], q2[:, 0:128], k2[:, 0:128], False, True))
                PE.mute(mm(b.ap[:, 128:384], q1[:, 128:256], k1, True, False))
                tt = PE.do(mm(b.ap[:, 128:384], q2[:, 128:256], k2, False, True))
                es, r = soft(i, b, tt, CM, ISQ, [fl[i - 2][0]] if i > 1 else [])
                ns = []
                for t, (c0, c1) in enumerate(((0, 128), (128, 384))):
                    ns.append(V.do(lambda e, c0=c0, c1=c1, t=t, i=i: e.tensor_scalar(
                        LB[i % 2][:, c0:c1], LB[i % 2][:, c0:c1], rinv[:, i % 3, t:t + 1], None, ALU.mult), r))
                sm_[i] = ns
            if 0 <= i - 1 < 16:
                fl[i - 1] = flip(i - 1, sm_[i - 1], [og[i - 3][0]] if i >= 3 else [])
            if i >= 2:
                h = i - 2
                b, f = bank()
                PE.wait(*f)
                PE.wait(fl[h][1])
                PT = PTB[h % 2]
                vm = VM[(h // 4) % 2]
                v0, v1 = (vm[:, t, (h % 4) * 128:(h % 4 + 1) * 128] for t in range(2))
                PE.mute(mm(b.ap[:, 0:128], v0, PT[:, 0:128], True, True))
                PE.mute(mm(b.ap[:, 128:256], v0, PT[:, 128:256], True, False))
                tt = PE.do(mm(b.ap[:, 128:256], v1, PT[:, 256:384], False, True))
                r = V.do(lambda e, b=b, h=h: e.tensor_tensor(SGM[:, h, :], b.ap[:, 0:256], SGM[:, h, :], ALU.mult), tt, sgt[h])
                b.free = [r]
                og[h] = (tt, r)
            if i % 4 == 1 and 1 <= i and i // 4 + 1 < 4:
                nxt = group(i // 4 + 1, [og[i - 2][0]] if i >= 4 else [])
                next(nxt)
            elif nxt is not None and i < 16:
                for _ in range(2):
                    next(nxt, None)
                if i % 4 == 3:
                    run(nxt)
                    nxt = None
        OS = (at(16 * KB, 16, 256, of=arena_r), at(32 * KB, 16, 256, of=arena_r))
        t_sp = split(flat(SGM), flat(OS[0]), flat(OS[1]), 4096, [og[15][1]])
        t_fg = G.dma(GBA, A["final_norm_g"].partition_broadcast(128), DSem("dfg"), og[15][1], rot[0])
        t_X, sq = project_out((*OS, t_sp), 16, GBB, t_gate, [t_X, *t_sp[15]])

        r = V.do(lambda e: e.tensor_reduce(st[:, 10:12], SQ, AX.X, ALU.add), *sq)
        r = S.do(lambda e: e.activation(st[:, 10:12], st[:, 10:12], ACT.Sqrt, bias=epsc), r)
        r = V.do(lambda e: e.reciprocal(st[:, 10:12], st[:, 10:12]), r)
        sq = []
        for n in range(4):
            for t in range(2):
                xs = X[:, t, n * 512:(n + 1) * 512]
                t_X = V.do(lambda e, t=t, n=n, xs=xs: e.scalar_tensor_tensor(
                    out=xs, in0=xs, scalar=st[:, 10 + t:11 + t], in1=GBA[:, n * 512:(n + 1) * 512],
                    op0=ALU.mult, op1=ALU.mult), r, t_fg)
                sq.append(S.do(lambda e, t=t, n=n, xs=xs: e.activation(
                    at(YG + 1024 + 512 * t, 512), xs, ACT.Square, scale=float(D) ** -0.5,
                    accum_out=SQ[:, t, n:n + 1]), t_X, *sq[-2:-1]))

        t_ht = norm_T(t_X, colA[:, 48:64], None, sq, 12, sq)
        HX = (*HT, t_ht)
        d2 = DSem("d2")
        DM, DC, DS = GBA[:, 0:384], GBA[:, 384:640], GBA[:, 640:896]
        t_d2 = G.dma(GBA[:, 0:896], A["table"][:, K_DM:K_END], d2, t_X)
        O = at(YG, 2, D)
        FV, DV = at(YG + 4096, 2, 1024), at(YG + 6144, 2, 1024)
        FQ, FK, DQ, DK = (at(W + i * 2048, 8, 256) for i in range(4))
        RAW2 = [at(152 * KB, 512), at(144 * KB + 1408, 512)]
        RT2 = [at(152 * KB + 512 + 512 * i, 512) for i in range(2)]
        LF, LA, LM = (at(152 * KB + 1536 + 32 * i, 2, 16) for i in range(3))
        CTT, NCT = at(144 * KB + 896, 256), at(144 * KB + 1152, 256)

        b, f = bank()
        PE.wait(*f)
        b2, f = bank()
        PE.wait(*f)
        lb = [b, b2]
        for u in range(2):
            hi, lo, j = take_w()
            for t in range(2):
                for k in range(8):
                    kc = u * 8 + k
                    chunk(HX, kc)
                    ts_ = slice(t * 128, (t + 1) * 128)
                    tt = three(lb[t].ap[:, 0:16], (HT[0][:, kc, ts_], HT[1][:, kc, ts_]),
                               (hi[:, k * 16:(k + 1) * 16], lo[:, k * 16:(k + 1) * 16]), kc == 0, kc == 15)
            give_w(j, tt if tt else mark())
        for t in range(2):
            r = V.do(lambda e, t=t: e.tensor_tensor(LF[:, t, :], lb[t].ap[:, 0:16], fb, ALU.add), tt, t_fb, t_X)
            lb[t].free = [r]
        r2 = V.do(lambda e: e.scalar_tensor_tensor(out=LA, in0=LF, scalar=-1.0, in1=LF, op0=ALU.mult, op1=ALU.min), r)
        r3 = V.do(lambda e: e.tensor_scalar(LM, LF, 0.0, None, ALU.min), r)
        r2 = S.do(lambda e: e.activation(LA, LA, ACT.Exp), r2)
        r2 = S.do(lambda e: e.activation(LA, LA, ACT.Ln, bias=1.0), r2)
        t_lf = V.do(lambda e: e.tensor_tensor(LF, LM, LA, ALU.subtract), r2, r3)

        fq_done, dq_done = [], []

        def copy_T(dst, g, sc, done):
            def f(p, b, tt):
                c = 4 * g + 2 * p
                d = flat(dst[:, c:c + 2, :])
                done.append(S.do(lambda e: e.mul(d, b.ap, sc) if sc else e.copy(d, b.ap), tt, t_X, *t_ht[15]))
                return [done[-1]]
            return f

        ro, turns = [t_X], [0]
        PDm = cst[:, K_PD:K_PD + 128]

        def dil_T(dst, g, sc):
            def f(p, b, tt):
                c = 4 * g + 2 * p

                def done(t):
                    ro.append(t)
                    dq_done.append(t)

                k = turns[0] % 2
                turns[0] += 1
                return rotate(b, 2, flat(dst[:, c:c + 2, :]), PDm, DC, DS, tt, RAW2[k], RT2, sc, [t_X, *dq_done[-1 - k:]],
                              lambda: [ro[-1], t_d2], done)
            return f

        def copy_tok(dst, g, done):
            def f(t, b, tt):
                done.append(S.do(lambda e: e.copy(dst[:, t, g * 512:(g + 1) * 512], b.ap), tt, *t_ht[15]))
                return [done[-1]]
            return f

        for g in range(2):
            run(g_proj_T(HX, copy_T(FQ, g, 0.125, fq_done)))
        for g in range(2):
            run(g_proj_T(HX, copy_T(FK, g, None, fq_done)))
        for g in range(2):
            run(g_proj_tok(HX, copy_tok(FV, g, fq_done)))

        b, f = bank()
        PE.wait(*f)
        PE.wait(t_lf)
        PE.mute(mm(b.ap[0:16, 0:128], LF[:, 0, :], TRI, True, True))
        PE.mute(mm(b.ap[0:16, 128:256], LF[:, 0, :], ONES, True, False))
        tt = PE.do(mm(b.ap[0:16, 128:256], LF[:, 1, :], TRI, False, True))
        r1 = V.do(lambda e, b=b: e.tensor_copy(CTT[0:16, :], b.ap[0:16, 0:256]), tt)
        r2 = V.do(lambda e, b=b: e.tensor_scalar(NCT[0:16, :], b.ap[0:16, 0:256], -1.0, None, ALU.mult), tt)
        b.free = [r2]
        PE.wait(r1, r2, *fq_done)

        def dil_work():
            for g in range(2):
                yield from g_proj_T(HX, dil_T(DQ, g, 0.125))
            for g in range(2):
                yield from g_proj_T(HX, dil_T(DK, g, None))
            for g in range(2):
                yield from g_proj_tok(HX, copy_tok(DV, g, dq_done))

        def heads(qT, kT, vt, col0, mask, fox, items, t_first):
            fl, sm_, pv = {}, {}, {}
            ob = None
            for i in range(16 + 2):
                if i < 16:
                    b, f = bank()
                    PE.wait(*f)
                    rb, c = 64 * (i % 2), i // 2
                    q, k = qT[rb:rb + 64, c, :], kT[rb:rb + 64, c, :]
                    one = IDN[0:16, i:i + 1]
                    for c0, q0, n in ((0, 0, 128), (128, 128, 256)):
                        o = b.ap[:, c0:c0 + n]
                        fn = mm(o, q[:, q0:q0 + 128], k[:, 0:n], True, not fox)
                        if fox:
                            PE.mute(fn)
                            PE.mute(mm(o, one.broadcast_to([16, 128]), NCT[0:16, 0:n], False, False))
                            fn = mm(o, CTT[0:16, q0:q0 + 128], one.broadcast_to([16, n]), False, True)
                        tt = PE.do(fn)
                    es, r = soft(i, b, tt, mask, 1.0, ([fl[i - 2][0]] if i > 1 else []) + t_first)
                    sm_[i] = (es, r)
                    next(items, None)
                if 0 <= i - 1 < 16:
                    fl[i - 1] = flip(i - 1, sm_[i - 1][0], [pv[i - 3][0]] if i >= 3 else [])
                if i < 16 and i % 2:
                    next(items, None)
                if i >= 2:
                    h = i - 2
                    b, f = bank()
                    PE.wait(*f)
                    PE.wait(fl[h][1])
                    PT = PTB[h % 2]
                    v0, v1 = vt[:, 0, h * 64:(h + 1) * 64], vt[:, 1, h * 64:(h + 1) * 64]
                    PE.mute(mm(b.ap[:, 0:64], PT[:, 0:128], v0, True, True))
                    PE.mute(mm(b.ap[:, 64:128], PT[:, 128:256], v0, True, False))
                    tt = PE.do(mm(b.ap[:, 64:128], PT[:, 256:384], v1, False, True))
                    for t in range(2):
                        r = V.do(lambda e, b=b, h=h, t=t: e.tensor_scalar(
                            O[:, t, col0 + h * 64:col0 + h * 64 + 64], b.ap[:, t * 64:t * 64 + 64],
                            rinv[:, h % 3, t:t + 1], None, ALU.mult), tt, sm_[h][1])
                    b.free = [r]
                    pv[h] = (tt, r)
            return pv[15][1]

        items = dil_work()
        t_o1 = heads(FQ, FK, FV, 0, CM, True, items, list(t_ht[15]))
        run(items)
        PE.wait(*dq_done)
        t_o2 = heads(DQ, DK, DV, 1024, DM, False, iter(()), [t_d2])
        ns = {}
        for t in range(2):
            for part, to in ((0, t_o1), (1, t_o2)):
                ap = O[:, t, part * 1024:(part + 1) * 1024]
                r = stat_of(ap, 1024, 16 + 2 * t + part, at(W + (2 * t + part) * 1024, 1024), to, t_o2)
                rr = V.do(lambda e, ap=ap, t=t, part=part: e.tensor_scalar(
                    ap, ap, st[:, 16 + 2 * t + part:17 + 2 * t + part], None, ALU.mult), r)
                ns[t, part] = rr
        t_ff = G.dma(GBB, A["ffn_norm_gain_2"][0].partition_broadcast(128), DSem("dff"), t_o2)
        t_mt = turn_over(O, (0, 16), HT, colA[:, 88:104], None, lambda t, k: ns[t, k // 8], [t_o2], YG + 4096)
        t_X, sq = project_out((*HT, t_mt), 16, None, None, t_mt[15])

        after = [t_X]
        HN = at(YG, 2, D)
        QT = at(YG + 4096, 16, 256)
        t_ht = norm_T(t_X, colA[:, 64:80], None, sq, 20, sq)
        HX = (*HT, t_ht)
        t_hn = []
        for t in range(2):
            t_hn.append(V.do(lambda e, t=t: e.tensor_tensor(HN[:, t, :], HN[:, t, :], GBB, ALU.mult), *t_ht[15], t_ff))
        KT = at(W, 16, 128)
        JUNK = at(16 * KB, D)
        pz = [W + 2048]

        def pt(*shape):
            o = pz[0]
            pz[0] += int(np.prod(shape))
            return at(o, *shape)

        SC, CA, EQ = pt(D), pt(4, 256), pt(64, 16)
        VAL, IDX, IDF = pt(16, 16), pt(16, 16), pt(16, 16)
        WK = GBA[:, 768:1024]
        TV, TC = pt(8, 16), pt(128)
        II = [GBA[:, 0 + 128 * i:128 + 128 * i] for i in range(2)]
        IF = [GBA[:, 256 + 128 * i:384 + 128 * i] for i in range(2)]
        EF = [GBA[:, 512 + 128 * i:640 + 128 * i] for i in range(2)]
        EI = [pt(128) for _ in range(2)]
        GT = [pt(8, 16) for _ in range(2)]
        HD = [pt(128) for _ in range(2)]
        GS = pt(8)
        assert pz[0] <= 192 * KB, pz[0]

        ki = pos[0]
        pos[0] += 1
        assert plan[ki][0] == "raw"
        PE.wait(landed[ki], landed[ki + 1])
        pos[0] += 1
        kt = []
        for g in range(4):
            b, f = bank()
            PE.wait(*f)
            wk_ = raws[(ki + g // 2) % 8][0]
            for j in range(4):
                tt = PE.do(lambda e, b=b, g=g, j=j, wk_=wk_: e.transpose(
                    b.ap[:, j * 128:(j + 1) * 128], wk_[:, (4 * (g % 2) + j) * 128:(4 * (g % 2) + j + 1) * 128], IDN))
            r = V.do(lambda e, b=b, g=g: e.tensor_copy(KT[:, 4 * g:4 * g + 4, :].rearrange("p a b -> p (a b)"), b.ap), tt, t_o2, *t_mt[15])
            b.free = [r]
            kt.append(r)
            if g % 2:
                free_raw(ki + g // 2, tt)
        IOTA = cst[:, K_IOTA:K_IOTA + 16]
        t_sel = {}

        def top16(src, val, idx, wk, r):
            r = V.do(lambda e: e.max(val[:, 0:8], src), r)
            yield r
            r = V.do(lambda e: e.max_index(idx[:, 0:8], val[:, 0:8], src), r)
            yield r
            r = V.do(lambda e: e.match_replace(wk, val[:, 0:8], src, -3.0e38), r)
            yield r
            r = V.do(lambda e: e.max(val[:, 8:16], wk), r)
            yield r
            r = V.do(lambda e: e.max_index(idx[:, 8:16], val[:, 8:16], wk), r)
            yield r

        def select(t, r):
            sc = {}
            for hf in range(2):
                PE.wait(*kt)
                for g in (2 * hf, 2 * hf + 1):
                    b, f = bank()
                    PE.wait(*f)
                    for j in range(4):
                        tt = PE.do(mm(b.ap[:, j * 128:(j + 1) * 128], QT[:, 4 * g + j, t * 128:(t + 1) * 128],
                                      KT[:, 4 * g + j, :], True, True))
                    q = S.do(lambda e, b=b, g=g: e.copy(SC[:, g * 512:(g + 1) * 512], b.ap), tt, r)
                    b.free = [q]
                    sc[g] = q
                a = slice(8 * hf, 8 * hf + 8)
                for hp in range(8 * hf, 8 * hf + 8):
                    for r in top16(SC[:, hp * 128:(hp + 1) * 128], VAL[:, hp, :], IDX[:, hp, :].bitcast(U32),
                                   WK[:, 0:128], [sc[hp // 4], r]):
                        yield
                V2 = VAL[:, a, :].rearrange("p (h a) k -> p h a k", a=2)
                I2 = IDF[:, a, :].rearrange("p (h a) k -> p h a k", a=2)
                r = V.do(lambda e, a=a: e.tensor_copy(IDF[:, a, :], IDX[:, a, :].bitcast(U32)), r)
                yield
                r = V.do(lambda e, V2=V2: e.tensor_tensor(
                    CA.rearrange("p h (i j) -> p h i j", i=16),
                    V2[:, :, 0, :].unsqueeze(3).broadcast_to([128, 4, 16, 16]),
                    V2[:, :, 1, :].unsqueeze(2).broadcast_to([128, 4, 16, 16]), ALU.add), r)
                yield
                for h in range(4 * hf, 4 * hf + 4):
                    for r in top16(CA[:, h % 4, :], TV[:, h, :], TC[:, h * 16:(h + 1) * 16].bitcast(U32), WK, r):
                        yield
                s6 = slice(64 * hf, 64 * hf + 64)
                ra = V.do(lambda e, s6=s6: e.tensor_scalar(II[0][:, s6].bitcast(U32), TC[:, s6].bitcast(U32), 4, None,
                                                           ALU.logical_shift_right), r)
                yield
                rb = V.do(lambda e, s6=s6: e.tensor_scalar(II[1][:, s6].bitcast(U32), TC[:, s6].bitcast(U32), 15, None,
                                                           ALU.bitwise_and), r)
                yield
                E3 = EQ
                E4 = E3.rearrange("p (h k) i -> p h k i", h=4)
                for p in range(2):
                    r = V.do(lambda e, p=p, s6=s6: e.tensor_copy(IF[p][:, s6], II[p][:, s6].bitcast(U32)), ra, rb)
                    yield
                    r = V.do(lambda e, p=p, s6=s6, E3=E3: e.tensor_tensor(
                        E3, IF[p][:, s6].unsqueeze(2).broadcast_to([128, 64, 16]),
                        IOTA.unsqueeze(1).broadcast_to([128, 64, 16]), ALU.is_equal), r)
                    yield
                    r = V.do(lambda e, p=p, E4=E4, I2=I2: e.tensor_tensor(
                        E4, E4, I2[:, :, p, :].unsqueeze(2).broadcast_to([128, 4, 16, 16]), ALU.mult), r)
                    yield
                    r = V.do(lambda e, p=p, s6=s6, E3=E3: e.tensor_reduce(EF[p][:, s6], E3, AX.X, ALU.add), r)
                    yield
                r = V.do(lambda e, s6=s6: e.scalar_tensor_tensor(out=EI[t][:, s6].bitcast(U32), in0=EF[0][:, s6], scalar=128.0,
                                                                 in1=EF[1][:, s6], op0=ALU.mult, op1=ALU.add), r)
                t_sel[(t, hf)] = r
                yield
            r = V.do(lambda e: e.tensor_tensor(GT[t], TV, TV[:, :, 0:1].broadcast_to([128, 8, 16]), ALU.subtract), r)
            yield
            r = S.do(lambda e: e.activation(GT[t], GT[t], ACT.Exp), r)
            yield
            r = V.do(lambda e: e.tensor_reduce(GS, GT[t], AX.X, ALU.add), r)
            yield
            r = V.do(lambda e: e.reciprocal(GS, GS), r)
            yield
            t_gt[t] = V.do(lambda e: e.tensor_tensor(GT[t], GT[t], GS.unsqueeze(2).broadcast_to([128, 8, 16]), ALU.mult), r)
            yield

        t_gt = {}

        def selects():
            yield from select(0, None)
            yield from select(1, t_gt[0])

        sel = selects()
        for g in range(4):
            def ev(p, b, tt, g=g):
                c = 4 * g + 2 * p
                kt.append(S.do(lambda e: e.copy(flat(QT[:, c:c + 2, :]), b.ap), tt, *t_ht[15]))
                return [kt[-1]]
            for _ in g_proj_T(HX, ev):
                if g < 2:
                    continue
                for _ in range(8):
                    if (0, 0) not in t_sel:
                        next(sel)
        t_ring = kt[-1]
        while (0, 0) not in t_sel:
            next(sel)
        gsem = [DSem(f"g{i}") for i in range(NG)]
        gbuf = [at(RAWS + i * 2048, D) for i in range(NG)]
        last = [t_ring] * NG
        cnt = [0]
        t_f2 = G.dma(GBB, A["final_norm_gain_2"].partition_broadcast(128), DSem("df2"), *t_hn)

        def gather(tab, t, j):
            i = cnt[0] % NG
            cnt[0] += 1
            ds = gsem[i]
            G.wait(t_sel[(t, j // 64)], last[i], t_ring)
            G.q.append(lambda e: e.indirect_dma_start(
                out=gbuf[i], out_offset=None, in_=tab,
                in_offset=bass.IndirectOffsetOnAxis(ap=EI[t][:, j:j + 1].bitcast(U32), axis=0)).then_inc(ds.sem, 16))
            ds.n += 16
            return i, (ds.sem, ds.n)

        down, up = A["peer_down_2"][0], A["peer_up_2"][0]
        todo = [(down, t, j) for t in range(2) for j in range(128)] + [(up, t, j) for t in range(2) for j in range(128)]
        co = [None, None]
        rprev = None
        for n, (tab, t, j) in enumerate(todo):
            if n:
                next(sel, None)
                next(sel, None)
            i, tg = gather(tab, t, j)
            if tab is down:
                rprev = V.do(lambda e, i=i, t=t, j=j: e.tensor_tensor_reduce(
                    JUNK, gbuf[i], HN[:, t, :], 1.0, 0.0, ALU.mult, ALU.add, HD[t][:, j:j + 1]), tg, rprev)
                if j == 127:
                    r = S.do(lambda e, t=t: e.activation(HD[t], HD[t], ACT.Gelu_apprx_tanh), rprev)
                    co[t] = (r, t)
            else:
                if j == 0:
                    rprev = V.do(lambda e, t=t: e.tensor_tensor(HD[t], HD[t], GT[t].rearrange("p a b -> p (a b)"), ALU.mult),
                                 co[t][0], rprev, t_gt[t])
                rprev = V.do(lambda e, i=i, t=t, j=j: e.scalar_tensor_tensor(
                    out=X[:, t, :], in0=gbuf[i], scalar=HD[t][:, j:j + 1], in1=X[:, t, :], op0=ALU.mult, op1=ALU.add),
                    tg, rprev)
                if j == 127:
                    r = stat_of(X[:, t, :], D, 24 + t, SC, rprev)
                    r = V.do(lambda e, t=t: e.scalar_tensor_tensor(out=X[:, t, :], in0=X[:, t, :], scalar=st[:, 24 + t:25 + t],
                                                                   in1=GBB, op0=ALU.mult, op1=ALU.mult), r, t_f2)
                    if t == 0:
                        dout = DSem("dout")
                    t_out = SP.dma(out[0][t * 128:(t + 1) * 128, :], X[:, t, :], dout, r)
                    rprev = r
            last[i] = rprev
        SP.wait(t_out)
        assert pos[0] == len(plan) == sent[0], (pos, len(plan), sent)

        block = ctx.enter_context(nc.Block())
        block.sync(SP.run)
        block.gpsimd(G.run)
        block.scalar(S.run)
        block.vector(V.run)
        block.tensor(PE.run)


_INS = ["x", "c", "positions", "ada_w", "ada_b", "norm_g", "ret_w_in", "ret_gn_g", "ret_w_out", "mla_w_in",
        "mla_q_norm_g", "mla_w_uq", "mla_kv_norm_g", "mla_w_ukv", "mla_w_out", "final_norm_g", "attn_norm_gain_2",
        "w_in_2", "forget_bias_2", "fox_out_gain_2", "dil_out_gain_2", "w_out_2", "ffn_norm_gain_2",
        "peer_query_2", "peer_sub_keys_2", "peer_down_2", "peer_up_2", "final_norm_gain_2"]


def kernel(**inputs):
    import concourse.bacc as _bacc
    from concourse.bass_utils import run_bass_kernel_spmd as _run

    nc = _bacc.Bacc("TRN2", target_bir_lowering=False, num_devices=1)
    arrays, A = {}, {}
    table, decay = tables()
    every = {n: np.ascontiguousarray(inputs[n]) for n in _INS}
    every["table"], every["decay"] = table, decay
    for name, a in every.items():
        arrays[f"in_{name}"] = a
        A[name] = nc.dram_tensor(f"in_{name}", a.shape, mybir.dt.from_np(a.dtype), kind="ExternalInput").ap()
    out = nc.dram_tensor("out_0", (1, 256, D), F, kind="ExternalOutput").ap()
    build(nc, A, out)
    r = _run(nc, [arrays], core_ids=[0])
    return r.results[0]["out_0"]
```
